# Optimizing a Trainium2 kernel written in Bass

```python
import jax, jax.numpy as jnp
from jax import lax
import numpy as np
import math

D_MODEL = 2048
BATCH = 1
SEQ = 256
DEPTH = 1

GRID_W = 64
D_MIX = D_MODEL
NH_A = 4
DH_A = D_MIX // 2 // NH_A
W_A = NH_A * DH_A
NH_B = 8
DH_B = (D_MIX - W_A) // NH_B
W_B = NH_B * DH_B
CHUNK = 64
WIN_ROWS_MAX = 8
WIN_COLS = 16
D_FF = ((8 * D_MODEL // 3 + 255) // 256) * 256
CONV_W = 3
N_MOD = 6
N_GATES = 4 * NH_A
IN_SIZES = (W_A, W_A, W_A, W_A, N_GATES, W_B, W_B, W_B)
IN_COLS = sum(IN_SIZES)
IN_SPLITS = tuple(int(s) for s in np.cumsum(IN_SIZES)[:-1])
EPS = 1e-6


def rms_norm(x, g):
    xf = x.astype(jnp.float32)
    y = xf * lax.rsqrt(jnp.mean(xf * xf, axis=-1, keepdims=True) + EPS)
    return (y * g.astype(jnp.float32)).astype(x.dtype)

def modulate(h, shift, scale):
    return h * (1 + scale[:, None, :]) + shift[:, None, :]

def to_heads(t, n_heads):
    b, s, _ = t.shape
    return t.reshape(b, s, n_heads, -1).transpose(0, 2, 1, 3)

def from_heads(t):
    b, h, s, d = t.shape
    return t.transpose(0, 2, 1, 3).reshape(b, s, h * d)

def mlstm_scan(q, k, v, log_i, log_f):
    b_, h_, s_, d_ = q.shape
    nc = s_ // CHUNK

    def chunks(t):
        return jnp.moveaxis(t.reshape(t.shape[:2] + (nc, CHUNK) + t.shape[3:]), 2, 0)

    xs = (chunks(q), chunks(k), chunks(v), chunks(log_i), chunks(log_f))
    lower = jnp.tril(jnp.ones((CHUNK, CHUNK), dtype=bool))

    def step(carry, inp):
        C, n, m = carry
        qc, kc, vc, li, lf = inp
        bcum = jnp.cumsum(lf, axis=-1)
        gsum = bcum[..., -1]
        log_d = jnp.where(lower, bcum[..., :, None] - bcum[..., None, :] + li[..., None, :], -jnp.inf)
        m_inter = bcum + m[..., None]
        m_t = jnp.maximum(m_inter, jnp.max(log_d, axis=-1))
        s = jnp.einsum('bhtd,bhsd->bhts', qc, kc) * jnp.exp(log_d - m_t[..., None])
        a = jnp.exp(m_inter - m_t)
        num = jnp.einsum('bhts,bhse->bhte', s, vc) + a[..., None] * jnp.einsum('bhtd,bhde->bhte', qc, C)
        den = jnp.sum(s, axis=-1) + a * jnp.einsum('bhtd,bhd->bht', qc, n)
        h = num / jnp.maximum(jnp.abs(den), jnp.exp(-m_t))[..., None]
        log_w = gsum[..., None] - bcum + li
        m_new = jnp.maximum(gsum + m, jnp.max(log_w, axis=-1))
        decay = jnp.exp(gsum + m - m_new)
        w = jnp.exp(log_w - m_new[..., None])
        C = decay[..., None, None] * C + jnp.einsum('bhs,bhsd,bhse->bhde', w, kc, vc)
        n = decay[..., None] * n + jnp.einsum('bhs,bhsd->bhd', w, kc)
        return (C, n, m_new), h

    init = (jnp.zeros((b_, h_, d_, d_), jnp.float32),
            jnp.zeros((b_, h_, d_), jnp.float32),
            jnp.full((b_, h_), -1e30, jnp.float32))
    _, hs = lax.scan(step, init, xs)
    return jnp.moveaxis(hs, 0, 2).reshape(b_, h_, s_, d_)

def mlstm_bidirectional(q, k, v, gates):
    i_f, f_f, i_b, f_b = jnp.split(gates, 4, axis=1)
    h_fwd = mlstm_scan(q, k, v, i_f, jax.nn.log_sigmoid(f_f))
    flip = lambda t: jnp.flip(t, axis=2)
    h_bwd = flip(mlstm_scan(flip(q), flip(k), flip(v), flip(i_b), flip(jax.nn.log_sigmoid(f_b))))
    return h_fwd + h_bwd

def neighborhood_attention(q, k, v, rpb):
    b_, h_, s_, d_ = q.shape
    rows = s_ // GRID_W
    kr = min(WIN_ROWS_MAX, rows)
    kc = WIN_COLS
    grid = lambda t: t.reshape(b_, h_, rows, GRID_W, d_)
    q, k, v = grid(q), grid(k), grid(v)
    row_start = jnp.clip(jnp.arange(rows) - kr // 2, 0, rows - kr)
    cols = jnp.arange(GRID_W)
    col_idx = jnp.clip(cols - kc // 2, 0, GRID_W - kc)[:, None] + jnp.arange(kc)
    dc = col_idx - cols[:, None] + (WIN_COLS - 1)
    scale = d_ ** -0.5

    def row_block(r):
        rs = row_start[r]
        qr = lax.dynamic_index_in_dim(q, r, axis=2, keepdims=False)
        kb = lax.dynamic_slice_in_dim(k, rs, kr, axis=2)[:, :, :, col_idx]
        vb = lax.dynamic_slice_in_dim(v, rs, kr, axis=2)[:, :, :, col_idx]
        dr = rs + jnp.arange(kr) - r + (WIN_ROWS_MAX - 1)
        bias = rpb[:, dr[None, :, None], dc[:, None, :]]
        s = jnp.einsum('bhcd,bhrcjd->bhcrj', qr, kb).astype(jnp.float32) * scale + bias.astype(jnp.float32)
        p = jax.nn.softmax(s.reshape(b_, h_, GRID_W, kr * kc), axis=-1).reshape(s.shape)
        return jnp.einsum('bhcrj,bhrcjd->bhcd', p.astype(v.dtype), vb)

    out = lax.map(row_block, jnp.arange(rows))
    return jnp.moveaxis(out, 0, 2).reshape(b_, h_, s_, d_)

def conv_glu(h, w_up, conv_w, conv_b, w_down):
    u, g = jnp.split(h @ w_up, 2, axis=-1)
    s_ = g.shape[1]
    pad = CONV_W // 2
    gp = jnp.pad(g, ((0, 0), (pad, pad), (0, 0)))
    g = sum(gp[:, j:j + s_] * conv_w[j] for j in range(CONV_W)) + conv_b
    return (jax.nn.gelu(g, approximate=False) * u) @ w_down

def first_inputs(seed: int = 0) -> dict:
    key = jax.random.key(seed)
    ks = jax.random.split(key, 20)
    nrm = jax.random.normal
    f32 = jnp.float32
    x = nrm(ks[0], (BATCH, SEQ, D_MODEL), f32)
    c = nrm(ks[1], (BATCH, D_MODEL), f32)
    w_ada = nrm(ks[2], (DEPTH, D_MODEL, N_MOD * D_MODEL), f32) * (0.5 * D_MODEL ** -0.5)
    b_ada = nrm(ks[3], (DEPTH, N_MOD * D_MODEL), f32) * 0.02
    g_norm1 = 1.0 + 0.02 * nrm(ks[4], (DEPTH, D_MODEL), f32)
    w_in = nrm(ks[5], (DEPTH, D_MODEL, IN_COLS), f32) * D_MODEL ** -0.5
    gk = jax.random.split(ks[6], 4)
    b_gates = jnp.concatenate([
        0.1 * nrm(gk[0], (DEPTH, NH_A), f32),
        3.0 + 0.5 * nrm(gk[1], (DEPTH, NH_A), f32),
        0.1 * nrm(gk[2], (DEPTH, NH_A), f32),
        3.0 + 0.5 * nrm(gk[3], (DEPTH, NH_A), f32),
    ], axis=-1)
    g_head_a = 1.0 + 0.02 * nrm(ks[7], (DEPTH, W_A), f32)
    rpb = 0.1 * nrm(ks[8], (DEPTH, NH_B, 2 * WIN_ROWS_MAX - 1, 2 * WIN_COLS - 1), f32)
    w_out = nrm(ks[9], (DEPTH, D_MIX, D_MODEL), f32) * D_MIX ** -0.5
    g_norm2 = 1.0 + 0.02 * nrm(ks[10], (DEPTH, D_MODEL), f32)
    w_up = nrm(ks[11], (DEPTH, D_MODEL, 2 * D_FF), f32) * D_MODEL ** -0.5
    conv_w = nrm(ks[12], (DEPTH, CONV_W, D_FF), f32) * CONV_W ** -0.5
    conv_b = 0.02 * nrm(ks[13], (DEPTH, D_FF), f32)
    w_down = nrm(ks[14], (DEPTH, D_FF, D_MODEL), f32) * D_FF ** -0.5
    g_final = 1.0 + 0.02 * nrm(ks[15], (D_MODEL,), f32)
    return {'x': x, 'c': c, 'w_ada': w_ada, 'b_ada': b_ada, 'g_norm1': g_norm1, 'w_in': w_in,
            'b_gates': b_gates, 'g_head_a': g_head_a, 'rpb': rpb, 'w_out': w_out, 'g_norm2': g_norm2,
            'w_up': w_up, 'conv_w': conv_w, 'conv_b': conv_b, 'w_down': w_down, 'g_final': g_final}

def first_block(x, c, w_ada, b_ada, g_norm1, w_in, b_gates, g_head_a, rpb, w_out, g_norm2,
              w_up, conv_w, conv_b, w_down, g_final):
    f32 = jnp.float32
    for l in range(DEPTH):
        mod = jax.nn.silu(c) @ w_ada[l] + b_ada[l]
        sh1, sc1, ga1, sh2, sc2, ga2 = jnp.split(mod, N_MOD, axis=-1)

        h = modulate(rms_norm(x, g_norm1[l]), sh1, sc1)
        qa, ka, va, oa, gates, qb, kb, vb = jnp.split(h @ w_in[l], IN_SPLITS, axis=-1)

        q_a = to_heads(qa, NH_A).astype(f32)
        k_a = to_heads(ka, NH_A).astype(f32) * (DH_A ** -0.5)
        v_a = to_heads(va, NH_A).astype(f32)
        g_a = (gates.astype(f32) + b_gates[l].astype(f32)).transpose(0, 2, 1)
        h_a = mlstm_bidirectional(q_a, k_a, v_a, g_a)
        h_a = h_a * lax.rsqrt(jnp.mean(h_a * h_a, axis=-1, keepdims=True) + EPS)
        h_a = (from_heads(h_a) * g_head_a[l] * jax.nn.sigmoid(oa.astype(f32))).astype(x.dtype)

        h_b = from_heads(neighborhood_attention(to_heads(qb, NH_B), to_heads(kb, NH_B),
                                                to_heads(vb, NH_B), rpb[l])).astype(x.dtype)

        mixed = jnp.concatenate([h_a, h_b], axis=-1) @ w_out[l]
        x = x + ga1[:, None, :] * mixed

        h = modulate(rms_norm(x, g_norm2[l]), sh2, sc2)
        x = x + ga2[:, None, :] * conv_glu(h, w_up[l], conv_w[l], conv_b[l], w_down[l])
    return rms_norm(x, g_final)


HEAD_DIM = 64
A_Q_HEADS = 16
A_KV_HEADS = 4
A_GROUP = A_Q_HEADS // A_KV_HEADS
WINDOW = 128
B_HEADS = 16
BLOCK = 128
D_FF_2 = ((8 * D_MODEL // 3 + 255) // 256) * 256

A_Q_W = A_Q_HEADS * HEAD_DIM
A_KV_W = A_KV_HEADS * HEAD_DIM
B_W = B_HEADS * HEAD_DIM
IN_SPLITS_2 = (A_Q_W, A_KV_W, A_KV_W, B_W, B_W, B_W, D_MODEL, D_MODEL)
IN_WIDTH = sum(IN_SPLITS_2)
IN_OFFSETS = tuple(int(o) for o in np.cumsum(IN_SPLITS_2)[:-1])


def rmsnorm(x, g):
    xf = x.astype(jnp.float32)
    inv = lax.rsqrt(jnp.mean(xf * xf, axis=-1, keepdims=True) + EPS)
    return (xf * inv * g.astype(jnp.float32)).astype(x.dtype)

def alibi_slopes(n_heads):
    h = jnp.arange(1, n_heads + 1, dtype=jnp.float32)
    return jnp.exp2(-8.0 * h / n_heads)

def sliding_window_attention(q, k, v, sinks):
    B, S = q.shape[0], q.shape[1]
    nb = S // BLOCK
    qb = q.reshape(B, nb, BLOCK, A_KV_HEADS, A_GROUP, HEAD_DIM)
    kb = k.reshape(B, nb, BLOCK, A_KV_HEADS, HEAD_DIM)
    vb = v.reshape(B, nb, BLOCK, A_KV_HEADS, HEAD_DIM)
    pad_k = jnp.zeros_like(kb[:, :1])
    pad_v = jnp.zeros_like(vb[:, :1])
    kk = jnp.concatenate([jnp.concatenate([pad_k, kb[:, :-1]], axis=1), kb], axis=2)
    vv = jnp.concatenate([jnp.concatenate([pad_v, vb[:, :-1]], axis=1), vb], axis=2)

    scale = 1.0 / math.sqrt(HEAD_DIM)
    s = jnp.einsum('bnqhgd,bnkhd->bnhgqk', qb, kk).astype(jnp.float32) * scale

    qi = jnp.arange(BLOCK)[:, None]
    ki = jnp.arange(2 * BLOCK)[None, :]
    dist = (BLOCK + qi - ki)
    blk = jnp.arange(nb)[:, None, None]
    valid = (dist >= 0) & (dist < WINDOW)
    valid = valid[None] & ((blk > 0) | (ki[None] >= BLOCK))

    slopes = alibi_slopes(A_Q_HEADS).reshape(A_KV_HEADS, A_GROUP)
    s = s - slopes[:, :, None, None] * dist.astype(jnp.float32)[None, None]
    s = jnp.where(valid[None, :, None, None], s, -jnp.inf)

    sink = sinks.astype(jnp.float32).reshape(A_KV_HEADS, A_GROUP)[None, None, :, :, None, None]
    sink = jnp.broadcast_to(sink, s.shape[:-1] + (1,))
    p = jax.nn.softmax(jnp.concatenate([s, sink], axis=-1), axis=-1)[..., :-1]
    o = jnp.einsum('bnhgqk,bnkhd->bnqhgd', p.astype(v.dtype), vv)
    return o.reshape(B, S, A_Q_W)

def stick_breaking_attention(q, k, v):
    B, S = q.shape[0], q.shape[1]
    nb = S // BLOCK
    scale = 1.0 / math.sqrt(HEAD_DIM)
    qb = q.reshape(B, nb, BLOCK, B_HEADS, HEAD_DIM).transpose(1, 0, 2, 3, 4)
    kpos = jnp.arange(S)

    def one_block(args):
        qblk, i = args
        z = jnp.einsum('bqhd,bkhd->bhqk', qblk, k).astype(jnp.float32) * scale
        tpos = i * BLOCK + jnp.arange(BLOCK)
        causal = kpos[None, :] < tpos[:, None]
        log_beta = jax.nn.log_sigmoid(z)
        log_fail = jnp.where(causal, jax.nn.log_sigmoid(-z), 0.0)
        suffix = lax.cumsum(log_fail, axis=3, reverse=True) - log_fail
        a = jnp.where(causal, jnp.exp(log_beta + suffix), 0.0)
        return jnp.einsum('bhqk,bkhd->bqhd', a.astype(v.dtype), v)

    o = lax.map(one_block, (qb, jnp.arange(nb)))
    return o.transpose(1, 0, 2, 3, 4).reshape(B, S, B_W)

def swiglu(h, w_in, w_down):
    gu = h @ w_in
    gate, up = jnp.split(gu, 2, axis=-1)
    return (jax.nn.silu(gate) * up) @ w_down

def second_inputs(seed: int = 0) -> dict:
    key = jax.random.key(seed)
    ks = jax.random.split(key, 12)
    f32 = jnp.float32

    def w(k, shape, fan_in):
        return jax.random.normal(k, shape, f32) * (fan_in ** -0.5)

    def gain(k, shape):
        return 1.0 + 0.02 * jax.random.normal(k, shape, f32)

    return {
        "x": jax.random.normal(ks[0], (BATCH, SEQ, D_MODEL), f32),
        "norm_mix_g": gain(ks[1], (DEPTH, D_MODEL)),
        "w_in": w(ks[2], (DEPTH, D_MODEL, IN_WIDTH), D_MODEL),
        "sink_logits": 0.5 * jax.random.normal(ks[3], (DEPTH, A_Q_HEADS), f32),
        "w_branch_a": w(ks[4], (DEPTH, A_Q_W, D_MODEL), A_Q_W),
        "w_branch_b": w(ks[5], (DEPTH, B_W, D_MODEL), B_W),
        "w_out": w(ks[6], (DEPTH, D_MODEL, D_MODEL), D_MODEL),
        "norm_ffn_g": gain(ks[7], (DEPTH, D_MODEL)),
        "w_ffn_in": w(ks[8], (DEPTH, D_MODEL, 2 * D_FF_2), D_MODEL),
        "w_ffn_down": w(ks[9], (DEPTH, D_FF_2, D_MODEL), D_FF_2),
        "norm_final_g": gain(ks[10], (D_MODEL,)),
    }

def second_block(x, norm_mix_g, w_in, sink_logits, w_branch_a, w_branch_b, w_out,
              norm_ffn_g, w_ffn_in, w_ffn_down, norm_final_g):
    B, S, _ = x.shape
    for layer in range(DEPTH):
        h = rmsnorm(x, norm_mix_g[layer])
        proj = h @ w_in[layer]
        qa, ka, va, qb, kb, vb, ga, gb = jnp.split(proj, IN_OFFSETS, axis=-1)

        ya = sliding_window_attention(
            qa.reshape(B, S, A_Q_HEADS, HEAD_DIM),
            ka.reshape(B, S, A_KV_HEADS, HEAD_DIM),
            va.reshape(B, S, A_KV_HEADS, HEAD_DIM),
            sink_logits[layer]) @ w_branch_a[layer]
        yb = stick_breaking_attention(
            qb.reshape(B, S, B_HEADS, HEAD_DIM),
            kb.reshape(B, S, B_HEADS, HEAD_DIM),
            vb.reshape(B, S, B_HEADS, HEAD_DIM)) @ w_branch_b[layer]

        merged = jax.nn.sigmoid(ga) * ya + jax.nn.sigmoid(gb) * yb
        x = x + merged @ w_out[layer]
        x = x + swiglu(rmsnorm(x, norm_ffn_g[layer]), w_ffn_in[layer], w_ffn_down[layer])
    return rmsnorm(x, norm_final_g)


def setup_inputs(seed=0):
    out = dict(first_inputs(seed))
    for name, value in second_inputs(seed + 1).items():
        if name != "x":
            out[name + "_2"] = value
    return out


def reference(
    x, c, w_ada, b_ada, g_norm1, w_in, b_gates, g_head_a, rpb, w_out, g_norm2, w_up, conv_w,
    conv_b, w_down, g_final, norm_mix_g_2, w_in_2, sink_logits_2, w_branch_a_2, w_branch_b_2,
    w_out_2, norm_ffn_g_2, w_ffn_in_2, w_ffn_down_2, norm_final_g_2,
):
    x = first_block(
        x, c, w_ada, b_ada, g_norm1, w_in, b_gates, g_head_a, rpb, w_out, g_norm2, w_up, conv_w,
        conv_b, w_down, g_final,
    )
    return second_block(
        x, norm_mix_g_2, w_in_2, sink_logits_2, w_branch_a_2, w_branch_b_2, w_out_2,
        norm_ffn_g_2, w_ffn_in_2, w_ffn_down_2, norm_final_g_2,
    )


_drawn_inputs = setup_inputs


def setup_inputs(seed=0):
    import zlib

    import numpy as np

    out = dict(_drawn_inputs(seed))
    spreads = {}
    factors = {'g_norm1': 7.778,
     'g_head_a': 8.0,
     'rpb': 8.0,
     'g_norm2': 7.418,
     'conv_b': 8.0,
     'norm_mix_g_2': 5.243,
     'sink_logits_2': 20.412,
     'norm_ffn_g_2': 4.088,
     'norm_final_g_2': 7.626}
    for name, (base, spread) in spreads.items():
        noise = np.random.default_rng([zlib.crc32(name.encode()), seed]).standard_normal(out[name].shape)
        drawn = base * np.exp(spread * noise) if base else spread * noise
        out[name] = __import__('jax').numpy.asarray(drawn.astype(out[name].dtype))
    for name, factor in factors.items():
        out[name] = (out[name] * factor).astype(out[name].dtype)
    return out
```

```python
from contextlib import ExitStack

import concourse.bass as bass
from concourse import mybir

F32 = mybir.dt.float32
F32R = mybir.dt.float32r
I32 = mybir.dt.int32
ALU = mybir.AluOpType
ACT = mybir.ActivationFunctionType
AX_X = mybir.AxisListType.X

P = 128
S = 256
ST = S // P
CW = 512
KB = 2
RING = 4
NEG = -1e30
EPS = 1e-6
ADA_W = 1024


class Gemm:

    def __init__(self, w, chunks, block0, chunk0, col0, col_e, col_i):
        self.w = w.rearrange("(t p) n -> p t n", p=P)
        self.kts = w.shape[0] // P
        self.nb = self.kts // KB
        self.chunks, self.block0, self.chunk0 = chunks, block0, chunk0
        self.col0, self.col_e, self.col_i = col0, col_e, col_i
        assert (2 * self.nb) % RING == 0 and block0 % RING == 0

    def block(self, i, e, j):
        return self.block0 + e * self.nb + j + i * (2 * self.nb)

    def slot(self, e, j):
        return (e * self.nb + j) % RING

    def turn(self, i, e, j):
        return self.block0 // RING + (e * self.nb + j) // RING + i * (2 * self.nb // RING)

    def done(self, i, e):
        return self.block0 + (e + 1) * self.nb + i * (2 * self.nb)

    def chunk(self, i, e):
        return self.chunk0 + e + i * 2

    def bank(self, e):
        return (self.chunk0 + e) % 2

    def col(self, i, e):
        return self.col0 + e * self.col_e + i * self.col_i


def walk(eng, chunks, step):
    step(0, 0, True)
    pairs = (chunks - 1) // 2
    if pairs > 1:
        with eng.Fori(0, pairs) as i:
            step(i, 1, False)
            step(i + 1, 0, False)
    elif pairs == 1:
        step(0, 1, False)
        step(1, 0, False)
    if chunks % 2 == 0:
        step((chunks - 1) // 2, 1, False)


def two_blocks(nc, x, c, w_ada, b_ada, g_norm1, w_in, b_gates, g_head_a, rpb, w_out, g_norm2, w_up,
               conv_w, conv_b, w_down, g_final, norm_mix_g_2, w_in_2, sink_logits_2, w_branch_a_2,
               w_branch_b_2, w_out_2, norm_ffn_g_2, w_ffn_in_2, w_ffn_down_2, norm_final_g_2, out):
    D = x.shape[2]
    DT = D // P
    F = w_down.shape[1]
    FT = F // P
    HA = b_gates.shape[1] // 4
    DA = g_head_a.shape[1] // HA
    WA = HA * DA
    HB = rpb.shape[1]
    RR, RC = rpb.shape[2], rpb.shape[3]
    GW = 64
    GR = S // GW
    WC = 16
    DB = WA // HB
    HS, HK, DH = 16, 4, 64
    NJ = GR + 2
    w_ada, w_in, w_out, w_up, w_down = w_ada[0], w_in[0], w_out[0], w_up[0], w_down[0]
    w_in_2, w_out_2, w_ffn_in_2, w_ffn_down_2 = w_in_2[0], w_out_2[0], w_ffn_in_2[0], w_ffn_down_2[0]
    w_branch_a_2, w_branch_b_2 = w_branch_a_2[0], w_branch_b_2[0]
    GATES0 = 4 * WA
    QB0 = GATES0

    gemms = []

    def gemm(w, chunks, col0=0, col_e=CW, col_i=2 * CW):
        last = gemms[-1] if gemms else None
        g = Gemm(w, chunks, last.block0 + last.chunks * last.nb if last else 0,
                 last.chunk0 + last.chunks if last else 0, col0, col_e, col_i)
        gemms.append(g)
        return g

    g_in_a = gemm(w_in, GATES0 // CW)
    g_in_b = gemm(w_in, 3 * WA // CW, col0=GATES0 + 4 * HA)
    g_out = gemm(w_out, D // CW)
    g_up = gemm(w_up, 2 * F // CW, col_e=F, col_i=CW)
    g_down = gemm(w_down, D // CW)
    g_in2 = gemm(w_in_2, w_in_2.shape[1] // CW)
    g_bra = gemm(w_branch_a_2, D // CW)
    g_brb = gemm(w_branch_b_2, D // CW)
    g_out2 = gemm(w_out_2, D // CW)
    g_up2 = gemm(w_ffn_in_2, 2 * F // CW, col_e=F, col_i=CW)
    g_down2 = gemm(w_ffn_down_2, D // CW)

    ctx = ExitStack()

    def sb(name, shape, dt=F32, scope=ctx):
        return scope.enter_context(nc.sbuf_tensor(name, shape, dt))

    def sem(name):
        return ctx.enter_context(nc.semaphore(name))

    with ctx:
        raw = sb("raw", [P, RING, KB, CW])
        w_hi = sb("w_hi", [P, RING, KB, CW], F32R)
        w_lo = sb("w_lo", [P, RING, KB, CW], F32R)
        xres = sb("xres", [P, ST, D])
        h_hi = sb("h_hi", [P, DT, S], F32R)
        h_lo = sb("h_lo", [P, DT, S], F32R)
        gate2 = sb("gate2", [P, D])
        ident = sb("ident", [P, P])
        ones = sb("ones", [P, P])
        diag = sb("diag", [P, ST, P])
        vcol = sb("vcol", [P, 3, 88])
        stat = sb("stat", [P, 16])
        mod = sb("mod", [P, 4, DT])
        c_act = sb("c_act", [P, DT])
        VC = {"c": 0, "g1": 16, "g2": 32, "mixg": 48, "ffng": 64, "ghead": 80}

        s1 = ExitStack()
        proj = sb("proj", [P, ST, 7 * WA], scope=s1)
        ga1 = sb("ga1", [P, D], scope=s1)
        acc = sb("acc", [P, 4, ADA_W], scope=s1)
        ada_ring = sb("ada_ring", [P, 2, ADA_W], scope=s1)
        sel = sb("sel", [HA, HA, P], scope=s1)
        flip = sb("flip", [P, P], scope=s1)
        mask_f = sb("mask_f", [P, S], scope=s1)
        mask_b = sb("mask_b", [P, S], scope=s1)
        gsb = sb("gsb", [P, ST, 4 * HA], scope=s1)
        gcol = sb("gcol", [P, ST, 4, HA], scope=s1)
        bg = sb("bg", [HA, 4], scope=s1)
        hcol = sb("hcol", [P, 3, 8], scope=s1)
        nst = sb("nst", [P, 2, 3, 2], scope=s1)
        ada_first = proj[:, :, :].rearrange("p a b -> p (a b)")[:, 0:8 * ADA_W].rearrange(
            "p (s n) -> p s n", s=8)
        vrows = proj[0:88, 1, 1536:1536 + 3 * P].rearrange("p (a b) -> p a b", a=3)
        wg = proj[:, 1, 2048:2048 + DT * 4 * HA].rearrange("p (t n) -> p t n", t=DT)
        wg_hi = sb("wg_hi", [P, DT, 4 * HA], F32R, scope=s1)
        wg_lo = sb("wg_lo", [P, DT, 4 * HA], F32R, scope=s1)
        accf = acc[:, :, :].rearrange("p a b -> p (a b)")
        hf = accf[:, 0:1024].rearrange("p (b a s) -> p b a s", b=2, a=2)
        ml_qk = accf[:, 1024:2048].rearrange("p (q d s) -> p q d s", q=2, d=2)
        ml_e = accf[:, 2048:2048 + 768]
        GTR = accf[0:HA, 2816:3840].rearrange("p (y s) -> p y s", y=4)
        ga_t = accf[0:HA, 0:1024].rearrange("p (y s) -> p y s", y=4)
        na_qk = accf[:, 0:1024].rearrange("p (b q s) -> p b q s", b=2, q=2)
        na_sc = accf[:, 1024:2048].rearrange("p (b t s) -> p b t s", b=2, t=2)
        na_pt = accf[:, 2048:3072].rearrange("p (b t s) -> p b t s", b=2, t=2)
        na_bias = accf[:, 3072:3072 + 2 * NJ * GW].rearrange("p (b j c) -> p b j c", b=2, j=NJ)
        xt1 = accf[:, 0:2048].rearrange("p (b t n) -> p b t n", b=2, t=2)
        s1.close()

        s2 = ExitStack()
        a_hi = sb("a_hi", [P, FT, S], F32R, scope=s2)
        a_lo = sb("a_lo", [P, FT, S], F32R, scope=s2)
        ff = sb("ff", [P, 2, ST, CW], scope=s2)
        hf_ff = ff[:, 0].rearrange("p b (a s) -> p b a s", a=2)
        g4 = ff[:, 1].rearrange("p t (a s) -> p (t a) s", a=2)
        s2.close()

        s3 = ExitStack()
        proj2 = sb("proj2", [P, ST, w_in_2.shape[1]], scope=s3)
        tmp = sb("tmp", [P, 7680], scope=s3)
        sink = sb("sink", [P, HS], scope=s3)
        hf_tmp = tmp[:, 0:1024].rearrange("p (b a s) -> p b a s", b=2, a=2)
        s3.close()

        gp = [ctx.enter_context(nc.psum_tensor(f"gp{i}", [P, ST, CW], F32)) for i in range(2)]
        tp = ctx.enter_context(nc.psum_tensor("tp", [P, 4, CW], F32))

        raw_landed = [sem(f"raw_landed{i}") for i in range(RING)]
        hi_ready = sem("hi_ready")
        lo_ready = sem("lo_ready")
        block_used = sem("block_used")
        drained = [sem(f"drained{i}") for i in range(ST)]
        ada1_landed = [sem(f"ada1_landed{i}") for i in range(8)]
        ada_landed = [sem(f"ada_landed{i}") for i in range(2)]
        ada_summed = sem("ada_summed")
        acc_clear = sem("acc_clear")
        acc_bias = [sem(f"acc_bias{i}") for i in range(4)]
        mod_sum = sem("mod_sum")
        mod_ready = sem("mod_ready")
        x_landed = sem("x_landed")
        vec_landed = sem("vec_landed")
        wg_landed = sem("wg_landed")
        const_ready = sem("const_ready")
        vec_t = sem("vec_t")
        vec_ready = sem("vec_ready")
        silu_ready = sem("silu_ready")
        wg_split = sem("wg_split")
        wg_high = sem("wg_high")
        gates_mm = sem("gates_mm")
        gates_out = sem("gates_out")
        x_final = sem("x_final")
        sq_ready = sem("sq_ready")
        ms_ready = sem("ms_ready")
        rms_ready = sem("rms_ready")
        diag_ready = sem("diag_ready")
        xt_ready = sem("xt_ready")
        h_full = sem("h_full")
        h_high = sem("h_high")
        h_ready = sem("h_ready")
        act_chain = sem("act_chain")
        dve_chain = sem("dve_chain")
        pool_chain = sem("pool_chain")
        gt_mm = sem("gt_mm")
        gt_ready = sem("gt_ready")
        gl_abs = sem("gl_abs")
        gl_ln = sem("gl_ln")
        gm_ready = sem("gm_ready")
        em_ready = sem("em_ready")
        gc_mm = sem("gc_mm")
        gc_ready = sem("gc_ready")
        ml_t = sem("ml_t")
        ml_tq = sem("ml_tq")
        ml_s = sem("ml_s")
        ml_arg = sem("ml_arg")
        ml_exp = sem("ml_exp")
        ml_p = sem("ml_p")
        ml_num = sem("ml_num")
        ml_den = sem("ml_den")
        ml_h = sem("ml_h")
        ml_sq = sem("ml_sq")
        ml_ms = sem("ml_ms")
        ml_rms = sem("ml_rms")
        ml_out = sem("ml_out")
        na_bias_landed = [sem(f"na_bias_landed{i}") for i in range(2)]
        na_bias_ready = sem("na_bias_ready")
        na_t = sem("na_t")
        na_tq = sem("na_tq")
        na_s = sem("na_s")
        na_max = sem("na_max")
        na_exp = sem("na_exp")
        na_p = sem("na_p")
        na_ptm = sem("na_ptm")
        na_ptc = sem("na_ptc")
        na_o = sem("na_o")
        na_hi = sem("na_hi")
        na_lo = sem("na_lo")
        xt_made = sem("xt_made")
        ff_conv = sem("ff_conv")
        ff_u = sem("ff_u")
        ff_g = sem("ff_g")
        ff_t = sem("ff_t")
        ff_act = sem("ff_act")
        ff_mul = sem("ff_mul")
        ff_hi = sem("ff_hi")
        ff_lo = sem("ff_lo")
        gain_landed = sem("gain_landed")
        gain_used = sem("gain_used")
        sink_landed = sem("sink_landed")
        nd_ready = sem("nd_ready")
        q2_t = sem("q2_t")
        q2_c = sem("q2_c")
        kdup_ready = sem("kdup_ready")
        sw_s = sem("sw_s")
        sw_bias = sem("sw_bias")
        sw_max = sem("sw_max")
        sw_exp = sem("sw_exp")
        sw_p = sem("sw_p")
        sw_ptm = sem("sw_ptm")
        sw_ptc = sem("sw_ptc")
        o2_mm = sem("o2_mm")
        o2_hi = sem("o2_hi")
        o2_lo = sem("o2_lo")
        sk_z = sem("sk_z")
        sk_l = sem("sk_l")
        sk_sp = sem("sk_sp")
        sk_lb = sem("sk_lb")
        sk_suf = sem("sk_suf")
        sk_arg = sem("sk_arg")
        sk_exp = sem("sk_exp")
        sk_a = sem("sk_a")
        sk_mask = sem("sk_mask")
        sig_ready = sem("sig_ready")
        merge_a = sem("merge_a")
        merge_b = sem("merge_b")
        merged = sem("merged")
        out_ready = sem("out_ready")
        out_landed = sem("out_landed")

        PART2 = 4 * DT
        PART3 = PART2 + 6 * DT
        ADA_N = PART3 + 2 * DT
        NP8 = DT // 2
        HB_NORM0, HB_ML, HB_NORM1, HB_NORM2 = 0, NP8, NP8 + 4, 2 * NP8 + 4
        HB_MERGE, HB_NORM3 = 3 * NP8 + 4, 4 * NP8 + 4

        def carve(a, n):
            return tmp[:, a:a + n]
        Q2 = carve(0, 2048).rearrange("p (t s) -> p t s", t=8)
        K2 = carve(2048, 2048).rearrange("p (t s) -> p t s", t=8)
        kdup = carve(4096, 1024).rearrange("p (t g u d) -> p t g u d", t=ST, g=HK, u=2)
        ND = carve(4096 + 1024, 384)
        NDI = carve(4096 + 1024 + 384, 384)
        TB = carve(2048 + 1024, 768).rearrange("p (b n) -> p b n", b=2)
        SC = carve(5888, 768).rearrange("p (b n) -> p b n", b=2)
        PT = carve(5888 + 768, 768).rearrange("p (b n) -> p b n", b=2)
        SW = carve(7424, 64).rearrange("p (b a n) -> p b a n", b=2, a=4)
        LL = carve(4096, 768).rearrange("p (b n) -> p b n", b=2)
        SP_ = carve(4864, 768).rearrange("p (b n) -> p b n", b=2)
        LB = carve(5888, 768).rearrange("p (b n) -> p b n", b=2)
        AA = carve(5888 + 768, 768).rearrange("p (b n) -> p b n", b=2)
        M2 = gate2[:, 0:256].rearrange("p (a b) -> p a b", a=2)
        TRI = gate2[:, 256:384]
        QA2, KA2 = 0, HS * DH
        VA2 = KA2 + HK * DH
        QS2 = VA2 + HK * DH
        KS2, VS2 = QS2 + HS * DH, QS2 + 2 * HS * DH
        GA2 = QS2 + 3 * HS * DH
        GB2 = GA2 + D
        SW_N = S + P

        def chain(sem_, eng):
            count = [0]

            def link(ins):
                count[0] += 1
                ins.then_inc(sem_, 1)
                eng.wait_ge(sem_, count[0])
            return link

        block = ctx.enter_context(nc.Block())

        @block.sync
        def _(sp):
            def load(g, i, e, j):
                b = g.block(i, e, j)
                if not isinstance(b, int) or b >= RING:
                    sp.wait_ge(lo_ready, b - (RING - 1))
                s = g.slot(e, j)
                sp.dma_start(raw[:, s], g.w[:, j * KB:(j + 1) * KB, bass.ds(g.col(i, e), CW)]
                             ).then_inc(raw_landed[s], 16)

            def ada(a, slot, k, col):
                if not isinstance(a, int) or a >= PART2 + 2:
                    sp.wait_ge(ada_summed, a - 1)
                sp.dma_start(ada_ring[:, slot, :], w_ada[bass.ds(k * P, P), col:col + ADA_W]
                             ).then_inc(ada_landed[slot], 16)

            sp.dma_start(xres[:, 0, :], x[0, 0:P, :]).then_inc(x_landed, 16)
            sp.dma_start(xres[:, 1, :], x[0, P:S, :]).then_inc(x_landed, 16)
            for k in range(2):
                for p in range(4):
                    sp.dma_start(ada_first[:, 4 * k + p, :],
                                 w_ada[k * P:(k + 1) * P, p * ADA_W:(p + 1) * ADA_W]
                                 ).then_inc(ada1_landed[4 * k + p], 16)
            with sp.Fori(1, DT // 2) as i:
                for k in range(2):
                    for p in range(4):
                        sp.wait_ge(ada_summed, i * 8 + (4 * k + p - 7))
                        sp.dma_start(ada_first[:, 4 * k + p, :],
                                     w_ada[bass.ds(i * 2 * P + k * P, P), p * ADA_W:(p + 1) * ADA_W]
                                     ).then_inc(ada1_landed[4 * k + p], 16)

            def prime(g):
                for j in range(RING):
                    load(g, 0, 0, j)

            def stream(g, side=None, nxt=None):
                def step(i, e, first):
                    for j in range(g.nb):
                        if not (first and j < RING):
                            load(g, i, e, j)
                        if side:
                            side(i, e, j)
                walk(sp, g.chunks, step)
                if nxt:
                    prime(nxt)

            def ada_in(k0):
                def side(i, e, j):
                    if j < 6:
                        ada(i * 12 + (PART2 + 6 * (k0 + e) + j), j % 2, i * 2 + (k0 + e), 2 * D + j * ADA_W)
                return side

            def ada_out(i, e, j):
                ada(i * 16 + (PART3 + 8 * e + j), j % 2, i * 8 + (4 * e + j // 2), 5 * D + (j % 2) * ADA_W)

            prime(g_in_a)
            stream(g_in_a, ada_in(0), g_in_b)
            stream(g_in_b, ada_in(g_in_a.chunks), g_out)
            for k in range(g_in_a.chunks + g_in_b.chunks, DT):
                for j in range(6):
                    ada(PART2 + 6 * k + j, j % 2, k, 2 * D + j * ADA_W)
            for n in range(HB):
                if n >= 2:
                    sp.wait_ge(na_s, n - 1)
                else:
                    sp.wait_ge(ml_out, 1)
                for a in range(2):
                    src = bass.AP(tensor=rpb.tensor, offset=rpb.offset + n * RR * RC
                                  + (RR // 2 - 2 - a) * RC + RC // 2 - (GW - 1),
                                  ap=[[1, GW], [RC, NJ], [1, GW]])
                    sp.dma_start(na_bias[a * GW:(a + 1) * GW, n % 2], src
                                 ).then_inc(na_bias_landed[n % 2], 16)
            stream(g_out, ada_out, g_up)
            stream(g_up, None, g_down)
            stream(g_down, None, g_in2)
            sp.wait_ge(drained[1], g_down.chunk0 + g_down.chunks)
            sp.dma_start(gate2[:, :], bass.AP(tensor=g_final.tensor, offset=g_final.offset,
                                              ap=[[0, P], [1, D]])).then_inc(gain_landed, 16)
            sp.wait_ge(x_final, 2 * (g_out.chunks + g_down.chunks))
            sp.dma_start(sink[:, :], bass.AP(tensor=sink_logits_2.tensor, offset=sink_logits_2.offset,
                                             ap=[[0, P], [1, HS]])).then_inc(sink_landed, 16)
            stream(g_in2, None, g_bra)
            stream(g_bra, None, g_brb)
            stream(g_brb, None, g_out2)
            sp.wait_ge(sk_a, HS)
            sp.wait_ge(sk_suf, HS)
            sp.dma_start(gate2[:, :], bass.AP(tensor=norm_final_g_2.tensor, offset=norm_final_g_2.offset,
                                              ap=[[0, P], [1, D]])).then_inc(gain_landed, 16)
            stream(g_out2, None, g_up2)
            stream(g_up2, None, g_down2)
            stream(g_down2)
            for t in range(ST):
                for q in range(2):
                    sp.wait_ge(out_ready, 2 * t + q + 1)
                    sp.dma_start(out[0, t * P:(t + 1) * P, q * (D // 2):(q + 1) * (D // 2)],
                                 xres[:, t, q * (D // 2):(q + 1) * (D // 2)]).then_inc(out_landed, 16)
            sp.wait_ge(out_landed, 16 * 2 * ST)

        @block.gpsimd
        def _(pool):
            link = chain(pool_chain, pool)

            def pred(ap, cmp, fill, base, pattern, mul):
                link(nc.gpsimd.affine_select(out=ap, in_=ap, compare_op=cmp, fill=fill, base=base,
                                             pattern=pattern, channel_multiplier=mul))
            def rows(tile, r, vec):
                n = vec.shape[0] // P
                pool.dma_start(vrows[r:r + n, tile, :], vec.rearrange("(t p) -> t p", p=P)
                               ).then_inc(vec_landed, 16)
            rows(0, VC["c"], c[0])
            rows(0, VC["g1"], g_norm1[0])
            rows(0, VC["g2"], g_norm2[0])
            rows(0, VC["mixg"], norm_mix_g_2[0])
            rows(0, VC["ffng"], norm_ffn_g_2[0])
            rows(0, VC["ghead"], g_head_a[0])
            rows(1, 0, conv_w[0, 0])
            rows(1, FT, conv_w[0, 1])
            rows(2, 0, conv_w[0, 2])
            rows(2, FT, conv_b[0])
            with nc.allow_non_contiguous_dma(reason="gate columns"):
                pool.dma_start(wg, w_in.rearrange("(t p) n -> p t n", p=P)[:, :, GATES0:GATES0 + 4 * HA]
                               ).then_inc(wg_landed, 16)
                pool.dma_start(bg[:, :], b_gates[0].rearrange("(y h) -> h y", h=HA)).then_inc(wg_landed, 16)
            link(nc.gpsimd.memset(ident[:, :], 0.0))
            pred(ident[:, :], ALU.not_equal, 1.0, 0, [[-1, P]], 1)
            link(nc.gpsimd.memset(acc[:, :, :], 0.0))
            pool.dma_start(accf[0:1, :], b_ada[0:1, 0:2 * D]).then_inc(acc_bias[0], 16)
            nc.gpsimd.memset(ones[:, :], 1.0).then_inc(const_ready, 1)
            link(nc.gpsimd.memset(sel[:, :, :], 0.0))
            pred(sel[:, :, :], ALU.not_equal, 1.0, 0, [[-1, HA], [0, P]], 1)
            link(nc.gpsimd.memset(flip[:, :], 0.0))
            pred(flip[:, :], ALU.not_equal, 1.0, -(GW - 1), [[1, P]], 1)
            pred(flip[:, :], ALU.not_equal, 1.0, -(3 * GW - 1), [[1, P]], 1)
            link(nc.gpsimd.memset(mask_f[:, :], 0.0))
            pred(mask_f[:, 0:P], ALU.is_ge, NEG, 0, [[1, P]], -1)
            link(nc.gpsimd.memset(mask_b[:, :], 0.0))
            nc.gpsimd.affine_select(out=mask_b[:, P:S], in_=mask_b[:, P:S], compare_op=ALU.is_ge, fill=NEG,
                                    base=0, pattern=[[-1, P]], channel_multiplier=1
                                    ).then_inc(const_ready, 1)
            link(nc.gpsimd.memset(ga1[:, :], 0.0))
            pool.dma_start(ga1[0:1, :], b_ada[0:1, 2 * D:3 * D]).then_inc(acc_bias[1], 16)
            link(nc.gpsimd.memset(gate2[:, :], 0.0))
            pool.dma_start(gate2[0:1, :], b_ada[0:1, 5 * D:6 * D]).then_inc(acc_bias[2], 16)
            pool.wait_ge(mod_ready, 1)
            pool.wait_ge(h_ready, NP8)
            link(nc.gpsimd.memset(acc[:, :, :], 0.0))
            pool.dma_start(accf[0:1, :], b_ada[0:1, 3 * D:5 * D]).then_inc(acc_bias[3], 16)
            for n in range(HB):
                pool.wait_ge(na_bias_landed[n % 2], 32 * (n // 2 + 1))
                for a in range(2):
                    v = na_bias[a * GW:(a + 1) * GW, n % 2]
                    pred(v[:, :, 0:GW - WC], ALU.is_ge, NEG, WC // 2 - (GW - 1), [[0, NJ], [1, GW - WC]], 1)
                    right = v[:, :, WC:GW]
                    nc.gpsimd.affine_select(out=right, in_=right, compare_op=ALU.is_ge, fill=NEG,
                                            base=GW - 1 + WC // 2 - 1 - WC, pattern=[[0, NJ], [-1, GW - WC]],
                                            channel_multiplier=-1).then_inc(na_bias_ready, 1)

            def add_x(g, buf):
                def step(i, e, first):
                    for t in range(ST):
                        pool.wait_ge(drained[t], g.chunk(i, e) + 1)
                        xs = xres[:, t, bass.ds(g.col(i, e), CW)]
                        nc.gpsimd.tensor_tensor(xs, xs, buf[:, e, t, :], ALU.add).then_inc(x_final, 1)
                walk(pool, g.chunks, step)
            add_x(g_out, xt1)
            add_x(g_down, ff)
            pool.wait_ge(gain_used, ST)
            for a, base in ((0, 0), (P, -P)):
                n = P if a == 0 else S
                nd = ND[:, a:a + n]
                link(nc.gpsimd.iota(NDI[:, a:a + n].bitcast(I32), [[1, n]], base=base, channel_multiplier=-1))
                link(nc.gpsimd.tensor_copy(nd, NDI[:, a:a + n].bitcast(I32)))
                pred(nd, ALU.is_ge, NEG, -base, [[-1, n]], 1)
                if a:
                    pred(nd, ALU.is_ge, NEG, P - 1 + base, [[1, n]], -1)
            link(nc.gpsimd.memset(M2, 1.0))
            pred(M2, ALU.is_gt, 0.0, 0, [[0, 2], [1, P]], -1)
            link(nc.gpsimd.memset(TRI, 1.0))
            nc.gpsimd.affine_select(out=TRI, in_=TRI, compare_op=ALU.is_gt, fill=0.0, base=0,
                                    pattern=[[-1, P]], channel_multiplier=1).then_inc(sk_mask, 1)
            pool.wait_ge(q2_c, 6)
            for h in range(HS):
                if h >= 2:
                    pool.wait_ge(sw_max, h - 1)
                slope = 2.0 ** (-8.0 * (h + 1) / HS)
                nc.gpsimd.tensor_scalar(TB[:, h % 2], ND, slope, None, ALU.mult).then_inc(sw_bias, 1)
            for h in range(HS):
                pool.wait_ge(sk_exp, h + 1)
                av = AA[:, h % 2].rearrange("p (a b) -> p a b", a=3)[:, 0:3:2, :]
                nc.gpsimd.tensor_tensor(av, av, M2, ALU.mult).then_inc(sk_a, 1)

            def step_b(i, e, first):
                for t in range(ST):
                    pool.wait_ge(drained[t], g_brb.chunk(i, e) + 1)
                    m = proj2[:, t, bass.ds(GA2 + g_brb.col(i, e), CW)]
                    nc.gpsimd.tensor_tensor(m, m, proj2[:, t, bass.ds(GB2 + g_brb.col(i, e), CW)],
                                            ALU.add).then_inc(merged, 1)
            walk(pool, g_brb.chunks, step_b)

        @block.scalar
        def _(act):
            link = chain(act_chain, act)

            def split(g, i, e, j):
                b, s = g.block(i, e, j), g.slot(e, j)
                act.wait_ge(raw_landed[s], 16 * (g.turn(i, e, j) + 1))
                if not isinstance(b, int) or b >= RING:
                    act.wait_ge(block_used, b - (RING - 1))
                nc.scalar.copy(w_hi[:, s], raw[:, s]).then_inc(hi_ready, 1)

            def prime(g):
                for j in range(RING):
                    split(g, 0, 0, j)

            def stream(g, drain, side=None, nxt=None):
                def step(i, e, first):
                    for j in range(g.nb):
                        if not (first and j < RING):
                            split(g, i, e, j)
                        if j == RING - 1 and not first:
                            drain(i if e else i - 1, 1 - e)
                    if side and not first and e == 0:
                        side(i - 1)
                walk(act, g.chunks, step)
                if nxt:
                    prime(nxt)
                drain((g.chunks - 1) // 2, (g.chunks - 1) % 2)
                if side:
                    side(g.chunks // 2 - 1)

            def chunk_done(g, i, e):
                act.wait_ge(block_used, g.done(i, e))

            def drain_proj(g, dst, col0):
                def drain(i, e):
                    chunk_done(g, i, e)
                    nc.scalar.copy(dst[:, 0, bass.ds(col0 + i * 2 * CW + e * CW, CW)], gp[g.bank(e)][:, 0, :]
                                   ).then_inc(drained[0], 1)
                return drain

            def square(n):
                for t in range(ST):
                    nc.scalar.activation(tp[:, :, :].rearrange("p a b -> p (a b)"), xres[:, t, :],
                                         ACT.Square, accum_out=stat[:, t:t + 1]).then_inc(sq_ready, 1)
                    act.wait_ge(sq_ready, ST * n + t + 1)
                act.wait_ge(ms_ready, n + 1)
                nc.scalar.activation(stat[:, 4:6], stat[:, 2:4], ACT.Sqrt).then_inc(rms_ready, 1)

            def high(base, n, kt0, src):
                for kp in range(n):
                    act.wait_ge(h_full, base + kp + 1)
                    nc.scalar.copy(h_hi[:, kt0 + 2 * kp:kt0 + 2 * kp + 2, :], src[:, kp % 2]
                                   ).then_inc(h_high, 1)

            act.wait_ge(vec_t, 1)
            nc.scalar.copy(vcol[:, :, :], tp[:, 0:3, 0:88]).then_inc(vec_ready, 1)
            act.wait_ge(vec_ready, 1)
            nc.scalar.activation(c_act[:, :], vcol[:, 0, 0:DT], ACT.Silu).then_inc(silu_ready, 1)
            act.wait_ge(wg_landed, 32)
            nc.scalar.copy(wg_hi[:, :, :], wg).then_inc(wg_high, 1)
            act.wait_ge(x_landed, 32)
            square(0)
            prime(g_in_a)
            high(HB_NORM0, NP8, 0, hf)
            stream(g_in_a, drain_proj(g_in_a, proj, 0), nxt=g_in_b)
            stream(g_in_b, drain_proj(g_in_b, proj, QB0), nxt=g_out)
            act.wait_ge(gt_ready, 1)
            fg = GTR[:, 1:4:2, :]
            act.preload_act_table_set("natural_log_exp_and_others")
            link(nc.scalar.activation(ga_t[:, 0:2, :], fg, ACT.Abs))
            link(nc.scalar.activation(ga_t[:, 0:2, :], ga_t[:, 0:2, :], ACT.Exp, scale=-1.0))
            nc.scalar.activation(ga_t[:, 0:2, :], ga_t[:, 0:2, :], ACT.Ln, bias=1.0).then_inc(gl_ln, 1)
            act.wait_ge(gm_ready, 1)
            nc.scalar.activation(fg, fg, ACT.Exp, scale=-1.0).then_inc(em_ready, 1)
            for h in range(HA):
                act.wait_ge(ml_t, h + 1)
                nc.scalar.copy(ml_qk[:, 0], tp[:, 0, :].rearrange("p (d s) -> p d s", d=2)).then_inc(ml_tq, 1)
                nc.scalar.mul(ml_qk[:, 1], tp[:, 1, :].rearrange("p (d s) -> p d s", d=2), DA ** -0.5
                              ).then_inc(ml_tq, 1)
                act.wait_ge(ml_arg, h + 1)
                act.wait_ge(gc_ready, 1)
                for a, n, t, q in ((0, 256, 0, 0), (256, 128, 1, 0), (384, 128, 0, 2), (512, 256, 1, 2)):
                    nc.scalar.activation(ml_e[:, a:a + n], ml_e[:, a:a + n], ACT.Exp,
                                         bias=gcol[:, t, q, h:h + 1]).then_inc(ml_exp, 1)
                act.wait_ge(ml_num, h + 1)
                nc.scalar.activation(hcol[:, 0, 0:4], gp[1][:, 0, 0:4], ACT.Abs).then_inc(ml_den, 1)
                act.wait_ge(ml_h, h + 1)
                for t in range(ST):
                    nc.scalar.activation(gp[1][:, 1, 0:DA], proj[:, t, h * DA:(h + 1) * DA], ACT.Square,
                                         accum_out=hcol[:, 1, 2 * h + t:2 * h + t + 1]).then_inc(ml_sq, 1)
                    act.wait_ge(ml_sq, 2 * h + t + 1)
            act.wait_ge(ml_ms, 1)
            nc.scalar.activation(hcol[:, 2, :], hcol[:, 1, :], ACT.Sqrt).then_inc(ml_rms, 1)
            for t in range(ST):
                og = proj[:, t, 3 * WA:4 * WA]
                nc.scalar.activation(og, og, ACT.Sigmoid).then_inc(ml_rms, 1)
            high(HB_ML, WA // P // 2, 0, hf)
            act.preload_act_table_set("natural_log_exp_and_others")
            for step in range(HB + 3):
                n = step
                if n < HB:
                    act.wait_ge(na_t, n + 1)
                    if n < 2:
                        act.wait_ge(h_ready, HB_ML + 4)
                    nc.scalar.mul(na_qk[:, n % 2, 0], tp[:, n % 2, 0:S], DB ** -0.5).then_inc(na_tq, 1)
                    nc.scalar.copy(na_qk[:, n % 2, 1], tp[:, n % 2, S:2 * S]).then_inc(na_tq, 1)
                n = step - 1
                if 0 <= n < HB:
                    act.wait_ge(na_max, n + 1)
                    if n >= 2:
                        act.wait_ge(na_ptm, n - 1)
                    for t in range(ST):
                        nc.scalar.activation(na_sc[:, n % 2, t], tp[:, 2 + n % 2, t * S:(t + 1) * S], ACT.Exp,
                                             bias=nst[:, n % 2, 0, t:t + 1],
                                             accum_out=nst[:, n % 2, 1, t:t + 1]).then_inc(na_exp, 1)
                n = step - 2
                if 0 <= n < HB:
                    act.wait_ge(na_ptm, n + 1)
                    nc.scalar.copy(na_pt[:, n % 2], gp[0][:, n % 2, :].rearrange("p (t s) -> p t s", t=2)
                                   ).then_inc(na_ptc, 1)
                n = step - 3
                if n >= 0:
                    act.wait_ge(na_o, n + 1)
                    nc.scalar.copy(h_hi[:, HB + n, :], gp[1][:, n % 2, 0:S]).then_inc(na_hi, 1)

            def nothing(i, e):
                pass
            stream(g_out, nothing, nxt=g_up)
            act.wait_ge(x_final, 2 * g_out.chunks)
            square(1)
            high(HB_NORM1, NP8, 0, hf_ff)

            def drain_u(i, e):
                if e == 0:
                    chunk_done(g_up, i, e)
                    for t in range(ST):
                        act.wait_ge(drained[t], g_up.chunk(i, e))
                        nc.scalar.copy(ff[:, 0, t, :], gp[g_up.bank(e)][:, t, :]).then_inc(drained[t], 1)

            def glu_side(i):
                act.wait_ge(ff_conv, i * 12 + 12)
                nc.scalar.activation(g4, g4, ACT.Gelu).then_inc(ff_act, 1)
                act.wait_ge(ff_mul, i + 1)
                nc.scalar.copy(a_hi[:, bass.ds(i * 4, 4), :], g4).then_inc(ff_hi, 1)
            act.preload_act_table(ACT.Gelu)
            stream(g_up, drain_u, side=glu_side, nxt=g_down)
            stream(g_down, nothing, nxt=g_in2)
            act.wait_ge(x_final, 2 * (g_out.chunks + g_down.chunks))
            square(2)
            act.wait_ge(gain_used, ST)
            square(3)
            high(HB_NORM2, NP8, 0, hf_tmp)
            stream(g_in2, drain_proj(g_in2, proj2, 0), nxt=g_bra)
            act.preload_act_table_set("natural_log_exp_and_others")
            act.wait_ge(sink_landed, 16)
            for n in range(6):
                act.wait_ge(q2_t, n + 1)
                dst = Q2[:, 2 * n:2 * n + 2] if n < 4 else K2[:, 2 * (n - 4):2 * (n - 4) + 2]
                nc.scalar.copy(dst, tp[:, n % 4, :].rearrange("p (a s) -> p a s", a=2)).then_inc(q2_c, 1)
            for step in range(HS + 3):
                h = step - 1
                if 0 <= h < HS:
                    act.wait_ge(sw_max, h + 1)
                    for t, (a, n) in enumerate(((0, P), (P, S))):
                        nc.scalar.activation(SC[:, h % 2, a:a + n], SC[:, h % 2, a:a + n], ACT.Exp,
                                             bias=SW[:, h % 2, 1, t:t + 1], accum_out=SW[:, h % 2, 2, t:t + 1])
                    nc.scalar.activation(SW[:, h % 2, 3, 0:2], SW[:, h % 2, 1, 0:2], ACT.Exp,
                                         bias=sink[:, h:h + 1]).then_inc(sw_exp, 1)
                h = step - 2
                if 0 <= h < HS:
                    act.wait_ge(sw_ptm, h + 1)
                    nc.scalar.copy(PT[:, h % 2], gp[0][:, h % 2, 0:SW_N]).then_inc(sw_ptc, 1)
                h = step - 3
                if h >= 0 and h % 2:
                    act.wait_ge(o2_mm, h + 1)
                    nc.scalar.copy(h_hi[:, h // 2, :], gp[1][:, (h // 2) % 2, 0:S]).then_inc(o2_hi, 1)
            for n in range(8):
                act.wait_ge(q2_t, 6 + n + 1)
                src = tp[:, n % 4, :].rearrange("p (a s) -> p a s", a=2)
                if n < 4:
                    nc.scalar.copy(Q2[:, 2 * n:2 * n + 2], src).then_inc(q2_c, 1)
                else:
                    nc.scalar.mul(K2[:, 2 * (n - 4):2 * (n - 4) + 2], src, DH ** -0.5).then_inc(q2_c, 1)
            for step in range(HS + 3):
                h = step - 1
                if 0 <= h < HS:
                    act.wait_ge(sk_z, h + 1)
                    link(nc.scalar.activation(LL[:, h % 2], tp[:, h % 2, 0:SW_N], ACT.Abs))
                    link(nc.scalar.activation(LL[:, h % 2], LL[:, h % 2], ACT.Exp, scale=-1.0))
                    nc.scalar.activation(LL[:, h % 2], LL[:, h % 2], ACT.Ln, bias=1.0).then_inc(sk_l, 1)
                h = step - 2
                if 0 <= h < HS:
                    act.wait_ge(sk_arg, h + 1)
                    if h >= 2:
                        act.wait_ge(o2_mm, HS + h - 1)
                    nc.scalar.activation(AA[:, h % 2], LB[:, h % 2], ACT.Exp).then_inc(sk_exp, 1)
                h = step - 3
                if h >= 0 and h % 2:
                    act.wait_ge(o2_mm, HS + h + 1)
                    nc.scalar.copy(h_hi[:, 8 + h // 2, :], gp[1][:, (h // 2) % 2, 0:S]).then_inc(o2_hi, 1)
            for t in range(ST):
                gg = proj2[:, t, GA2:GA2 + 2 * D]
                nc.scalar.activation(gg, gg, ACT.Sigmoid).then_inc(sig_ready, 1)
            stream(g_bra, nothing, nxt=g_brb)
            stream(g_brb, nothing, nxt=g_out2)
            high(HB_MERGE, NP8, 0, hf_tmp)
            stream(g_out2, nothing, nxt=g_up2)
            for t in range(ST):
                act.wait_ge(drained[t], g_out2.chunk0 + g_out2.chunks)
            square(4)
            high(HB_NORM3, NP8, 0, hf_ff)

            def drain_gate(i, e):
                if e == 0:
                    chunk_done(g_up2, i, e)
                    for t in range(ST):
                        act.wait_ge(drained[t], g_up2.chunk(i, e))
                        nc.scalar.activation(ff[:, 0, t, :], gp[g_up2.bank(e)][:, t, :], ACT.Silu
                                             ).then_inc(drained[t], 1)

            def swiglu_side(i):
                act.wait_ge(ff_t, i + (g_up.chunks // 2 + 1))
                nc.scalar.copy(a_hi[:, bass.ds(i * 4, 4), :], tp[:, 0:2, :].rearrange(
                    "p a (b s) -> p (a b) s", b=2)).then_inc(ff_hi, 1)
            act.preload_act_table(ACT.Silu)
            stream(g_up2, drain_gate, side=swiglu_side, nxt=g_down2)
            stream(g_down2, nothing)
            for t in range(ST):
                act.wait_ge(drained[t], g_down2.chunk0 + g_down2.chunks)
            square(5)

        @block.tensor
        def _(pe):
            mm = nc.tensor.matmul

            def stream(g, hi, lo, kt0, ready, side=None):
                def step(i, e, first):
                    if not (first and g.chunk0 < 2):
                        for t in range(ST):
                            pe.wait_ge(drained[t], g.chunk(i, e) - 1)
                    for j in range(g.nb):
                        pe.wait_ge(lo_ready, g.block(i, e, j) + 1)
                        if first:
                            ready(j)
                        s = g.slot(e, j)
                        for k in range(KB):
                            kt = j * KB + k
                            for t in range(ST):
                                ps = slice(t * P, (t + 1) * P)
                                o = gp[g.bank(e)][:, t, :]
                                mm(o, hi[:, kt0 + kt, ps], w_hi[:, s, k, :], start=kt == 0, stop=False)
                                mm(o, hi[:, kt0 + kt, ps], w_lo[:, s, k, :], start=False, stop=False)
                                last = mm(o, lo[:, kt0 + kt, ps], w_hi[:, s, k, :], start=False,
                                          stop=kt == g.kts - 1)
                        last.then_inc(block_used, 1)
                        if side and e == 0 and not first and j == 3:
                            side(i - 1)
                walk(pe, g.chunks, step)
                if side:
                    side(g.chunks // 2 - 1)

            def h_pairs(base):
                return lambda j: pe.wait_ge(h_ready, base + j + 1)

            def transpose_x(n, base):
                pe.wait_ge(diag_ready, ST * (n + 1))
                for kp in range(NP8):
                    if kp >= 4:
                        pe.wait_ge(h_full, base + kp - 3)
                    for a in range(2):
                        kt = 2 * kp + a
                        for t in range(ST):
                            last = mm(tp[:, kp % 4, a * S + t * P:a * S + (t + 1) * P],
                                      xres[:, t, kt * P:(kt + 1) * P], diag[:, t, :], start=True, stop=True)
                    last.then_inc(xt_ready, 1)

            def transpose_in(base, n, src, col0):
                for kp in range(n):
                    if kp >= 4:
                        pe.wait_ge(h_full, base + kp - 3)
                    for a in range(2):
                        kt = 2 * kp + a
                        for t in range(ST):
                            last = nc.tensor.transpose(tp[:, kp % 4, a * S + t * P:a * S + (t + 1) * P],
                                                       src[:, t, col0 + kt * P:col0 + (kt + 1) * P], ident[:, :])
                    last.then_inc(xt_ready, 1)

            def sum_columns():
                for q in range(2 * DT):
                    last = mm(tp[:, 3, q:q + 1], acc[:, q // 8, (q % 8) * P:(q % 8 + 1) * P], ones[:, 0:1],
                              start=True, stop=True)
                return last

            def sum_broadcast(src):
                for q in range(4):
                    last = mm(gp[q // 2][:, q % 2, :], ones[:, :], src[:, q * CW:(q + 1) * CW],
                              start=True, stop=True)
                return last

            pe.wait_ge(const_ready, 1)
            pe.wait_ge(vec_landed, 160)
            for n in range(3):
                last = nc.tensor.transpose(tp[:, n, 0:88], vrows[:, n, :], ident[0:88, 0:88])
            last.then_inc(vec_t, 1)
            pe.wait_ge(ada_summed, PART2)
            pe.wait_ge(sq_ready, ST)
            sum_columns().then_inc(mod_sum, 1)
            pe.wait_ge(mod_ready, 1)
            transpose_x(0, HB_NORM0)
            stream(g_in_a, h_hi, h_lo, 0, h_pairs(HB_NORM0))
            pe.wait_ge(wg_split, 1)
            for t in range(ST):
                ps = slice(t * P, (t + 1) * P)
                o = tp[:, 0, t * 4 * HA:(t + 1) * 4 * HA]
                for kt in range(DT):
                    mm(o, h_hi[:, kt, ps], wg_hi[:, kt, :], start=kt == 0, stop=False)
                    mm(o, h_hi[:, kt, ps], wg_lo[:, kt, :], start=False, stop=False)
                    last = mm(o, h_lo[:, kt, ps], wg_hi[:, kt, :], start=False, stop=kt == DT - 1)
            last.then_inc(gates_mm, 1)
            stream(g_in_b, h_hi, h_lo, 0, lambda j: None)
            pe.wait_ge(ada_summed, PART3)
            for t in range(ST):
                pe.wait_ge(drained[t], g_out.chunk0)
            sum_broadcast(ga1)
            sum_columns().then_inc(mod_sum, 1)
            pe.wait_ge(gates_out, 1)
            for y in range(4):
                for t in range(ST):
                    last = nc.tensor.transpose(tp[0:HA, 1 + y // 2, (y % 2) * S + t * P:(y % 2) * S + (t + 1) * P],
                                               gsb[:, t, y * HA:(y + 1) * HA], ident[:, :])
            last.then_inc(gt_mm, 1)
            pe.wait_ge(em_ready, 1)
            for t in range(ST):
                for y in range(4):
                    q = (t * 4 + y) * HA
                    last = nc.tensor.transpose(tp[:, 0, q:q + HA], GTR[:, y, t * P:(t + 1) * P],
                                               ident[0:HA, 0:HA])
            last.then_inc(gc_mm, 1)
            pe.wait_ge(gc_ready, 1)
            pe.wait_ge(mod_ready, 3)
            for h in range(HA):
                if h:
                    pe.wait_ge(ml_tq, 2 * h)
                for q in range(2):
                    for d in range(2):
                        for t in range(ST):
                            col = q * WA + h * DA + d * P
                            last = nc.tensor.transpose(tp[:, q, d * S + t * P:d * S + (t + 1) * P],
                                                       proj[:, t, col:col + P], ident[:, :])
                last.then_inc(ml_t, 1)
                if h:
                    pe.wait_ge(ml_p, 4 * h)
                for q in range(2):
                    mm(tp[:, 2, q * S:(q + 1) * S], sel[:, h, :], ga_t[:, 2 + q, :], start=True, stop=True)
                pe.wait_ge(ml_tq, 2 * h + 2)
                for t in range(ST):
                    for d in range(2):
                        last = mm(tp[:, 3, t * S:(t + 1) * S], ml_qk[:, 1, d, t * P:(t + 1) * P],
                                  ml_qk[:, 0, d, :], start=d == 0, stop=d == 1)
                last.then_inc(ml_s, 1)
                pe.wait_ge(ml_p, 4 * h + 4)
                if h:
                    pe.wait_ge(ml_h, h)
                    pe.wait_ge(ml_sq, 2 * h)
                terms = {(0, 0): ((0, 0),), (1, 0): ((P, 0), (S, 1)),
                         (0, 1): ((S + P, 0), (2 * S, 1)), (1, 1): ((2 * S + P, 1),)}
                for (t, q), parts in terms.items():
                    for rhs_n in range(2):
                        for k, (a, ks) in enumerate(parts):
                            lhs = ml_e[:, a:a + P]
                            se = dict(start=k == 0, stop=k == len(parts) - 1)
                            if rhs_n == 0:
                                mm(gp[0][:, t, q * DA:(q + 1) * DA], lhs,
                                   proj[:, ks, 2 * WA + h * DA:2 * WA + (h + 1) * DA], **se)
                            else:
                                last = mm(gp[1][:, 0, 2 * t + q:2 * t + q + 1], lhs, ones[:, 0:1], **se)
                last.then_inc(ml_num, 1)
            pe.wait_ge(ml_out, 1)
            transpose_in(HB_ML, WA // P // 2, proj, 0)
            for step in range(HB + 3):
                n = step
                if n < HB:
                    if n < 2:
                        pe.wait_ge(h_full, HB_ML + 4)
                    if n >= 2:
                        pe.wait_ge(na_tq, 2 * (n - 1))
                    for q in range(2):
                        for t in range(ST):
                            col = QB0 + q * WA + n * DB
                            last = nc.tensor.transpose(tp[:, n % 2, q * S + t * P:q * S + (t + 1) * P],
                                                       proj[:, t, col:col + DB], ident[:, :])
                    last.then_inc(na_t, 1)
                n = step - 1
                if 0 <= n < HB:
                    pe.wait_ge(na_tq, 2 * (n + 1))
                    pe.wait_ge(na_bias_ready, 2 * (n + 1))
                    if n >= 2:
                        pe.wait_ge(na_exp, 2 * (n - 1))
                    for t in range(ST):
                        o = tp[:, 2 + n % 2, t * S:(t + 1) * S]
                        mm(o, flip[:, :], na_bias[:, n % 2, 2 - 2 * t:2 - 2 * t + GR, :], start=True, stop=False)
                        last = mm(o, na_qk[:, n % 2, 0, t * P:(t + 1) * P], na_qk[:, n % 2, 1, :],
                                  start=False, stop=True)
                    last.then_inc(na_s, 1)
                n = step - 2
                if 0 <= n < HB:
                    pe.wait_ge(na_p, n + 1)
                    if n >= 2:
                        pe.wait_ge(na_ptc, n - 1)
                    for k in range(ST):
                        for t in range(ST):
                            last = nc.tensor.transpose(gp[0][:, n % 2, k * S + t * P:k * S + (t + 1) * P],
                                                       na_sc[:, n % 2, t, k * P:(k + 1) * P], ident[:, :])
                    last.then_inc(na_ptm, 1)
                n = step - 3
                if n >= 0:
                    pe.wait_ge(na_ptc, n + 1)
                    if n >= 2:
                        pe.wait_ge(na_lo, n - 1)
                    for k in range(ST):
                        col = QB0 + 2 * WA + n * DB
                        last = mm(gp[1][:, n % 2, 0:S], proj[:, k, col:col + DB], na_pt[:, n % 2, k, :],
                                  start=k == 0, stop=k == 1)
                    last.then_inc(na_o, 1)

            def mixed_ready(j):
                if j < 4:
                    pe.wait_ge(h_ready, HB_ML + j + 1)
                    pe.wait_ge(na_lo, HB)
                else:
                    pe.wait_ge(na_lo, 2 * (j - 3))
            stream(g_out, h_hi, h_lo, 0, mixed_ready)
            pe.wait_ge(ada_summed, ADA_N)
            for t in range(ST):
                pe.wait_ge(drained[t], g_up.chunk0)
            sum_broadcast(gate2).then_inc(mod_sum, 1)
            transpose_x(1, HB_NORM1)
            pe.wait_ge(mod_ready, 5)

            def pair_up(i):
                for t in range(ST):
                    pe.wait_ge(drained[t], g_up.chunk(i, 1) + 1)
                for b in range(2):
                    for f in range(4):
                        for t in range(ST):
                            o = (f % 2) * S + t * P
                            last = nc.tensor.transpose(tp[:, 2 * b + f // 2, o:o + P],
                                                       ff[:, b, t, f * P:(f + 1) * P], ident[:, :])
                last.then_inc(ff_t, 1)
            stream(g_up, h_hi, h_lo, 0, h_pairs(HB_NORM1), pair_up)
            stream(g_down, a_hi, a_lo, 0, lambda j: pe.wait_ge(ff_lo, j // 2 + 1))
            transpose_x(2, HB_NORM2)
            stream(g_in2, h_hi, h_lo, 0, h_pairs(HB_NORM2))
            for t in range(ST):
                pe.wait_ge(drained[t], g_bra.chunk0)
            for n in range(6):
                if n == 4:
                    pe.wait_ge(kdup_ready, 1)
                if n >= 4:
                    pe.wait_ge(q2_c, n - 3)
                for a in range(2):
                    for t in range(ST):
                        src = (proj2[:, t, QA2 + (2 * n + a) * P:QA2 + (2 * n + a + 1) * P] if n < 4 else
                               kdup[:, t, 2 * (n - 4) + a].rearrange("p u d -> p (u d)"))
                        last = nc.tensor.transpose(tp[:, n % 4, a * S + t * P:a * S + (t + 1) * P], src,
                                                   ident[:, :])
                last.then_inc(q2_t, 1)

            def outputs(n0, h, v, w, q):
                half = slice((h % 2) * DH, (h % 2 + 1) * DH)
                if h % 2 == 0 and n0 + h >= 4:
                    pe.wait_ge(o2_lo, (n0 + h) // 2 - 1)
                bank = (h // 2) % 2
                mm(gp[1][half, bank, 0:S], proj2[:, 0, v:v + DH], w[:, 0:S], start=True, stop=False)
                mm(gp[1][half, bank, P:S], proj2[:, 1, v:v + DH], w[:, S:SW_N], start=False, stop=True
                   ).then_inc(o2_mm, 1)
            for step in range(HS + 3):
                h = step
                if h < HS:
                    if h == 0:
                        pe.wait_ge(q2_c, 6)
                    if h >= 2:
                        pe.wait_ge(sw_max, h - 1)
                    half = slice((h % 2) * DH, (h % 2 + 1) * DH)
                    g = h // (HS // HK)
                    mm(tp[:, h % 2, 0:P], Q2[half, h // 2, 0:P], K2[half, g, 0:P], start=True, stop=True)
                    mm(tp[:, h % 2, P:SW_N], Q2[half, h // 2, P:S], K2[half, g, :], start=True, stop=True
                       ).then_inc(sw_s, 1)
                h = step - 2
                if 0 <= h < HS:
                    pe.wait_ge(sw_p, h + 1)
                    if h >= 2:
                        pe.wait_ge(sw_ptc, h - 1)
                    for k in range(3):
                        last = nc.tensor.transpose(gp[0][:, h % 2, k * P:(k + 1) * P],
                                                   SC[:, h % 2, k * P:(k + 1) * P], ident[:, :])
                    last.then_inc(sw_ptm, 1)
                h = step - 3
                if h >= 0:
                    pe.wait_ge(sw_ptc, h + 1)
                    outputs(0, h, VA2 + (h // (HS // HK)) * DH, PT[:, h % 2], 0)
            for n in range(8):
                if n >= 4:
                    pe.wait_ge(q2_c, 6 + n - 3)
                col = (QS2 if n < 4 else KS2) + 2 * (n % 4) * P
                for a in range(2):
                    for t in range(ST):
                        last = nc.tensor.transpose(tp[:, n % 4, a * S + t * P:a * S + (t + 1) * P],
                                                   proj2[:, t, col + a * P:col + (a + 1) * P], ident[:, :])
                last.then_inc(q2_t, 1)
            pe.wait_ge(sk_mask, 1)
            for step in range(HS + 3):
                h = step
                if h < HS:
                    if h == 0:
                        pe.wait_ge(q2_c, 14)
                    if h >= 2:
                        pe.wait_ge(sk_lb, h - 1)
                    half = slice((h % 2) * DH, (h % 2 + 1) * DH)
                    mm(tp[:, h % 2, 0:S], K2[half, h // 2, 0:P], Q2[half, h // 2, :], start=True, stop=True)
                    mm(tp[:, h % 2, S:SW_N], K2[half, h // 2, P:S], Q2[half, h // 2, P:S], start=True, stop=True
                       ).then_inc(sk_z, 1)
                h = step - 1
                if 0 <= h < HS:
                    pe.wait_ge(sk_sp, h + 1)
                    if h >= 2:
                        pe.wait_ge(sk_arg, h - 1)
                    o = tp[:, 2 + h % 2]
                    mm(o[:, 0:S], TRI, SP_[:, h % 2, 0:S], start=True, stop=False)
                    mm(o[:, P:S], ones[:, :], SP_[:, h % 2, S:SW_N], start=False, stop=True)
                    mm(o[:, S:SW_N], TRI, SP_[:, h % 2, S:SW_N], start=True, stop=True).then_inc(sk_suf, 1)
                h = step - 3
                if h >= 0:
                    pe.wait_ge(sk_a, h + 1)
                    outputs(HS, h, VS2 + h * DH, AA[:, h % 2], 0)
            stream(g_bra, h_hi, h_lo, 0, lambda j: pe.wait_ge(o2_lo, HS))
            stream(g_brb, h_hi, h_lo, WA // P, lambda j: None)
            pe.wait_ge(merged, ST * g_brb.chunks)
            transpose_in(HB_MERGE, NP8, proj2, GA2)
            stream(g_out2, h_hi, h_lo, 0, h_pairs(HB_MERGE))
            transpose_x(3, HB_NORM3)

            def pair_up2(i):
                for t in range(ST):
                    pe.wait_ge(drained[t], g_up2.chunk(i, 1) + 1)
                for f in range(4):
                    for t in range(ST):
                        o = (f % 2) * S + t * P
                        last = nc.tensor.transpose(tp[:, f // 2, o:o + P], ff[:, 1, t, f * P:(f + 1) * P],
                                                   ident[:, :])
                last.then_inc(ff_t, 1)
            stream(g_up2, h_hi, h_lo, 0, h_pairs(HB_NORM3), pair_up2)
            stream(g_down2, a_hi, a_lo, 0, lambda j: pe.wait_ge(ff_lo, g_up.chunks // 2 + j // 2 + 1))

        @block.vector
        def _(dve):
            link = chain(dve_chain, dve)
            V = nc.vector

            def split(g, i, e, j):
                s = g.slot(e, j)
                dve.wait_ge(hi_ready, g.block(i, e, j) + 1)
                V.tensor_tensor(w_lo[:, s], raw[:, s], w_hi[:, s].bitcast(F32), ALU.subtract
                                ).then_inc(lo_ready, 1)

            def prime(g):
                for j in range(RING):
                    split(g, 0, 0, j)

            def stream(g, drain, side=None, each=None, nxt=None):
                def step(i, e, first):
                    for j in range(g.nb):
                        if not (first and j < RING):
                            split(g, i, e, j)
                        if j == RING - 1 and not first:
                            drain(i if e else i - 1, 1 - e)
                        if each:
                            each(i, e, j, first)
                    if side and not first and e == 0:
                        side(i - 1)
                walk(dve, g.chunks, step)
                if nxt:
                    prime(nxt)
                drain((g.chunks - 1) // 2, (g.chunks - 1) % 2)
                if side:
                    side(g.chunks // 2 - 1)

            def chunk_done(g, i, e):
                dve.wait_ge(block_used, g.done(i, e))

            def nothing(i, e):
                pass

            def drain_proj(g, dst, col0):
                def drain(i, e):
                    chunk_done(g, i, e)
                    V.tensor_copy(dst[:, 1, bass.ds(col0 + i * 2 * CW + e * CW, CW)], gp[g.bank(e)][:, 1, :]
                                  ).then_inc(drained[1], 1)
                return drain

            def norm_stats(n):
                dve.wait_ge(sq_ready, ST * (n + 1))
                V.tensor_scalar(stat[:, 2:4], stat[:, 0:2], 1.0 / D, EPS, ALU.mult, ALU.add
                                ).then_inc(ms_ready, 1)
                dve.wait_ge(rms_ready, n + 1)
                link(V.reciprocal(stat[:, 6:8], stat[:, 4:6]))

            def make_diag():
                for t in range(ST):
                    V.tensor_scalar(diag[:, t, :], ident[:, :], stat[:, 6 + t:7 + t], None, ALU.mult
                                    ).then_inc(diag_ready, 1)

            def handover(base, n, kt0, buf, scale=None, shift=None):
                def low(kp):
                    dve.wait_ge(h_high, base + kp + 1)
                    sl = slice(kt0 + 2 * kp, kt0 + 2 * kp + 2)
                    V.tensor_tensor(h_lo[:, sl, :], buf[:, kp % 2], h_hi[:, sl, :].bitcast(F32), ALU.subtract
                                    ).then_inc(h_ready, 1)
                for kp in range(n):
                    dve.wait_ge(xt_ready, base + kp + 1)
                    if kp >= 2:
                        dve.wait_ge(h_ready, base + kp - 1)
                    src = tp[:, kp % 4, :].rearrange("p (a s) -> p a s", a=2)
                    if scale is None:
                        last = V.tensor_copy(buf[:, kp % 2], src)
                    else:
                        for a in range(2):
                            kt = 2 * kp + a
                            if shift is None:
                                last = V.tensor_scalar(buf[:, kp % 2, a], src[:, a], scale[:, kt:kt + 1], None,
                                                       ALU.mult)
                            else:
                                last = V.tensor_scalar(buf[:, kp % 2, a], src[:, a], scale[:, kt:kt + 1],
                                                       shift[:, kt:kt + 1], ALU.mult, ALU.add)
                    last.then_inc(h_full, 1)
                    if kp:
                        low(kp - 1)
                low(n - 1)

            def mod_columns(which, g):
                V.tensor_copy(mod[:, 2 * which, :], tp[:, 3, 0:DT])
                link(V.scalar_tensor_tensor(mod[:, 2 * which + 1, :], tp[:, 3, DT:2 * DT], 1.0,
                                            vcol[:, 0, VC[g]:VC[g] + DT], ALU.add, ALU.mult))

            def add_ada(a, ring, k, dst):
                V.scalar_tensor_tensor(dst, ring, c_act[:, bass.ds(k, 1)], dst, ALU.mult, ALU.add
                                       ).then_inc(ada_summed, 1)

            dve.wait_ge(silu_ready, 1)
            dve.wait_ge(const_ready, 1)
            norm_stats(0)
            make_diag()
            dve.wait_ge(acc_bias[0], 16)

            def ada_part1(i, k2, peeled):
                for p in range(4):
                    dve.wait_ge(ada1_landed[4 * k2 + p], i * 16 + 16)
                    if not (peeled and k2 == 0):
                        dve.wait_ge(ada_summed, i * 8 + (4 * k2 + p - 3))
                    add_ada(None, ada_first[:, 4 * k2 + p, :], i * 2 + k2, acc[:, p, :])
            for k2 in range(2):
                ada_part1(0, k2, True)
            with dve.Fori(1, DT // 2) as i:
                for k2 in range(2):
                    ada_part1(i, k2, False)
            dve.wait_ge(wg_high, 1)
            V.tensor_tensor(wg_lo[:, :, :], wg, wg_hi[:, :, :].bitcast(F32), ALU.subtract).then_inc(wg_split, 1)
            dve.wait_ge(mod_sum, 1)
            mod_columns(0, "g1")
            V.memset(stat[:, 8:9], 0.0).then_inc(mod_ready, 1)
            prime(g_in_a)
            handover(HB_NORM0, NP8, 0, hf, mod[:, 1, :], mod[:, 0, :])

            def ada2(k0, piece_k_first):
                def each(i, e, j, first):
                    if j >= 6:
                        return
                    k = i * 2 + (k0 + e)
                    a = i * 12 + (PART2 + 6 * (k0 + e) + j)
                    dve.wait_ge(ada_landed[j % 2], i * 96 + 16 * (3 * (k0 + e) + j // 2 + 1))
                    if first and piece_k_first:
                        if j == 0:
                            dve.wait_ge(acc_bias[1], 16)
                        if j == 2:
                            dve.wait_ge(acc_bias[3], 16)
                    else:
                        dve.wait_ge(ada_summed, a - 5)
                    add_ada(a, ada_ring[:, j % 2, :], k,
                            ga1[:, j * ADA_W:(j + 1) * ADA_W] if j < 2 else acc[:, j - 2, :])
                return each
            stream(g_in_a, drain_proj(g_in_a, proj, 0), each=ada2(0, True), nxt=g_in_b)
            dve.wait_ge(gates_mm, 1)
            V.tensor_copy(gsb[:, :, :], tp[:, 0, 0:ST * 4 * HA].rearrange("p (t n) -> p t n", t=ST)
                          ).then_inc(gates_out, 1)
            each_b = ada2(g_in_a.chunks, False)
            stream(g_in_b, drain_proj(g_in_b, proj, QB0), each=each_b, nxt=g_out)
            for k in range(g_in_a.chunks + g_in_b.chunks, DT):
                for j in range(6):
                    each_b((k - g_in_a.chunks) // 2, k % 2, j, False)
            dve.wait_ge(mod_sum, 2)
            mod_columns(1, "g2")
            for b in range(2):
                V.tensor_copy(ga1[:, b * 2 * CW:(b + 1) * 2 * CW],
                              gp[b][:, :, :].rearrange("p t n -> p (t n)")).then_inc(mod_ready, 1)
            dve.wait_ge(gt_mm, 1)
            for y in range(4):
                link(V.tensor_scalar(GTR[:, y, :], tp[0:HA, 1 + y // 2, (y % 2) * S:(y % 2 + 1) * S],
                                     bg[:, y:y + 1], None, ALU.add))
            V.memset(stat[:, 9:10], 0.0).then_inc(gt_ready, 1)
            dve.wait_ge(gl_ln, 1)
            fg, ig = GTR[:, 1:4:2, :], GTR[:, 0:4:2, :]
            link(V.scalar_tensor_tensor(fg, fg, 0.0, ga_t[:, 0:2, :], ALU.min, ALU.subtract))
            bf, bb = ga_t[:, 0, :], ga_t[:, 1, :]
            link(V.tensor_tensor_scan(bf, GTR[:, 1, :], GTR[:, 1, :], 0.0, ALU.add, ALU.bypass))
            link(V.tensor_tensor_scan(bb[:, ::-1], GTR[:, 3, ::-1], GTR[:, 3, ::-1], 0.0, ALU.add, ALU.bypass))
            link(V.tensor_tensor(ig, ig, ga_t[:, 0:2, :], ALU.subtract))
            mf, mb = ga_t[:, 2, :], ga_t[:, 3, :]
            link(V.tensor_tensor_scan(mf, GTR[:, 0, :], GTR[:, 0, :], -3e38, ALU.max, ALU.bypass))
            link(V.tensor_tensor_scan(mb[:, ::-1], GTR[:, 2, ::-1], GTR[:, 2, ::-1], -3e38, ALU.max, ALU.bypass))
            V.tensor_tensor(fg, ga_t[:, 0:2, :], ga_t[:, 2:4, :], ALU.add).then_inc(gm_ready, 1)
            dve.wait_ge(gc_mm, 1)
            V.tensor_copy(gcol[:, :, :, :].rearrange("p t y h -> p (t y h)"), tp[:, 0, 0:ST * 4 * HA]
                          ).then_inc(gc_ready, 1)
            for h in range(HA):
                dve.wait_ge(ml_s, h + 1)
                if h:
                    dve.wait_ge(ml_num, h)
                for a, n, q, t0, m in ((0, S, 0, 0, mask_f[:, :]), (S, P, 0, P, mask_f[:, 0:P]),
                                       (S + P, P, 1, 0, mask_b[:, P:S]), (2 * S, S, 1, 0, mask_b[:, :])):
                    last = V.tensor_tensor(ml_e[:, a:a + n], m, tp[:, 2, q * S + t0:q * S + t0 + n],
                                           ALU.subtract)
                last.then_inc(ml_arg, 1)
                for k, (a, n, t, t0) in enumerate(((0, S, 0, 0), (S, P, 1, P), (S + P, P, 0, 0), (2 * S, S, 1, 0))):
                    dve.wait_ge(ml_exp, 4 * h + k + 1)
                    V.tensor_tensor(ml_e[:, a:a + n], ml_e[:, a:a + n], tp[:, 3, t * S + t0:t * S + t0 + n],
                                    ALU.mult).then_inc(ml_p, 1)
                dve.wait_ge(ml_den, h + 1)
                r = hcol[:, 0, 0:4].rearrange("p (t q) -> p t q", t=ST)
                link(V.tensor_tensor(r, r, gcol[:, :, 1:4:2, h], ALU.max))
                link(V.reciprocal(r, r))
                for t in range(ST):
                    ht = proj[:, t, h * DA:(h + 1) * DA]
                    link(V.tensor_scalar(ht, gp[0][:, t, 0:DA], hcol[:, 0, 2 * t:2 * t + 1], None, ALU.mult))
                    last = V.scalar_tensor_tensor(ht, gp[0][:, t, DA:2 * DA], hcol[:, 0, 2 * t + 1:2 * t + 2], ht,
                                                  ALU.mult, ALU.add)
                last.then_inc(ml_h, 1)
            dve.wait_ge(ml_sq, 2 * HA)
            V.tensor_scalar(hcol[:, 1, :], hcol[:, 1, :], 1.0 / DA, EPS, ALU.mult, ALU.add).then_inc(ml_ms, 1)
            dve.wait_ge(ml_rms, 1)
            link(V.reciprocal(hcol[:, 2, :], hcol[:, 2, :]))
            for t in range(ST):
                dve.wait_ge(ml_rms, 2 + t)
                for h in range(HA):
                    ht = proj[:, t, h * DA:(h + 1) * DA]
                    last = V.scalar_tensor_tensor(ht, ht, hcol[:, 2, 2 * h + t:2 * h + t + 1],
                                                  proj[:, t, 3 * WA + h * DA:3 * WA + (h + 1) * DA],
                                                  ALU.mult, ALU.mult)
            last.then_inc(ml_out, 1)
            handover(HB_ML, WA // P // 2, 0, hf, vcol[:, 0, VC["ghead"]:VC["ghead"] + 8])
            for step in range(HB + 3):
                n = step - 1
                if 0 <= n < HB:
                    dve.wait_ge(na_s, n + 1)
                    V.tensor_reduce(nst[:, n % 2, 0, :], tp[:, 2 + n % 2, :].rearrange("p (t s) -> p t s", t=ST),
                                    AX_X, ALU.max, negate=True).then_inc(na_max, 1)
                    dve.wait_ge(na_exp, 2 * (n + 1))
                    link(V.reciprocal(nst[:, n % 2, 2, :], nst[:, n % 2, 1, :]))
                    for t in range(ST):
                        last = V.tensor_scalar(na_sc[:, n % 2, t], na_sc[:, n % 2, t],
                                               nst[:, n % 2, 2, t:t + 1], None, ALU.mult)
                    last.then_inc(na_p, 1)
                n = step - 3
                if n >= 0:
                    dve.wait_ge(na_hi, n + 1)
                    V.tensor_tensor(h_lo[:, HB + n, :], gp[1][:, n % 2, 0:S], h_hi[:, HB + n, :].bitcast(F32),
                                    ALU.subtract).then_inc(na_lo, 1)

            def drain_gated(g, gate, buf, done0):
                def drain(i, e):
                    chunk_done(g, i, e)
                    c_ = 2 * i + e
                    if c_ >= 2:
                        dve.wait_ge(x_final, done0 + 2 * (c_ - 1))
                    for t in range(ST):
                        V.tensor_tensor(buf[:, e, t, :], gp[g.bank(e)][:, t, :], gate[:, bass.ds(g.col(i, e), CW)],
                                        ALU.mult).then_inc(drained[t], 1)
                return drain

            def ada3(i, e, j, first):
                a = i * 16 + (PART3 + 8 * e + j)
                dve.wait_ge(ada_landed[j % 2], i * 128 + 16 * (3 * DT + 4 * e + j // 2 + 1))
                if first and j < 2:
                    dve.wait_ge(acc_bias[2], 16)
                else:
                    dve.wait_ge(ada_summed, a - 1)
                add_ada(a, ada_ring[:, j % 2, :], i * 8 + (4 * e + j // 2),
                        gate2[:, (j % 2) * ADA_W:(j % 2 + 1) * ADA_W])
            stream(g_out, drain_gated(g_out, ga1, xt1, 0), each=ada3, nxt=g_up)
            dve.wait_ge(mod_sum, 3)
            for b in range(2):
                V.tensor_copy(gate2[:, b * 2 * CW:(b + 1) * 2 * CW],
                              gp[b][:, :, :].rearrange("p t n -> p (t n)")).then_inc(mod_ready, 1)
            norm_stats(1)
            make_diag()
            handover(HB_NORM1, NP8, 0, hf_ff, mod[:, 3, :], mod[:, 2, :])

            def drain_g(i, e):
                if e == 1:
                    chunk_done(g_up, i, e)
                    for t in range(ST):
                        dve.wait_ge(drained[t], g_up.chunk(i, e))
                        V.tensor_copy(ff[:, 1, t, :], gp[g_up.bank(e)][:, t, :]).then_inc(drained[t], 1)

            def glu_side(i):
                gt = tp[:, 2:4, :].rearrange("p b (a s) -> p (b a) s", a=2)
                ut = tp[:, 0:2, :].rearrange("p b (a s) -> p (b a) s", a=2)

                def col(tile, r, f):
                    return vcol[:, tile, bass.ds(i * 4 + (r + f), 1)]
                dve.wait_ge(ff_t, i + 1)
                for f in range(4):
                    V.tensor_scalar(g4[:, f, :], gt[:, f, :], col(1, FT, f), col(2, FT, f), ALU.mult, ALU.add
                                    ).then_inc(ff_conv, 1)
                for f in range(4):
                    dve.wait_ge(ff_conv, i * 12 + (f + 1))
                    V.scalar_tensor_tensor(g4[:, f, 1:S], gt[:, f, 0:S - 1], col(1, 0, f), g4[:, f, 1:S],
                                           ALU.mult, ALU.add).then_inc(ff_conv, 1)
                for f in range(4):
                    dve.wait_ge(ff_conv, i * 12 + (f + 5))
                    V.scalar_tensor_tensor(g4[:, f, 0:S - 1], gt[:, f, 1:S], col(2, 0, f), g4[:, f, 0:S - 1],
                                           ALU.mult, ALU.add).then_inc(ff_conv, 1)
                dve.wait_ge(ff_act, i + 1)
                V.tensor_tensor(g4, g4, ut, ALU.mult).then_inc(ff_mul, 1)
                dve.wait_ge(ff_hi, i + 1)
                V.tensor_tensor(a_lo[:, bass.ds(i * 4, 4), :], g4, a_hi[:, bass.ds(i * 4, 4), :].bitcast(F32),
                                ALU.subtract).then_inc(ff_lo, 1)
                dve.wait_ge(ff_lo, i + 1)
            stream(g_up, drain_g, side=glu_side, nxt=g_down)
            stream(g_down, drain_gated(g_down, gate2, ff, ST * g_out.chunks), nxt=g_in2)
            norm_stats(2)
            dve.wait_ge(gain_landed, 16)
            for t in range(ST):
                V.scalar_tensor_tensor(xres[:, t, :], xres[:, t, :], stat[:, 6 + t:7 + t], gate2[:, :],
                                       ALU.mult, ALU.mult).then_inc(gain_used, 1)
            norm_stats(3)
            make_diag()
            handover(HB_NORM2, NP8, 0, hf_tmp, vcol[:, 0, VC["mixg"]:VC["mixg"] + DT])
            stream(g_in2, drain_proj(g_in2, proj2, 0), nxt=g_bra)
            for t in range(ST):
                dve.wait_ge(drained[t], g_in2.chunk0 + g_in2.chunks)
            ka = proj2[:, :, KA2:KA2 + HK * DH].rearrange("p t (g d) -> p t g d", g=HK)
            for u in range(2):
                for t in range(ST):
                    last = V.tensor_copy(kdup[:, t, :, u, :], ka[:, t])
            last.then_inc(kdup_ready, 1)
            for step in range(HS + 3):
                h = step - 1
                if 0 <= h < HS:
                    sw = SW[:, h % 2]
                    dve.wait_ge(sw_s, h + 1)
                    dve.wait_ge(sw_bias, h + 1)
                    if h >= 2:
                        dve.wait_ge(sw_ptm, h - 1)
                    link(V.scalar_tensor_tensor(SC[:, h % 2], tp[:, h % 2, 0:SW_N], DH ** -0.5, TB[:, h % 2],
                                                ALU.mult, ALU.add))
                    V.tensor_reduce(sw[:, 0, 0:1], SC[:, h % 2, 0:P], AX_X, ALU.max)
                    link(V.tensor_reduce(sw[:, 0, 1:2], SC[:, h % 2, P:SW_N], AX_X, ALU.max))
                    V.tensor_scalar(sw[:, 1, 0:2], sw[:, 0, 0:2], sink[:, h:h + 1], -1.0, ALU.max, ALU.mult
                                    ).then_inc(sw_max, 1)
                    dve.wait_ge(sw_exp, h + 1)
                    link(V.tensor_tensor(sw[:, 2, 0:2], sw[:, 2, 0:2], sw[:, 3, 0:2], ALU.add))
                    link(V.reciprocal(sw[:, 2, 0:2], sw[:, 2, 0:2]))
                    for t, (a, n) in enumerate(((0, P), (P, S))):
                        last = V.tensor_scalar(SC[:, h % 2, a:a + n], SC[:, h % 2, a:a + n], sw[:, 2, t:t + 1],
                                               None, ALU.mult)
                    last.then_inc(sw_p, 1)
                h = step - 3
                if h >= 0 and h % 2:
                    dve.wait_ge(o2_hi, h // 2 + 1)
                    V.tensor_tensor(h_lo[:, h // 2, :], gp[1][:, (h // 2) % 2, 0:S],
                                    h_hi[:, h // 2, :].bitcast(F32), ALU.subtract).then_inc(o2_lo, 1)
            dve.wait_ge(sk_mask, 1)
            for step in range(HS + 3):
                h = step - 1
                if 0 <= h < HS:
                    z = tp[:, h % 2, 0:SW_N]
                    spv = SP_[:, h % 2].rearrange("p (a b) -> p a b", a=3)[:, 0:3:2, :]
                    dve.wait_ge(sk_l, h + 1)
                    if h >= 2:
                        dve.wait_ge(sk_suf, h - 1)
                    link(V.scalar_tensor_tensor(SP_[:, h % 2], z, 0.0, LL[:, h % 2], ALU.max, ALU.add))
                    V.tensor_tensor(spv, spv, M2, ALU.mult).then_inc(sk_sp, 1)
                    if h >= 2:
                        dve.wait_ge(sk_exp, h - 1)
                    V.scalar_tensor_tensor(LB[:, h % 2], z, 0.0, LL[:, h % 2], ALU.min, ALU.subtract
                                           ).then_inc(sk_lb, 1)
                h = step - 2
                if 0 <= h < HS:
                    dve.wait_ge(sk_suf, h + 1)
                    dve.wait_ge(sk_lb, h + 1)
                    V.tensor_tensor(LB[:, h % 2], LB[:, h % 2], tp[:, 2 + h % 2, 0:SW_N], ALU.subtract
                                    ).then_inc(sk_arg, 1)
                h = step - 3
                if h >= 0 and h % 2:
                    dve.wait_ge(o2_hi, HS // 2 + h // 2 + 1)
                    V.tensor_tensor(h_lo[:, 8 + h // 2, :], gp[1][:, (h // 2) % 2, 0:S],
                                    h_hi[:, 8 + h // 2, :].bitcast(F32), ALU.subtract).then_inc(o2_lo, 1)

            def drain_branch(g, col0):
                def drain(i, e):
                    chunk_done(g, i, e)
                    for t in range(ST):
                        dve.wait_ge(sig_ready, t + 1)
                        gate = proj2[:, t, bass.ds(col0 + g.col(i, e), CW)]
                        V.tensor_tensor(gate, gp[g.bank(e)][:, t, :], gate, ALU.mult).then_inc(drained[t], 1)
                return drain
            stream(g_bra, drain_branch(g_bra, GA2), nxt=g_brb)
            stream(g_brb, drain_branch(g_brb, GB2), nxt=g_out2)
            handover(HB_MERGE, NP8, 0, hf_tmp)

            def drain_add(g):
                def drain(i, e):
                    chunk_done(g, i, e)
                    for t in range(ST):
                        xs = xres[:, t, bass.ds(g.col(i, e), CW)]
                        V.tensor_tensor(xs, gp[g.bank(e)][:, t, :], xs, ALU.add).then_inc(drained[t], 1)
                return drain
            stream(g_out2, drain_add(g_out2), nxt=g_up2)
            norm_stats(4)
            make_diag()
            handover(HB_NORM3, NP8, 0, hf_ff, vcol[:, 0, VC["ffng"]:VC["ffng"] + DT])

            def drain_up(i, e):
                if e == 1:
                    chunk_done(g_up2, i, e)
                    for t in range(ST):
                        dve.wait_ge(drained[t], g_up2.chunk(i, 0) + 1)
                        V.tensor_tensor(ff[:, 1, t, :], gp[g_up2.bank(e)][:, t, :], ff[:, 0, t, :], ALU.mult
                                        ).then_inc(drained[t], 1)

            def swiglu_side(i):
                dve.wait_ge(ff_hi, i + (g_up.chunks // 2 + 1))
                sl = bass.ds(i * 4, 4)
                V.tensor_tensor(a_lo[:, sl, :], tp[:, 0:2, :].rearrange("p b (a s) -> p (b a) s", a=2),
                                a_hi[:, sl, :].bitcast(F32), ALU.subtract).then_inc(ff_lo, 1)
            stream(g_up2, drain_up, side=swiglu_side, nxt=g_down2)
            stream(g_down2, drain_add(g_down2))
            norm_stats(5)
            dve.wait_ge(gain_landed, 32)
            for t in range(ST):
                for q in range(2):
                    xs = xres[:, t, q * (D // 2):(q + 1) * (D // 2)]
                    V.scalar_tensor_tensor(xs, xs, stat[:, 6 + t:7 + t], gate2[:, q * (D // 2):(q + 1) * (D // 2)],
                                           ALU.mult, ALU.mult).then_inc(out_ready, 1)


_INS = ["x", "c", "w_ada", "b_ada", "g_norm1", "w_in", "b_gates", "g_head_a", "rpb", "w_out", "g_norm2",
        "w_up", "conv_w", "conv_b", "w_down", "g_final", "norm_mix_g_2", "w_in_2", "sink_logits_2",
        "w_branch_a_2", "w_branch_b_2", "w_out_2", "norm_ffn_g_2", "w_ffn_in_2", "w_ffn_down_2",
        "norm_final_g_2"]


def kernel(**inputs):
    import numpy as _np
    import concourse.bacc as _bacc
    from concourse import mybir as _mybir
    from concourse.bass_utils import run_bass_kernel_spmd as _run

    nc = _bacc.Bacc("TRN2", target_bir_lowering=False, num_devices=1)
    arrays, args = {}, []
    for name in _INS:
        a = _np.ascontiguousarray(inputs[name])
        arrays[f"in_{name}_dram"] = a
        args.append(nc.dram_tensor(f"in_{name}_dram", a.shape, _mybir.dt.from_np(a.dtype),
                                   kind="ExternalInput").ap())
    shape = inputs["x"].shape
    args.append(nc.dram_tensor("out_0_dram", shape, _mybir.dt.float32, kind="ExternalOutput").ap())
    two_blocks(nc, *args)
    r = _run(nc, [arrays], core_ids=[0])
    return r.results[0]["out_0_dram"]
```

```python
from contextlib import ExitStack

import concourse.bass as bass
from concourse import mybir

F32 = mybir.dt.float32
F32R = mybir.dt.float32r
I32 = mybir.dt.int32
ALU = mybir.AluOpType
ACT = mybir.ActivationFunctionType
AX_X = mybir.AxisListType.X

P = 128
S = 256
ST = S // P
CW = 512
KB = 2
RING = 4
NEG = -1e30
EPS = 1e-6
ADA_W = 1024


class Gemm:

    def __init__(self, w, chunks, block0, chunk0, col0, col_e, col_i):
        self.w = w.rearrange("(t p) n -> p t n", p=P)
        self.kts = w.shape[0] // P
        self.nb = self.kts // KB
        self.chunks, self.block0, self.chunk0 = chunks, block0, chunk0
        self.col0, self.col_e, self.col_i = col0, col_e, col_i
        assert (2 * self.nb) % RING == 0 and block0 % RING == 0

    def block(self, i, e, j):
        return self.block0 + e * self.nb + j + i * (2 * self.nb)

    def slot(self, e, j):
        return (e * self.nb + j) % RING

    def turn(self, i, e, j):
        return self.block0 // RING + (e * self.nb + j) // RING + i * (2 * self.nb // RING)

    def done(self, i, e):
        return self.block0 + (e + 1) * self.nb + i * (2 * self.nb)

    def chunk(self, i, e):
        return self.chunk0 + e + i * 2

    def bank(self, e):
        return (self.chunk0 + e) % 2

    def col(self, i, e):
        return self.col0 + e * self.col_e + i * self.col_i


def walk(eng, chunks, step):
    step(0, 0, True)
    pairs = (chunks - 1) // 2
    if pairs > 1:
        with eng.Fori(0, pairs) as i:
            step(i, 1, False)
            step(i + 1, 0, False)
    elif pairs == 1:
        step(0, 1, False)
        step(1, 0, False)
    if chunks % 2 == 0:
        step((chunks - 1) // 2, 1, False)


def walk_unrolled(eng, chunks, step):
    for c in range(chunks):
        step(c // 2, c % 2, c == 0)


def two_blocks(nc, x, c, w_ada, b_ada, g_norm1, w_in, b_gates, g_head_a, rpb, w_out, g_norm2, w_up,
               conv_w, conv_b, w_down, g_final, norm_mix_g_2, w_in_2, sink_logits_2, w_branch_a_2,
               w_branch_b_2, w_out_2, norm_ffn_g_2, w_ffn_in_2, w_ffn_down_2, norm_final_g_2, out):
    D = x.shape[2]
    DT = D // P
    F = w_down.shape[1]
    FT = F // P
    HA = b_gates.shape[1] // 4
    DA = g_head_a.shape[1] // HA
    WA = HA * DA
    HB = rpb.shape[1]
    RR, RC = rpb.shape[2], rpb.shape[3]
    GW = 64
    GR = S // GW
    WC = 16
    DB = WA // HB
    HS, HK, DH = 16, 4, 64
    NJ = GR + 2
    w_ada, w_in, w_out, w_up, w_down = w_ada[0], w_in[0], w_out[0], w_up[0], w_down[0]
    w_in_2, w_out_2, w_ffn_in_2, w_ffn_down_2 = w_in_2[0], w_out_2[0], w_ffn_in_2[0], w_ffn_down_2[0]
    w_branch_a_2, w_branch_b_2 = w_branch_a_2[0], w_branch_b_2[0]
    GATES0 = 4 * WA
    QB0 = GATES0

    gemms = []

    def gemm(w, chunks, col0=0, col_e=CW, col_i=2 * CW):
        last = gemms[-1] if gemms else None
        g = Gemm(w, chunks, last.block0 + last.chunks * last.nb if last else 0,
                 last.chunk0 + last.chunks if last else 0, col0, col_e, col_i)
        gemms.append(g)
        return g

    g_in_a = gemm(w_in, GATES0 // CW)
    g_in_b = gemm(w_in, 3 * WA // CW, col0=GATES0 + 4 * HA)
    g_out = gemm(w_out, D // CW)
    g_up = gemm(w_up, 2 * F // CW, col_e=F, col_i=CW)
    g_down = gemm(w_down, D // CW)
    N_QKV2 = HS * DH + 2 * HK * DH + 3 * HS * DH
    g_in2a = gemm(w_in_2, N_QKV2 // CW)
    g_in2b = gemm(w_in_2, 2 * D // CW, col0=N_QKV2)
    g_bra = gemm(w_branch_a_2, D // CW)
    g_brb = gemm(w_branch_b_2, D // CW)
    g_out2 = gemm(w_out_2, D // CW)
    g_up2 = gemm(w_ffn_in_2, 2 * F // CW, col_e=F, col_i=CW)
    g_down2 = gemm(w_ffn_down_2, D // CW)

    ctx = ExitStack()

    def sb(name, shape, dt=F32, scope=ctx):
        return scope.enter_context(nc.sbuf_tensor(name, shape, dt))

    def sem(name):
        return ctx.enter_context(nc.semaphore(name))

    with ctx:
        raw = sb("raw", [P, RING, KB, CW])
        w_hi = sb("w_hi", [P, RING, KB, CW], F32R)
        w_lo = sb("w_lo", [P, RING, KB, CW], F32R)
        xres = sb("xres", [P, ST, D])
        h_hi = sb("h_hi", [P, DT, S], F32R)
        h_lo = sb("h_lo", [P, DT, S], F32R)
        gate2 = sb("gate2", [P, D])
        ident = sb("ident", [P, P])
        ones = sb("ones", [P, P])
        diag = sb("diag", [P, ST, P])
        vcol = sb("vcol", [P, 3, 104])
        stat = sb("stat", [P, 16])
        rstd = sb("rstd", [P, 6, ST])
        rows2 = sb("rows2", [P, ST])
        ssq = sb("ssq", [P, ST, 4])
        junk = sb("junk", [P, CW])
        mod = sb("mod", [P, 4, DT])
        c_act = sb("c_act", [P, DT])
        VC = {"c": 0, "g1": 16, "g2": 32, "mixg": 48, "ffng": 64, "ghead": 80, "gfin": 88}

        s1 = ExitStack()
        proj = sb("proj", [P, ST, 7 * WA], scope=s1)
        ga1 = sb("ga1", [P, D], scope=s1)
        acc = sb("acc", [P, 4, ADA_W], scope=s1)
        ada_ring = sb("ada_ring", [P, 2, ADA_W], scope=s1)
        sel = sb("sel", [HA, HA, P], scope=s1)
        flip = sb("flip", [P, P], scope=s1)
        mask_f = sb("mask_f", [P, S], scope=s1)
        mask_b = sb("mask_b", [P, S], scope=s1)
        gsb = sb("gsb", [P, ST, 4 * HA], scope=s1)
        gcol = sb("gcol", [P, ST, 4, HA], scope=s1)
        bg = sb("bg", [HA, 4], scope=s1)
        hcol = sb("hcol", [P, 3, 8], scope=s1)
        nst = sb("nst", [P, 2, 3, 2], scope=s1)
        ada_first = proj[:, :, :].rearrange("p a b -> p (a b)")[:, 0:8 * ADA_W].rearrange(
            "p (s n) -> p s n", s=8)
        vrows = proj[0:104, 1, 1536:1536 + 3 * P].rearrange("p (a b) -> p a b", a=3)
        wg = proj[:, 1, 2048:2048 + DT * 4 * HA].rearrange("p (t n) -> p t n", t=DT)
        wg_hi = sb("wg_hi", [P, DT, 4 * HA], F32R, scope=s1)
        wg_lo = sb("wg_lo", [P, DT, 4 * HA], F32R, scope=s1)
        accf = acc[:, :, :].rearrange("p a b -> p (a b)")
        hf = accf[:, 0:1024].rearrange("p (b a s) -> p b a s", b=2, a=2)
        ml_qk = accf[:, 1024:2048].rearrange("p (q d s) -> p q d s", q=2, d=2)
        ml_e = accf[:, 2048:2048 + 768]
        GTR = accf[0:HA, 2816:3840].rearrange("p (y s) -> p y s", y=4)
        ga_t = accf[0:HA, 0:1024].rearrange("p (y s) -> p y s", y=4)
        na_qk = accf[:, 0:1024].rearrange("p (b q s) -> p b q s", b=2, q=2)
        na_sc = accf[:, 1024:2048].rearrange("p (b t s) -> p b t s", b=2, t=2)
        na_pt = accf[:, 2048:3072].rearrange("p (b t s) -> p b t s", b=2, t=2)
        na_bias = accf[:, 3072:3072 + 2 * NJ * GW].rearrange("p (b j c) -> p b j c", b=2, j=NJ)
        xt1 = accf[:, 0:2048].rearrange("p (b t n) -> p b t n", b=2, t=2)
        s1.close()

        s2 = ExitStack()
        a_hi = sb("a_hi", [P, FT, S], F32R, scope=s2)
        a_lo = sb("a_lo", [P, FT, S], F32R, scope=s2)
        ff = sb("ff", [P, 2, ST, CW], scope=s2)
        hf_ff = ff[:, 0].rearrange("p b (a s) -> p b a s", a=2)
        g4 = ff[:, 1].rearrange("p t (a s) -> p (t a) s", a=2)
        s2.close()

        s3 = ExitStack()
        proj2 = sb("proj2", [P, ST, N_QKV2], scope=s3)
        gates2 = sb("gates2", [P, ST, 2 * D], scope=s3)
        tmp = sb("tmp", [P, 7680], scope=s3)
        sink = sb("sink", [P, HS], scope=s3)
        s3.close()
        s4 = ExitStack()
        m_hi = sb("m_hi", [P, DT, S], F32R, scope=s4)
        m_lo = sb("m_lo", [P, DT, S], F32R, scope=s4)
        s4.close()

        gp = [ctx.enter_context(nc.psum_tensor(f"gp{i}", [P, ST, CW], F32)) for i in range(2)]
        tp = ctx.enter_context(nc.psum_tensor("tp", [P, 4, CW], F32))

        raw_landed = [sem(f"raw_landed{i}") for i in range(RING)]
        hi_ready = sem("hi_ready")
        lo_ready = sem("lo_ready")
        block_used = sem("block_used")
        drained = [sem(f"drained{i}") for i in range(ST)]
        ada1_landed = [sem(f"ada1_landed{i}") for i in range(8)]
        ada_landed = [sem(f"ada_landed{i}") for i in range(2)]
        ada_summed = sem("ada_summed")
        acc_clear = sem("acc_clear")
        acc_bias = [sem(f"acc_bias{i}") for i in range(4)]
        mod_sum = sem("mod_sum")
        mod_ready = sem("mod_ready")
        x_landed = [sem(f"x_landed{i}") for i in range(ST)]
        vec_landed = sem("vec_landed")
        wg_landed = sem("wg_landed")
        const_ready = sem("const_ready")
        vec_t = sem("vec_t")
        vec_ready = sem("vec_ready")
        silu_ready = sem("silu_ready")
        wg_split = sem("wg_split")
        wg_high = sem("wg_high")
        gates_mm = sem("gates_mm")
        gates_out = sem("gates_out")
        x_final = sem("x_final")
        sq_ready = sem("sq_ready")
        ms_ready = sem("ms_ready")
        rms_ready = sem("rms_ready")
        rows_ready = sem("rows_ready")
        diag_ready = sem("diag_ready")
        xt_ready = sem("xt_ready")
        h_full = sem("h_full")
        h_high = sem("h_high")
        h_ready = sem("h_ready")
        act_chain = sem("act_chain")
        dve_chain = sem("dve_chain")
        pool_chain = sem("pool_chain")
        gt_mm = sem("gt_mm")
        gt_ready = sem("gt_ready")
        gl_abs = sem("gl_abs")
        gl_ln = sem("gl_ln")
        gm_ready = sem("gm_ready")
        em_ready = sem("em_ready")
        gc_mm = sem("gc_mm")
        gc_ready = sem("gc_ready")
        ml_t = sem("ml_t")
        ml_tq = sem("ml_tq")
        ml_s = sem("ml_s")
        ml_arg = sem("ml_arg")
        ml_exp = sem("ml_exp")
        ml_p = sem("ml_p")
        ml_num = sem("ml_num")
        ml_den = sem("ml_den")
        ml_h = sem("ml_h")
        ml_sq = sem("ml_sq")
        ml_ms = sem("ml_ms")
        ml_rms = sem("ml_rms")
        ml_out = sem("ml_out")
        na_bias_landed = [sem(f"na_bias_landed{i}") for i in range(2)]
        na_bias_ready = sem("na_bias_ready")
        na_t = sem("na_t")
        na_tq = sem("na_tq")
        na_s = sem("na_s")
        na_max = sem("na_max")
        na_exp = sem("na_exp")
        na_p = sem("na_p")
        na_ptm = sem("na_ptm")
        na_ptc = sem("na_ptc")
        na_o = sem("na_o")
        na_hi = sem("na_hi")
        na_lo = sem("na_lo")
        xt_made = sem("xt_made")
        ff_conv = sem("ff_conv")
        ff_u = sem("ff_u")
        ff_g = sem("ff_g")
        ff_t = sem("ff_t")
        ff_act = sem("ff_act")
        ff_mul = sem("ff_mul")
        ff_hi = sem("ff_hi")
        ff_lo = sem("ff_lo")
        gain_landed = sem("gain_landed")
        gain_used = sem("gain_used")
        sink_landed = sem("sink_landed")
        nd_ready = sem("nd_ready")
        q2_t = sem("q2_t")
        q2_c = sem("q2_c")
        kdup_ready = sem("kdup_ready")
        sw_s = sem("sw_s")
        sw_bias = sem("sw_bias")
        sw_max = sem("sw_max")
        sw_exp = sem("sw_exp")
        sw_p = sem("sw_p")
        sw_ptm = sem("sw_ptm")
        sw_ptc = sem("sw_ptc")
        o2_mm = sem("o2_mm")
        o2_out = sem("o2_out")
        o2_hi = sem("o2_hi")
        o2_lo = sem("o2_lo")
        sk_z = sem("sk_z")
        sk_l = sem("sk_l")
        sk_sp = sem("sk_sp")
        sk_lb = sem("sk_lb")
        sk_suf = sem("sk_suf")
        sk_arg = sem("sk_arg")
        sk_exp = sem("sk_exp")
        sk_a = sem("sk_a")
        sk_mask = sem("sk_mask")
        sig_ready = sem("sig_ready")
        merge_a = sem("merge_a")
        merge_b = sem("merge_b")
        merged = sem("merged")
        out_ready = sem("out_ready")
        out_landed = sem("out_landed")

        PART2 = 4 * DT
        PART3 = PART2 + 6 * DT
        ADA_N = PART3 + 2 * DT
        NP8 = DT // 2
        HB_NORM0, HB_ML, HB_NORM1, HB_NORM2 = 0, NP8, NP8 + 4, 2 * NP8 + 4
        HB_MERGE, HB_NORM3 = 3 * NP8 + 4, 4 * NP8 + 4
        LAG = RING - 1
        SW0 = 7
        SK0 = SW0 + HS + 5
        SK1 = SK0 + 9
        SK_END = SK1 + HS + 5
        assert SK_END + LAG <= g_in2b.chunks * g_in2b.nb

        def carve(a, n):
            return tmp[:, a:a + n]
        Q2 = carve(0, 2048).rearrange("p (t s) -> p t s", t=8)
        K2 = carve(2048, 2048).rearrange("p (t s) -> p t s", t=8)
        kdup = carve(4096, 1024).rearrange("p (t g u d) -> p t g u d", t=ST, g=HK, u=2)
        ND = carve(4096 + 1024, 384)
        NDI = carve(4096 + 1024 + 384, 384)
        TB = carve(2048 + 1024, 768).rearrange("p (b n) -> p b n", b=2)
        SC = carve(5888, 768).rearrange("p (b n) -> p b n", b=2)
        PT = carve(5888 + 768, 768).rearrange("p (b n) -> p b n", b=2)
        SW = carve(7424, 64).rearrange("p (b a n) -> p b a n", b=2, a=4)
        LL = carve(4096, 768).rearrange("p (b n) -> p b n", b=2)
        SP_ = carve(4864, 768).rearrange("p (b n) -> p b n", b=2)
        LB = carve(5888, 768).rearrange("p (b n) -> p b n", b=2)
        AA = carve(5888 + 768, 768).rearrange("p (b n) -> p b n", b=2)
        M2 = gate2[:, 0:256].rearrange("p (a b) -> p a b", a=2)
        TRI = gate2[:, 256:384]
        QA2, KA2 = 0, HS * DH
        VA2 = KA2 + HK * DH
        QS2 = VA2 + HK * DH
        KS2, VS2 = QS2 + HS * DH, QS2 + 2 * HS * DH
        OA = proj2[:, :, QA2:QA2 + HS * DH].rearrange("p a (b s) -> p a b s", b=4)
        OS = proj2[:, :, QS2:QS2 + HS * DH].rearrange("p a (b s) -> p a b s", b=4)

        def mixer_out(kp):
            return (OA, OS)[kp // 4][:, (kp % 4) // 2, 2 * (kp % 2):2 * (kp % 2) + 2, :]
        SW_N = S + P

        def chain(sem_, eng):
            count = [0]

            def link(ins):
                count[0] += 1
                ins.then_inc(sem_, 1)
                eng.wait_ge(sem_, count[0])
            return link

        block = ctx.enter_context(nc.Block())

        @block.sync
        def _(sp):
            def load(g, i, e, j):
                b = g.block(i, e, j)
                if not isinstance(b, int) or b >= RING:
                    sp.wait_ge(lo_ready, b - (RING - 1))
                s = g.slot(e, j)
                sp.dma_start(raw[:, s], g.w[:, j * KB:(j + 1) * KB, bass.ds(g.col(i, e), CW)]
                             ).then_inc(raw_landed[s], 16)

            def ada(a, slot, k, col):
                if not isinstance(a, int) or a >= PART2 + 2:
                    sp.wait_ge(ada_summed, a - 1)
                sp.dma_start(ada_ring[:, slot, :], w_ada[bass.ds(k * P, P), col:col + ADA_W]
                             ).then_inc(ada_landed[slot], 16)

            sp.dma_start(xres[:, 0, :], x[0, 0:P, :]).then_inc(x_landed[0], 16)
            sp.dma_start(xres[:, 1, :], x[0, P:S, :]).then_inc(x_landed[1], 16)
            for k in range(2):
                for p in range(4):
                    sp.dma_start(ada_first[:, 4 * k + p, :],
                                 w_ada[k * P:(k + 1) * P, p * ADA_W:(p + 1) * ADA_W]
                                 ).then_inc(ada1_landed[4 * k + p], 16)
            with sp.Fori(1, DT // 2) as i:
                for k in range(2):
                    for p in range(4):
                        sp.wait_ge(ada_summed, i * 8 + (4 * k + p - 7))
                        sp.dma_start(ada_first[:, 4 * k + p, :],
                                     w_ada[bass.ds(i * 2 * P + k * P, P), p * ADA_W:(p + 1) * ADA_W]
                                     ).then_inc(ada1_landed[4 * k + p], 16)

            def prime(g):
                for j in range(RING):
                    load(g, 0, 0, j)

            def stream(g, side=None, nxt=None):
                def step(i, e, first):
                    for j in range(g.nb):
                        if not (first and j < RING):
                            load(g, i, e, j)
                        if side:
                            side(i, e, j)
                walk(sp, g.chunks, step)
                if nxt:
                    prime(nxt)

            def ada_in(k0):
                def side(i, e, j):
                    if j < 6:
                        ada(i * 12 + (PART2 + 6 * (k0 + e) + j), j % 2, i * 2 + (k0 + e), 2 * D + j * ADA_W)
                return side

            def ada_out(i, e, j):
                ada(i * 16 + (PART3 + 8 * e + j), j % 2, i * 8 + (4 * e + j // 2), 5 * D + (j % 2) * ADA_W)

            prime(g_in_a)
            stream(g_in_a, ada_in(0), g_in_b)
            stream(g_in_b, ada_in(g_in_a.chunks), g_out)
            for k in range(g_in_a.chunks + g_in_b.chunks, DT):
                for j in range(6):
                    ada(PART2 + 6 * k + j, j % 2, k, 2 * D + j * ADA_W)
            for n in range(HB):
                if n >= 2:
                    sp.wait_ge(na_s, n - 1)
                else:
                    sp.wait_ge(ml_out, 1)
                for a in range(2):
                    src = bass.AP(tensor=rpb.tensor, offset=rpb.offset + n * RR * RC
                                  + (RR // 2 - 2 - a) * RC + RC // 2 - (GW - 1),
                                  ap=[[1, GW], [RC, NJ], [1, GW]])
                    sp.dma_start(na_bias[a * GW:(a + 1) * GW, n % 2], src
                                 ).then_inc(na_bias_landed[n % 2], 16)
            stream(g_out, ada_out, g_up)
            stream(g_up, None, g_down)
            stream(g_down, None, g_in2a)
            sp.wait_ge(drained[1], g_down.chunk0 + g_down.chunks)
            sp.dma_start(gate2[:, :], bass.AP(tensor=g_final.tensor, offset=g_final.offset,
                                              ap=[[0, P], [1, D]])).then_inc(gain_landed, 16)
            sp.wait_ge(x_final, 2 * (g_out.chunks + g_down.chunks))
            sp.dma_start(sink[:, :], bass.AP(tensor=sink_logits_2.tensor, offset=sink_logits_2.offset,
                                             ap=[[0, P], [1, HS]])).then_inc(sink_landed, 16)
            stream(g_in2a, None, g_in2b)
            stream(g_in2b, None, g_bra)
            stream(g_bra, None, g_brb)
            stream(g_brb, None, g_out2)
            sp.wait_ge(sk_a, HS)
            sp.wait_ge(sk_suf, HS)
            sp.dma_start(gate2[:, :], bass.AP(tensor=norm_final_g_2.tensor, offset=norm_final_g_2.offset,
                                              ap=[[0, P], [1, D]])).then_inc(gain_landed, 16)
            stream(g_out2, None, g_up2)
            stream(g_up2, None, g_down2)
            stream(g_down2)
            for t in range(ST):
                for q in range(2):
                    sp.wait_ge(out_ready, 2 * t + q + 1)
                    sp.dma_start(out[0, t * P:(t + 1) * P, q * (D // 2):(q + 1) * (D // 2)],
                                 xres[:, t, q * (D // 2):(q + 1) * (D // 2)]).then_inc(out_landed, 16)
            sp.wait_ge(out_landed, 16 * 2 * ST)

        @block.gpsimd
        def _(pool):
            link = chain(pool_chain, pool)

            def pred(ap, cmp, fill, base, pattern, mul):
                link(nc.gpsimd.affine_select(out=ap, in_=ap, compare_op=cmp, fill=fill, base=base,
                                             pattern=pattern, channel_multiplier=mul))
            def rows(tile, r, vec):
                n = vec.shape[0] // P
                pool.dma_start(vrows[r:r + n, tile, :], vec.rearrange("(t p) -> t p", p=P)
                               ).then_inc(vec_landed, 16)
            rows(0, VC["c"], c[0])
            rows(0, VC["g1"], g_norm1[0])
            rows(0, VC["g2"], g_norm2[0])
            rows(0, VC["mixg"], norm_mix_g_2[0])
            rows(0, VC["ffng"], norm_ffn_g_2[0])
            rows(0, VC["ghead"], g_head_a[0])
            rows(0, VC["gfin"], g_final)
            rows(1, 0, conv_w[0, 0])
            rows(1, FT, conv_w[0, 1])
            rows(2, 0, conv_w[0, 2])
            rows(2, FT, conv_b[0])
            with nc.allow_non_contiguous_dma(reason="gate columns"):
                pool.dma_start(wg, w_in.rearrange("(t p) n -> p t n", p=P)[:, :, GATES0:GATES0 + 4 * HA]
                               ).then_inc(wg_landed, 16)
                pool.dma_start(bg[:, :], b_gates[0].rearrange("(y h) -> h y", h=HA)).then_inc(wg_landed, 16)
            link(nc.gpsimd.memset(ident[:, :], 0.0))
            pred(ident[:, :], ALU.not_equal, 1.0, 0, [[-1, P]], 1)
            link(nc.gpsimd.memset(acc[:, :, :], 0.0))
            pool.dma_start(accf[0:1, :], b_ada[0:1, 0:2 * D]).then_inc(acc_bias[0], 16)
            nc.gpsimd.memset(ones[:, :], 1.0).then_inc(const_ready, 1)
            link(nc.gpsimd.memset(sel[:, :, :], 0.0))
            pred(sel[:, :, :], ALU.not_equal, 1.0, 0, [[-1, HA], [0, P]], 1)
            link(nc.gpsimd.memset(flip[:, :], 0.0))
            pred(flip[:, :], ALU.not_equal, 1.0, -(GW - 1), [[1, P]], 1)
            pred(flip[:, :], ALU.not_equal, 1.0, -(3 * GW - 1), [[1, P]], 1)
            link(nc.gpsimd.memset(mask_f[:, :], 0.0))
            pred(mask_f[:, 0:P], ALU.is_ge, NEG, 0, [[1, P]], -1)
            link(nc.gpsimd.memset(mask_b[:, :], 0.0))
            nc.gpsimd.affine_select(out=mask_b[:, P:S], in_=mask_b[:, P:S], compare_op=ALU.is_ge, fill=NEG,
                                    base=0, pattern=[[-1, P]], channel_multiplier=1
                                    ).then_inc(const_ready, 1)
            link(nc.gpsimd.memset(ga1[:, :], 0.0))
            pool.dma_start(ga1[0:1, :], b_ada[0:1, 2 * D:3 * D]).then_inc(acc_bias[1], 16)
            link(nc.gpsimd.memset(gate2[:, :], 0.0))
            pool.dma_start(gate2[0:1, :], b_ada[0:1, 5 * D:6 * D]).then_inc(acc_bias[2], 16)
            pool.wait_ge(mod_ready, 1)
            pool.wait_ge(h_ready, NP8)
            link(nc.gpsimd.memset(acc[:, :, :], 0.0))
            pool.dma_start(accf[0:1, :], b_ada[0:1, 3 * D:5 * D]).then_inc(acc_bias[3], 16)
            for n in range(HB):
                pool.wait_ge(na_bias_landed[n % 2], 32 * (n // 2 + 1))
                for a in range(2):
                    v = na_bias[a * GW:(a + 1) * GW, n % 2]
                    pred(v[:, :, 0:GW - WC], ALU.is_ge, NEG, WC // 2 - (GW - 1), [[0, NJ], [1, GW - WC]], 1)
                    right = v[:, :, WC:GW]
                    nc.gpsimd.affine_select(out=right, in_=right, compare_op=ALU.is_ge, fill=NEG,
                                            base=GW - 1 + WC // 2 - 1 - WC, pattern=[[0, NJ], [-1, GW - WC]],
                                            channel_multiplier=-1).then_inc(na_bias_ready, 1)

            def add_x(g, buf):
                def step(i, e, first):
                    for t in range(ST):
                        pool.wait_ge(drained[t], g.chunk(i, e) + 1)
                        xs = xres[:, t, bass.ds(g.col(i, e), CW)]
                        nc.gpsimd.tensor_tensor(xs, xs, buf[:, e, t, :], ALU.add).then_inc(x_final, 1)
                walk(pool, g.chunks, step)
            add_x(g_out, xt1)
            add_x(g_down, ff)
            pool.wait_ge(gain_used, ST)
            for a, base in ((0, 0), (P, -P)):
                n = P if a == 0 else S
                nd = ND[:, a:a + n]
                link(nc.gpsimd.iota(NDI[:, a:a + n].bitcast(I32), [[1, n]], base=base, channel_multiplier=-1))
                link(nc.gpsimd.tensor_copy(nd, NDI[:, a:a + n].bitcast(I32)))
                pred(nd, ALU.is_ge, NEG, -base, [[-1, n]], 1)
                if a:
                    pred(nd, ALU.is_ge, NEG, P - 1 + base, [[1, n]], -1)
            link(nc.gpsimd.memset(M2, 1.0))
            pred(M2, ALU.is_gt, 0.0, 0, [[0, 2], [1, P]], -1)
            link(nc.gpsimd.memset(TRI, 1.0))
            nc.gpsimd.affine_select(out=TRI, in_=TRI, compare_op=ALU.is_gt, fill=0.0, base=0,
                                    pattern=[[-1, P]], channel_multiplier=1).then_inc(sk_mask, 1)
            for h in range(HS):
                if h >= 2:
                    pool.wait_ge(sw_max, h - 1)
                slope = 2.0 ** (-8.0 * (h + 1) / HS)
                nc.gpsimd.tensor_scalar(TB[:, h % 2], ND, slope, None, ALU.mult).then_inc(sw_bias, 1)
            for h in range(HS):
                pool.wait_ge(sk_exp, h + 1)
                av = AA[:, h % 2].rearrange("p (a b) -> p a b", a=3)[:, 0:3:2, :]
                nc.gpsimd.tensor_tensor(av, av, M2, ALU.mult).then_inc(sk_a, 1)

            def step_b(i, e, first):
                for t in range(ST):
                    pool.wait_ge(drained[t], g_brb.chunk(i, e) + 1)
                    m = gates2[:, t, bass.ds(g_brb.col(i, e), CW)]
                    nc.gpsimd.tensor_tensor(m, m, gates2[:, t, bass.ds(D + g_brb.col(i, e), CW)],
                                            ALU.add).then_inc(merged, 1)
            walk(pool, g_brb.chunks, step_b)

        @block.scalar
        def _(act):
            link = chain(act_chain, act)

            def split(g, i, e, j):
                b, s = g.block(i, e, j), g.slot(e, j)
                act.wait_ge(raw_landed[s], 16 * (g.turn(i, e, j) + 1))
                if not isinstance(b, int) or b >= RING:
                    act.wait_ge(block_used, b - (RING - 1))
                nc.scalar.copy(w_hi[:, s], raw[:, s]).then_inc(hi_ready, 1)

            def prime(g):
                for j in range(RING):
                    split(g, 0, 0, j)

            def stream(g, drain, side=None, each=None, nxt=None, unrolled=False):
                def step(i, e, first):
                    for j in range(g.nb):
                        if not (first and j < RING):
                            split(g, i, e, j)
                        if j == RING - 1 and not first:
                            drain(i if e else i - 1, 1 - e)
                        if each:
                            each(i, e, j, first)
                    if side and not first and e == 0:
                        side(i - 1)
                (walk_unrolled if unrolled else walk)(act, g.chunks, step)
                if nxt:
                    prime(nxt)
                drain((g.chunks - 1) // 2, (g.chunks - 1) % 2)
                if side:
                    side(g.chunks // 2 - 1)

            def chunk_done(g, i, e):
                act.wait_ge(block_used, g.done(i, e))

            def drain_proj(g, dst, col0):
                def drain(i, e):
                    chunk_done(g, i, e)
                    nc.scalar.copy(dst[:, 0, bass.ds(col0 + i * 2 * CW + e * CW, CW)], gp[g.bank(e)][:, 0, :]
                                   ).then_inc(drained[0], 1)
                return drain

            def square(n, c, x_ready):
                for t in range(ST):
                    x_ready(t)
                    if c == 0 and n and t == 0:
                        act.wait_ge(ms_ready, n)
                    k = 4 * ST * n + c * ST + t
                    if k:
                        act.wait_ge(sq_ready, k)
                    nc.scalar.activation(junk[:, :], xres[:, t, c * CW:(c + 1) * CW], ACT.Square,
                                         accum_out=ssq[:, t, c:c + 1]).then_inc(sq_ready, 1)

            def root(n):
                act.wait_ge(ms_ready, n + 1)
                nc.scalar.activation(stat[:, 4:6], stat[:, 2:4], ACT.Sqrt).then_inc(rms_ready, 1)

            def added(g, c, done0):
                return lambda t: act.wait_ge(x_final, done0 + ST * c + t + 1)

            def drained_to(g, c):
                return lambda t: act.wait_ge(drained[t], g.chunk0 + c + 1)

            def high(full0, base, src):
                for kp in range(NP8):
                    act.wait_ge(h_full, full0 + kp + 1)
                    nc.scalar.copy(h_hi[:, 2 * kp:2 * kp + 2, :], src[:, kp % 2]).then_inc(h_high, 1)

            def high_direct(base, kps, dst, scale=None):
                for kp in kps:
                    act.wait_ge(xt_ready, base + kp + 1)
                    src = tp[:, kp % 4, :].rearrange("p (a s) -> p a s", a=2)
                    if scale is None:
                        last = nc.scalar.copy(dst[:, 2 * kp:2 * kp + 2, :], src)
                    else:
                        for a in range(2):
                            kt = 2 * kp + a
                            last = nc.scalar.activation(dst[:, kt, :], src[:, a], ACT.Identity,
                                                        scale=scale[:, kt:kt + 1])
                    last.then_inc(h_high, 1)

            act.wait_ge(vec_t, 1)
            nc.scalar.copy(vcol[:, 0, :], tp[:, 0, 0:104]).then_inc(vec_ready, 1)
            nc.scalar.copy(vcol[:, 1:3, 0:2 * FT], tp[:, 1:3, 0:2 * FT]).then_inc(vec_ready, 1)
            act.wait_ge(vec_ready, 1)
            nc.scalar.activation(c_act[:, :], vcol[:, 0, 0:DT], ACT.Silu).then_inc(silu_ready, 1)
            act.wait_ge(wg_landed, 32)
            nc.scalar.copy(wg_hi[:, :, :], wg).then_inc(wg_high, 1)
            for c_ in range(4):
                square(0, c_, lambda t: act.wait_ge(x_landed[t], 16))
            root(0)
            prime(g_in_a)
            high(0, HB_NORM0, hf)
            stream(g_in_a, drain_proj(g_in_a, proj, 0), nxt=g_in_b)
            stream(g_in_b, drain_proj(g_in_b, proj, QB0), nxt=g_out)
            act.wait_ge(gt_ready, 1)
            fg = GTR[:, 1:4:2, :]
            act.preload_act_table_set("natural_log_exp_and_others")
            link(nc.scalar.activation(ga_t[:, 0:2, :], fg, ACT.Abs))
            link(nc.scalar.activation(ga_t[:, 0:2, :], ga_t[:, 0:2, :], ACT.Exp, scale=-1.0))
            nc.scalar.activation(ga_t[:, 0:2, :], ga_t[:, 0:2, :], ACT.Ln, bias=1.0).then_inc(gl_ln, 1)
            act.wait_ge(gm_ready, 1)
            nc.scalar.activation(fg, fg, ACT.Exp, scale=-1.0).then_inc(em_ready, 1)
            for h in range(HA):
                act.wait_ge(ml_t, h + 1)
                nc.scalar.copy(ml_qk[:, 0], tp[:, 0, :].rearrange("p (d s) -> p d s", d=2)).then_inc(ml_tq, 1)
                nc.scalar.mul(ml_qk[:, 1], tp[:, 1, :].rearrange("p (d s) -> p d s", d=2), DA ** -0.5
                              ).then_inc(ml_tq, 1)
                act.wait_ge(ml_arg, h + 1)
                act.wait_ge(gc_ready, 1)
                for a, n, t, q in ((0, 256, 0, 0), (256, 128, 1, 0), (384, 128, 0, 2), (512, 256, 1, 2)):
                    nc.scalar.activation(ml_e[:, a:a + n], ml_e[:, a:a + n], ACT.Exp,
                                         bias=gcol[:, t, q, h:h + 1]).then_inc(ml_exp, 1)
                act.wait_ge(ml_num, h + 1)
                nc.scalar.activation(hcol[:, 0, 0:4], gp[1][:, 0, 0:4], ACT.Abs).then_inc(ml_den, 1)
                act.wait_ge(ml_h, h + 1)
                for t in range(ST):
                    nc.scalar.activation(gp[1][:, 1, 0:DA], proj[:, t, h * DA:(h + 1) * DA], ACT.Square,
                                         accum_out=hcol[:, 1, 2 * h + t:2 * h + t + 1]).then_inc(ml_sq, 1)
                    act.wait_ge(ml_sq, 2 * h + t + 1)
            act.wait_ge(ml_ms, 1)
            nc.scalar.activation(hcol[:, 2, :], hcol[:, 1, :], ACT.Sqrt).then_inc(ml_rms, 1)
            for t in range(ST):
                og = proj[:, t, 3 * WA:4 * WA]
                nc.scalar.activation(og, og, ACT.Sigmoid).then_inc(ml_rms, 1)
            high_direct(HB_ML, range(4), h_hi, vcol[:, 0, VC["ghead"]:VC["ghead"] + 8])
            act.preload_act_table_set("natural_log_exp_and_others")
            for step in range(HB + 3):
                n = step
                if n < HB:
                    act.wait_ge(na_t, n + 1)
                    if n < 2:
                        act.wait_ge(h_ready, HB_ML + 4)
                    nc.scalar.mul(na_qk[:, n % 2, 0], tp[:, n % 2, 0:S], DB ** -0.5).then_inc(na_tq, 1)
                    nc.scalar.copy(na_qk[:, n % 2, 1], tp[:, n % 2, S:2 * S]).then_inc(na_tq, 1)
                n = step - 1
                if 0 <= n < HB:
                    act.wait_ge(na_max, n + 1)
                    if n >= 2:
                        act.wait_ge(na_ptm, n - 1)
                    for t in range(ST):
                        nc.scalar.activation(na_sc[:, n % 2, t], tp[:, 2 + n % 2, t * S:(t + 1) * S], ACT.Exp,
                                             bias=nst[:, n % 2, 0, t:t + 1],
                                             accum_out=nst[:, n % 2, 1, t:t + 1]).then_inc(na_exp, 1)
                n = step - 2
                if 0 <= n < HB:
                    act.wait_ge(na_ptm, n + 1)
                    nc.scalar.copy(na_pt[:, n % 2], gp[0][:, n % 2, :].rearrange("p (t s) -> p t s", t=2)
                                   ).then_inc(na_ptc, 1)
                n = step - 3
                if n >= 0:
                    act.wait_ge(na_o, n + 1)
                    nc.scalar.copy(h_hi[:, HB + n, :], gp[1][:, n % 2, 0:S]).then_inc(na_hi, 1)

            def nothing(i, e):
                pass
            def quarter(n, g, x_ready):
                def each(i, e, j, first):
                    if j == 7 and not first:
                        square(n, 2 * i + e - 1, x_ready(2 * i + e - 1))
                return each

            def x_out(c_):
                return added(g_out, c_, 0)

            def x_down(c_):
                return added(g_down, c_, ST * g_out.chunks)

            stream(g_out, nothing, each=quarter(1, g_out, x_out), nxt=g_up)
            square(1, 3, x_out(3))
            root(1)
            high(NP8, HB_NORM1, hf_ff)

            def drain_u(i, e):
                if e == 0:
                    chunk_done(g_up, i, e)
                    for t in range(ST):
                        act.wait_ge(drained[t], g_up.chunk(i, e))
                        nc.scalar.copy(ff[:, 0, t, :], gp[g_up.bank(e)][:, t, :]).then_inc(drained[t], 1)

            def glu_side(i):
                act.wait_ge(ff_conv, i * 12 + 12)
                nc.scalar.activation(g4, g4, ACT.Gelu).then_inc(ff_act, 1)
                act.wait_ge(ff_mul, i + 1)
                nc.scalar.copy(a_hi[:, bass.ds(i * 4, 4), :], g4).then_inc(ff_hi, 1)
            act.preload_act_table(ACT.Gelu)
            stream(g_up, drain_u, side=glu_side, nxt=g_down)
            def early(n, base, x_ready, scale):
                def each(i, e, j, first):
                    c_ = 2 * i + e - 1
                    if j == 7 and not first:
                        square(n, c_, x_ready(c_))
                        high_direct(base, (2 * c_, 2 * c_ + 1), h_hi, scale)
                return each
            gain2 = vcol[:, 0, VC["gfin"]:VC["gfin"] + DT]
            gain3 = vcol[:, 0, VC["ffng"]:VC["ffng"] + DT]
            stream(g_down, nothing, each=early(2, HB_NORM2, x_down, gain2), nxt=g_in2a)
            high_direct(HB_NORM2, (6, 7), h_hi, gain2)
            square(2, 3, x_down(3))

            def scaled_drain(g, dst, rows):
                def drain(i, e):
                    chunk_done(g, i, e)
                    if g is g_in2a:
                        act.wait_ge(rows_ready, 1)
                    nc.scalar.activation(dst[:, 0, bass.ds(i * 2 * CW + e * CW, CW)], gp[g.bank(e)][:, 0, :],
                                         ACT.Identity, scale=rows[:, 0:1]).then_inc(drained[0], 1)
                return drain

            def between(i, e, j, first):
                if first:
                    if j == 4:
                        root(2)
                    if j in (5, 6):
                        for c_ in (0, 1) if j == 5 else (2, 3):
                            square(3, c_, lambda t: act.wait_ge(gain_used, ST))
                    if j == 7:
                        root(3)
            stream(g_in2a, scaled_drain(g_in2a, proj2, rows2), each=between, nxt=g_in2b)
            act.preload_act_table_set("natural_log_exp_and_others")

            def mixers(k):
                if k < 6:
                    n = k
                    act.wait_ge(q2_t, n + 1)
                    dst = Q2[:, 2 * n:2 * n + 2] if n < 4 else K2[:, 2 * (n - 4):2 * (n - 4) + 2]
                    nc.scalar.copy(dst, tp[:, n % 4, :].rearrange("p (a s) -> p a s", a=2)).then_inc(q2_c, 1)
                if SW0 <= k < SK0:
                    h = k - SW0
                    if h < HS:
                        if h == 0:
                            act.wait_ge(sink_landed, 16)
                        act.wait_ge(sw_max, h + 1)
                        for t, (a, n) in enumerate(((0, P), (P, S))):
                            nc.scalar.activation(SC[:, h % 2, a:a + n], SC[:, h % 2, a:a + n], ACT.Exp,
                                                 bias=SW[:, h % 2, 1, t:t + 1],
                                                 accum_out=SW[:, h % 2, 2, t:t + 1])
                        nc.scalar.activation(SW[:, h % 2, 3, 0:2], SW[:, h % 2, 1, 0:2], ACT.Exp,
                                             bias=sink[:, h:h + 1]).then_inc(sw_exp, 1)
                    h = k - SW0 - 2
                    if 0 <= h < HS:
                        act.wait_ge(sw_ptm, h + 1)
                        if h >= 2:
                            act.wait_ge(o2_mm, h - 1)
                        nc.scalar.copy(PT[:, h % 2], tp[:, 2, 0:SW_N]).then_inc(sw_ptc, 1)
                    h = k - SW0 - 4
                    if 0 <= h < HS and h % 2:
                        act.wait_ge(o2_mm, h + 1)
                        nc.scalar.copy(OA[:, h // 8, (h // 2) % 4], tp[:, 3, 0:S]).then_inc(o2_out, 1)
                if SK0 <= k < SK0 + 8:
                    n = k - SK0
                    act.wait_ge(q2_t, 6 + n + 1)
                    src = tp[:, n % 4, :].rearrange("p (a s) -> p a s", a=2)
                    if n < 4:
                        nc.scalar.copy(Q2[:, 2 * n:2 * n + 2], src).then_inc(q2_c, 1)
                    else:
                        nc.scalar.mul(K2[:, 2 * (n - 4):2 * (n - 4) + 2], src, DH ** -0.5).then_inc(q2_c, 1)
                if SK1 <= k < SK_END:
                    h = k - SK1
                    if h < HS:
                        act.wait_ge(sk_z, h + 1)
                        if h >= 2:
                            act.wait_ge(sk_lb, h - 1)
                        link(nc.scalar.activation(LL[:, h % 2], tp[:, h % 2, 0:SW_N], ACT.Abs))
                        link(nc.scalar.activation(LL[:, h % 2], LL[:, h % 2], ACT.Exp, scale=-1.0))
                        nc.scalar.activation(LL[:, h % 2], LL[:, h % 2], ACT.Ln, bias=1.0).then_inc(sk_l, 1)
                    h = k - SK1 - 2
                    if 0 <= h < HS:
                        act.wait_ge(sk_arg, h + 1)
                        if h >= 2:
                            act.wait_ge(o2_mm, HS + h - 1)
                        nc.scalar.activation(AA[:, h % 2], LB[:, h % 2], ACT.Exp).then_inc(sk_exp, 1)
                    h = k - SK1 - 4
                    if 0 <= h < HS and h % 2:
                        act.wait_ge(o2_mm, HS + h + 1)
                        nc.scalar.copy(OS[:, h // 8, (h // 2) % 4], tp[:, 3, 0:S]).then_inc(o2_out, 1)

            def mix_each(i, e, j, first):
                k = (2 * i + e) * g_in2b.nb + j - LAG
                if k >= 0:
                    mixers(k)
            stream(g_in2b, scaled_drain(g_in2b, gates2, rows2), each=mix_each, nxt=g_bra, unrolled=True)
            act.wait_ge(o2_out, HS)
            for kp in range(NP8):
                nc.scalar.copy(h_hi[:, 2 * kp:2 * kp + 2, :], mixer_out(kp)).then_inc(o2_hi, 1)
            for t in range(ST):
                act.wait_ge(drained[t], g_bra.chunk0)

            def gate_sigmoid(g, col0):
                def each(i, e, j, first):
                    if j == 0:
                        for t in range(ST):
                            gg = gates2[:, t, bass.ds(col0 + g.col(i, e), CW)]
                            nc.scalar.activation(gg, gg, ACT.Sigmoid).then_inc(sig_ready, 1)
                return each
            stream(g_bra, nothing, each=gate_sigmoid(g_bra, 0), nxt=g_brb)
            stream(g_brb, nothing, each=gate_sigmoid(g_brb, D), nxt=g_out2)
            high_direct(HB_MERGE, range(NP8), m_hi)
            def x_out2(c_):
                return drained_to(g_out2, c_)
            stream(g_out2, nothing, each=early(4, HB_NORM3, x_out2, gain3), nxt=g_up2)
            high_direct(HB_NORM3, (6, 7), h_hi, gain3)
            square(4, 3, x_out2(3))

            def root4(i, e, j, first):
                if first and j == 4:
                    root(4)

            def drain_gate(i, e):
                if e == 0:
                    chunk_done(g_up2, i, e)
                    for t in range(ST):
                        act.wait_ge(drained[t], g_up2.chunk(i, e))
                        act.wait_ge(rows_ready, 2)
                        nc.scalar.activation(ff[:, 0, t, :], gp[g_up2.bank(e)][:, t, :], ACT.Silu,
                                             scale=rstd[:, 4, t:t + 1]).then_inc(drained[t], 1)

            def swiglu_side(i):
                act.wait_ge(ff_t, i + (g_up.chunks // 2 + 1))
                nc.scalar.copy(a_hi[:, bass.ds(i * 4, 4), :], tp[:, 0:2, :].rearrange(
                    "p a (b s) -> p (a b) s", b=2)).then_inc(ff_hi, 1)
            stream(g_up2, drain_gate, side=swiglu_side, each=root4, nxt=g_down2)

            def x_down2(c_):
                return drained_to(g_down2, c_)
            stream(g_down2, nothing, each=quarter(5, g_down2, x_down2))
            square(5, 3, x_down2(3))
            root(5)

        @block.tensor
        def _(pe):
            mm = nc.tensor.matmul

            def stream(g, hi, lo, kt0, ready, side=None, each=None, unrolled=False):
                def step(i, e, first):
                    if not (first and g.chunk0 < 2):
                        for t in range(ST):
                            pe.wait_ge(drained[t], g.chunk(i, e) - 1)
                    for j in range(g.nb):
                        pe.wait_ge(lo_ready, g.block(i, e, j) + 1)
                        if first:
                            ready(j)
                        s = g.slot(e, j)
                        for k in range(KB):
                            kt = j * KB + k
                            for t in range(ST):
                                ps = slice(t * P, (t + 1) * P)
                                o = gp[g.bank(e)][:, t, :]
                                mm(o, hi[:, kt0 + kt, ps], w_hi[:, s, k, :], start=kt == 0, stop=False)
                                mm(o, hi[:, kt0 + kt, ps], w_lo[:, s, k, :], start=False, stop=False)
                                last = mm(o, lo[:, kt0 + kt, ps], w_hi[:, s, k, :], start=False,
                                          stop=kt == g.kts - 1)
                        last.then_inc(block_used, 1)
                        if side and e == 0 and not first and j == 3:
                            side(i - 1)
                        if each:
                            each(i, e, j, first)
                (walk_unrolled if unrolled else walk)(pe, g.chunks, step)
                if side:
                    side(g.chunks // 2 - 1)

            def h_pairs(base):
                return lambda j: pe.wait_ge(h_ready, base + j + 1)

            def transpose_x(n, base, full0):
                pe.wait_ge(diag_ready, ST * (n + 1))
                for kp in range(NP8):
                    if kp >= 4:
                        pe.wait_ge(h_full, full0 + kp - 3)
                    for a in range(2):
                        kt = 2 * kp + a
                        for t in range(ST):
                            last = mm(tp[:, kp % 4, a * S + t * P:a * S + (t + 1) * P],
                                      xres[:, t, kt * P:(kt + 1) * P], diag[:, t, :], start=True, stop=True)
                    last.then_inc(xt_ready, 1)

            def transpose_in(base, kps, src, col0, ready=None):
                for kp in kps:
                    if kp >= 4:
                        pe.wait_ge(h_ready, base + kp - 3)
                    for a in range(2):
                        kt = 2 * kp + a
                        for t in range(ST):
                            if ready:
                                ready(t)
                            last = nc.tensor.transpose(tp[:, kp % 4, a * S + t * P:a * S + (t + 1) * P],
                                                       src[:, t, col0 + kt * P:col0 + (kt + 1) * P], ident[:, :])
                    last.then_inc(xt_ready, 1)

            def sum_columns():
                for q in range(2 * DT):
                    last = mm(tp[:, 3, q:q + 1], acc[:, q // 8, (q % 8) * P:(q % 8 + 1) * P], ones[:, 0:1],
                              start=True, stop=True)
                return last

            def sum_broadcast(src):
                for q in range(4):
                    last = mm(gp[q // 2][:, q % 2, :], ones[:, :], src[:, q * CW:(q + 1) * CW],
                              start=True, stop=True)
                return last

            pe.wait_ge(const_ready, 1)
            pe.wait_ge(vec_landed, 11 * 16)
            for n, r in enumerate((104, 2 * FT, 2 * FT)):
                last = nc.tensor.transpose(tp[:, n, 0:r], vrows[0:r, n, :], ident[0:r, 0:r])
            last.then_inc(vec_t, 1)
            pe.wait_ge(ada_summed, PART2)
            pe.wait_ge(sq_ready, ST)
            sum_columns().then_inc(mod_sum, 1)
            pe.wait_ge(mod_ready, 1)
            transpose_x(0, HB_NORM0, 0)
            stream(g_in_a, h_hi, h_lo, 0, h_pairs(HB_NORM0))
            pe.wait_ge(wg_split, 1)
            for t in range(ST):
                ps = slice(t * P, (t + 1) * P)
                o = tp[:, 0, t * 4 * HA:(t + 1) * 4 * HA]
                for kt in range(DT):
                    mm(o, h_hi[:, kt, ps], wg_hi[:, kt, :], start=kt == 0, stop=False)
                    mm(o, h_hi[:, kt, ps], wg_lo[:, kt, :], start=False, stop=False)
                    last = mm(o, h_lo[:, kt, ps], wg_hi[:, kt, :], start=False, stop=kt == DT - 1)
            last.then_inc(gates_mm, 1)
            stream(g_in_b, h_hi, h_lo, 0, lambda j: None)
            pe.wait_ge(ada_summed, PART3)
            for t in range(ST):
                pe.wait_ge(drained[t], g_out.chunk0)
            sum_broadcast(ga1)
            sum_columns().then_inc(mod_sum, 1)
            pe.wait_ge(gates_out, 1)
            for y in range(4):
                for t in range(ST):
                    last = nc.tensor.transpose(tp[0:HA, 1 + y // 2, (y % 2) * S + t * P:(y % 2) * S + (t + 1) * P],
                                               gsb[:, t, y * HA:(y + 1) * HA], ident[:, :])
            last.then_inc(gt_mm, 1)
            pe.wait_ge(em_ready, 1)
            for t in range(ST):
                for y in range(4):
                    q = (t * 4 + y) * HA
                    last = nc.tensor.transpose(tp[:, 0, q:q + HA], GTR[:, y, t * P:(t + 1) * P],
                                               ident[0:HA, 0:HA])
            last.then_inc(gc_mm, 1)
            pe.wait_ge(gc_ready, 1)
            pe.wait_ge(mod_ready, 3)
            for h in range(HA):
                if h:
                    pe.wait_ge(ml_tq, 2 * h)
                for q in range(2):
                    for d in range(2):
                        for t in range(ST):
                            col = q * WA + h * DA + d * P
                            last = nc.tensor.transpose(tp[:, q, d * S + t * P:d * S + (t + 1) * P],
                                                       proj[:, t, col:col + P], ident[:, :])
                last.then_inc(ml_t, 1)
                if h:
                    pe.wait_ge(ml_p, 4 * h)
                for q in range(2):
                    mm(tp[:, 2, q * S:(q + 1) * S], sel[:, h, :], ga_t[:, 2 + q, :], start=True, stop=True)
                pe.wait_ge(ml_tq, 2 * h + 2)
                for t in range(ST):
                    for d in range(2):
                        last = mm(tp[:, 3, t * S:(t + 1) * S], ml_qk[:, 1, d, t * P:(t + 1) * P],
                                  ml_qk[:, 0, d, :], start=d == 0, stop=d == 1)
                last.then_inc(ml_s, 1)
                pe.wait_ge(ml_p, 4 * h + 4)
                if h:
                    pe.wait_ge(ml_h, h)
                    pe.wait_ge(ml_sq, 2 * h)
                terms = {(0, 0): ((0, 0),), (1, 0): ((P, 0), (S, 1)),
                         (0, 1): ((S + P, 0), (2 * S, 1)), (1, 1): ((2 * S + P, 1),)}
                for (t, q), parts in terms.items():
                    for rhs_n in range(2):
                        for k, (a, ks) in enumerate(parts):
                            lhs = ml_e[:, a:a + P]
                            se = dict(start=k == 0, stop=k == len(parts) - 1)
                            if rhs_n == 0:
                                mm(gp[0][:, t, q * DA:(q + 1) * DA], lhs,
                                   proj[:, ks, 2 * WA + h * DA:2 * WA + (h + 1) * DA], **se)
                            else:
                                last = mm(gp[1][:, 0, 2 * t + q:2 * t + q + 1], lhs, ones[:, 0:1], **se)
                last.then_inc(ml_num, 1)
            pe.wait_ge(ml_out, 1)
            transpose_in(HB_ML, range(4), proj, 0)
            for step in range(HB + 3):
                n = step
                if n < HB:
                    if n < 2:
                        pe.wait_ge(h_ready, HB_ML + 4)
                    if n >= 2:
                        pe.wait_ge(na_tq, 2 * (n - 1))
                    for q in range(2):
                        for t in range(ST):
                            col = QB0 + q * WA + n * DB
                            last = nc.tensor.transpose(tp[:, n % 2, q * S + t * P:q * S + (t + 1) * P],
                                                       proj[:, t, col:col + DB], ident[:, :])
                    last.then_inc(na_t, 1)
                n = step - 1
                if 0 <= n < HB:
                    pe.wait_ge(na_tq, 2 * (n + 1))
                    pe.wait_ge(na_bias_ready, 2 * (n + 1))
                    if n >= 2:
                        pe.wait_ge(na_exp, 2 * (n - 1))
                    for t in range(ST):
                        o = tp[:, 2 + n % 2, t * S:(t + 1) * S]
                        mm(o, flip[:, :], na_bias[:, n % 2, 2 - 2 * t:2 - 2 * t + GR, :], start=True, stop=False)
                        last = mm(o, na_qk[:, n % 2, 0, t * P:(t + 1) * P], na_qk[:, n % 2, 1, :],
                                  start=False, stop=True)
                    last.then_inc(na_s, 1)
                n = step - 2
                if 0 <= n < HB:
                    pe.wait_ge(na_p, n + 1)
                    if n >= 2:
                        pe.wait_ge(na_ptc, n - 1)
                    for k in range(ST):
                        for t in range(ST):
                            last = nc.tensor.transpose(gp[0][:, n % 2, k * S + t * P:k * S + (t + 1) * P],
                                                       na_sc[:, n % 2, t, k * P:(k + 1) * P], ident[:, :])
                    last.then_inc(na_ptm, 1)
                n = step - 3
                if n >= 0:
                    pe.wait_ge(na_ptc, n + 1)
                    if n >= 2:
                        pe.wait_ge(na_lo, n - 1)
                    for k in range(ST):
                        col = QB0 + 2 * WA + n * DB
                        last = mm(gp[1][:, n % 2, 0:S], proj[:, k, col:col + DB], na_pt[:, n % 2, k, :],
                                  start=k == 0, stop=k == 1)
                    last.then_inc(na_o, 1)

            def mixed_ready(j):
                if j < 4:
                    pe.wait_ge(h_ready, HB_ML + j + 1)
                    pe.wait_ge(na_lo, HB)
                else:
                    pe.wait_ge(na_lo, 2 * (j - 3))
            stream(g_out, h_hi, h_lo, 0, mixed_ready)
            pe.wait_ge(ada_summed, ADA_N)
            for t in range(ST):
                pe.wait_ge(drained[t], g_up.chunk0)
            sum_broadcast(gate2).then_inc(mod_sum, 1)
            transpose_x(1, HB_NORM1, NP8)
            pe.wait_ge(mod_ready, 5)

            def pair_up(i):
                for t in range(ST):
                    pe.wait_ge(drained[t], g_up.chunk(i, 1) + 1)
                for b in range(2):
                    for f in range(4):
                        for t in range(ST):
                            o = (f % 2) * S + t * P
                            last = nc.tensor.transpose(tp[:, 2 * b + f // 2, o:o + P],
                                                       ff[:, b, t, f * P:(f + 1) * P], ident[:, :])
                last.then_inc(ff_t, 1)
            stream(g_up, h_hi, h_lo, 0, h_pairs(HB_NORM1), pair_up)

            def early(base, x_ready):
                def each(i, e, j, first):
                    c_ = 2 * i + e - 1
                    if j == 3 and not first:
                        transpose_in(base, (2 * c_, 2 * c_ + 1), xres, 0, x_ready(c_))
                return each

            def late(base, x_ready):
                def each(i, e, j, first):
                    if first and j == 1:
                        transpose_in(base, (6, 7), xres, 0, x_ready(3))
                return each

            def x_down(c_):
                return lambda t: pe.wait_ge(x_final, ST * (g_out.chunks + c_) + t + 1)
            stream(g_down, a_hi, a_lo, 0, lambda j: pe.wait_ge(ff_lo, j // 2 + 1),
                   each=early(HB_NORM2, x_down))
            stream(g_in2a, h_hi, h_lo, 0, h_pairs(HB_NORM2), each=late(HB_NORM2, x_down))

            def outputs(n0, h, v, w):
                half = slice((h % 2) * DH, (h % 2 + 1) * DH)
                if h % 2 == 0 and n0 + h:
                    pe.wait_ge(o2_out, (n0 + h) // 2)
                mm(tp[half, 3, 0:S], proj2[:, 0, v:v + DH], w[:, 0:S], start=True, stop=False)
                mm(tp[half, 3, P:S], proj2[:, 1, v:v + DH], w[:, S:SW_N], start=False, stop=True
                   ).then_inc(o2_mm, 1)

            def mixers(k):
                if k < 6:
                    n = k
                    if n == 0:
                        for t in range(ST):
                            pe.wait_ge(drained[t], g_in2b.chunk0)
                    if n == 4:
                        pe.wait_ge(kdup_ready, 1)
                    if n >= 4:
                        pe.wait_ge(q2_c, n - 3)
                    for a in range(2):
                        for t in range(ST):
                            src = (proj2[:, t, QA2 + (2 * n + a) * P:QA2 + (2 * n + a + 1) * P] if n < 4 else
                                   kdup[:, t, 2 * (n - 4) + a].rearrange("p u d -> p (u d)"))
                            last = nc.tensor.transpose(tp[:, n % 4, a * S + t * P:a * S + (t + 1) * P], src,
                                                       ident[:, :])
                    last.then_inc(q2_t, 1)
                if SW0 <= k < SK0:
                    h = k - SW0
                    if h < HS:
                        if h == 0:
                            pe.wait_ge(q2_c, 6)
                        if h >= 2:
                            pe.wait_ge(sw_max, h - 1)
                        half = slice((h % 2) * DH, (h % 2 + 1) * DH)
                        g = h // (HS // HK)
                        mm(tp[:, h % 2, 0:P], Q2[half, h // 2, 0:P], K2[half, g, 0:P], start=True, stop=True)
                        mm(tp[:, h % 2, P:SW_N], Q2[half, h // 2, P:S], K2[half, g, :], start=True, stop=True
                           ).then_inc(sw_s, 1)
                    h = k - SW0 - 2
                    if 0 <= h < HS:
                        pe.wait_ge(sw_p, h + 1)
                        if h >= 1:
                            pe.wait_ge(sw_ptc, h)
                        for m in range(3):
                            last = nc.tensor.transpose(tp[:, 2, m * P:(m + 1) * P],
                                                       SC[:, h % 2, m * P:(m + 1) * P], ident[:, :])
                        last.then_inc(sw_ptm, 1)
                    h = k - SW0 - 4
                    if 0 <= h < HS:
                        pe.wait_ge(sw_ptc, h + 1)
                        outputs(0, h, VA2 + (h // (HS // HK)) * DH, PT[:, h % 2])
                if SK0 <= k < SK0 + 8:
                    n = k - SK0
                    if n == 0:
                        pe.wait_ge(o2_out, HS // 2)
                    if n >= 4:
                        pe.wait_ge(q2_c, 6 + n - 3)
                    col = (QS2 if n < 4 else KS2) + 2 * (n % 4) * P
                    for a in range(2):
                        for t in range(ST):
                            last = nc.tensor.transpose(tp[:, n % 4, a * S + t * P:a * S + (t + 1) * P],
                                                       proj2[:, t, col + a * P:col + (a + 1) * P], ident[:, :])
                    last.then_inc(q2_t, 1)
                if SK1 <= k < SK_END:
                    h = k - SK1
                    if h < HS:
                        if h == 0:
                            pe.wait_ge(q2_c, 14)
                        if h >= 2:
                            pe.wait_ge(sk_lb, h - 1)
                        half = slice((h % 2) * DH, (h % 2 + 1) * DH)
                        mm(tp[:, h % 2, 0:S], K2[half, h // 2, 0:P], Q2[half, h // 2, :], start=True, stop=True)
                        mm(tp[:, h % 2, S:SW_N], K2[half, h // 2, P:S], Q2[half, h // 2, P:S], start=True,
                           stop=True).then_inc(sk_z, 1)
                    h = k - SK1 - 2
                    if 0 <= h < HS:
                        pe.wait_ge(sk_sp, h + 1)
                        pe.wait_ge(sk_mask, 1)
                        if h >= 1:
                            pe.wait_ge(sk_arg, h)
                        o = tp[:, 2]
                        mm(o[:, 0:S], TRI, SP_[:, h % 2, 0:S], start=True, stop=False)
                        mm(o[:, P:S], ones[:, :], SP_[:, h % 2, S:SW_N], start=False, stop=True)
                        mm(o[:, S:SW_N], TRI, SP_[:, h % 2, S:SW_N], start=True, stop=True).then_inc(sk_suf, 1)
                    h = k - SK1 - 4
                    if 0 <= h < HS:
                        pe.wait_ge(sk_a, h + 1)
                        outputs(HS, h, VS2 + h * DH, AA[:, h % 2])

            def mix_each(i, e, j, first):
                mixers((2 * i + e) * g_in2b.nb + j)
            stream(g_in2b, h_hi, h_lo, 0, lambda j: None, each=mix_each, unrolled=True)
            stream(g_bra, h_hi, h_lo, 0, lambda j: pe.wait_ge(o2_lo, j + 1))
            stream(g_brb, h_hi, h_lo, WA // P, lambda j: pe.wait_ge(o2_lo, g_bra.nb + j + 1))
            pe.wait_ge(merged, ST * g_brb.chunks)
            transpose_in(HB_MERGE, range(NP8), gates2, 0)

            def x_out2(c_):
                return lambda t: pe.wait_ge(drained[t], g_out2.chunk0 + c_ + 1)
            stream(g_out2, m_hi, m_lo, 0, h_pairs(HB_MERGE), each=early(HB_NORM3, x_out2))

            def pair_up2(i):
                for t in range(ST):
                    pe.wait_ge(drained[t], g_up2.chunk(i, 1) + 1)
                for f in range(4):
                    for t in range(ST):
                        o = (f % 2) * S + t * P
                        last = nc.tensor.transpose(tp[:, f // 2, o:o + P], ff[:, 1, t, f * P:(f + 1) * P],
                                                   ident[:, :])
                last.then_inc(ff_t, 1)
            stream(g_up2, h_hi, h_lo, 0, h_pairs(HB_NORM3), pair_up2, each=late(HB_NORM3, x_out2))
            stream(g_down2, a_hi, a_lo, 0, lambda j: pe.wait_ge(ff_lo, g_up.chunks // 2 + j // 2 + 1))

        @block.vector
        def _(dve):
            link = chain(dve_chain, dve)
            V = nc.vector

            def split(g, i, e, j):
                s = g.slot(e, j)
                dve.wait_ge(hi_ready, g.block(i, e, j) + 1)
                V.tensor_tensor(w_lo[:, s], raw[:, s], w_hi[:, s].bitcast(F32), ALU.subtract
                                ).then_inc(lo_ready, 1)

            def prime(g):
                for j in range(RING):
                    split(g, 0, 0, j)

            def stream(g, drain, side=None, each=None, before=None, nxt=None, unrolled=False):
                def step(i, e, first):
                    for j in range(g.nb):
                        if before:
                            before(i, e, j, first)
                        if not (first and j < RING):
                            split(g, i, e, j)
                        if j == RING - 1 and not first:
                            drain(i if e else i - 1, 1 - e)
                        if each:
                            each(i, e, j, first)
                    if side and not first and e == 0:
                        side(i - 1)
                (walk_unrolled if unrolled else walk)(dve, g.chunks, step)
                if nxt:
                    prime(nxt)
                drain((g.chunks - 1) // 2, (g.chunks - 1) % 2)
                if side:
                    side(g.chunks // 2 - 1)

            def chunk_done(g, i, e):
                dve.wait_ge(block_used, g.done(i, e))

            def nothing(i, e):
                pass

            def drain_proj(g, dst, col0):
                def drain(i, e):
                    chunk_done(g, i, e)
                    V.tensor_copy(dst[:, 1, bass.ds(col0 + i * 2 * CW + e * CW, CW)], gp[g.bank(e)][:, 1, :]
                                  ).then_inc(drained[1], 1)
                return drain

            def norm_stats(n):
                dve.wait_ge(sq_ready, 4 * ST * (n + 1))
                link(V.tensor_reduce(stat[:, 0:2], ssq[:, :, :], AX_X, ALU.add))
                V.tensor_scalar(stat[:, 2:4], stat[:, 0:2], 1.0 / D, EPS, ALU.mult, ALU.add
                                ).then_inc(ms_ready, 1)
                dve.wait_ge(rms_ready, n + 1)
                link(V.reciprocal(rstd[:, n, :], stat[:, 4:6]))

            def make_diag(n):
                for t in range(ST):
                    V.tensor_scalar(diag[:, t, :], ident[:, :], rstd[:, n, t:t + 1], None, ALU.mult
                                    ).then_inc(diag_ready, 1)

            def handover(full0, base, buf, scale, shift):
                def low(kp):
                    dve.wait_ge(h_high, base + kp + 1)
                    sl = slice(2 * kp, 2 * kp + 2)
                    V.tensor_tensor(h_lo[:, sl, :], buf[:, kp % 2], h_hi[:, sl, :].bitcast(F32), ALU.subtract
                                    ).then_inc(h_ready, 1)
                for kp in range(NP8):
                    dve.wait_ge(xt_ready, base + kp + 1)
                    if kp >= 2:
                        dve.wait_ge(h_ready, base + kp - 1)
                    for a in range(2):
                        kt = 2 * kp + a
                        last = V.tensor_scalar(buf[:, kp % 2, a], tp[:, kp % 4, a * S:(a + 1) * S],
                                               scale[:, kt:kt + 1], shift[:, kt:kt + 1], ALU.mult, ALU.add)
                    last.then_inc(h_full, 1)
                    if kp:
                        low(kp - 1)
                low(NP8 - 1)

            def low_direct(base, kps, hi, lo, scale=None):
                for kp in kps:
                    dve.wait_ge(h_high, base + kp + 1)
                    src = tp[:, kp % 4, :].rearrange("p (a s) -> p a s", a=2)
                    sl = slice(2 * kp, 2 * kp + 2)
                    if scale is None:
                        last = V.tensor_tensor(lo[:, sl, :], src, hi[:, sl, :].bitcast(F32), ALU.subtract)
                    else:
                        for a in range(2):
                            kt = 2 * kp + a
                            last = V.scalar_tensor_tensor(lo[:, kt, :], src[:, a], scale[:, kt:kt + 1],
                                                          hi[:, kt, :].bitcast(F32), ALU.mult, ALU.subtract)
                    last.then_inc(h_ready, 1)

            def mod_columns(which, g):
                V.tensor_copy(mod[:, 2 * which, :], tp[:, 3, 0:DT])
                link(V.scalar_tensor_tensor(mod[:, 2 * which + 1, :], tp[:, 3, DT:2 * DT], 1.0,
                                            vcol[:, 0, VC[g]:VC[g] + DT], ALU.add, ALU.mult))

            def add_ada(a, ring, k, dst):
                V.scalar_tensor_tensor(dst, ring, c_act[:, bass.ds(k, 1)], dst, ALU.mult, ALU.add
                                       ).then_inc(ada_summed, 1)

            dve.wait_ge(silu_ready, 1)
            link(V.tensor_tensor(vcol[:, 0, VC["gfin"]:VC["gfin"] + DT], vcol[:, 0, VC["gfin"]:VC["gfin"] + DT],
                                 vcol[:, 0, VC["mixg"]:VC["mixg"] + DT], ALU.mult))
            dve.wait_ge(const_ready, 1)
            norm_stats(0)
            make_diag(0)
            dve.wait_ge(acc_bias[0], 16)

            def ada_part1(i, k2, peeled):
                for p in range(4):
                    dve.wait_ge(ada1_landed[4 * k2 + p], i * 16 + 16)
                    if not (peeled and k2 == 0):
                        dve.wait_ge(ada_summed, i * 8 + (4 * k2 + p - 3))
                    add_ada(None, ada_first[:, 4 * k2 + p, :], i * 2 + k2, acc[:, p, :])
            for k2 in range(2):
                ada_part1(0, k2, True)
            with dve.Fori(1, DT // 2) as i:
                for k2 in range(2):
                    ada_part1(i, k2, False)
            dve.wait_ge(wg_high, 1)
            V.tensor_tensor(wg_lo[:, :, :], wg, wg_hi[:, :, :].bitcast(F32), ALU.subtract).then_inc(wg_split, 1)
            dve.wait_ge(mod_sum, 1)
            mod_columns(0, "g1")
            V.memset(stat[:, 8:9], 0.0).then_inc(mod_ready, 1)
            prime(g_in_a)
            handover(0, HB_NORM0, hf, mod[:, 1, :], mod[:, 0, :])

            def ada2(k0, piece_k_first):
                def each(i, e, j, first):
                    if j >= 6:
                        return
                    k = i * 2 + (k0 + e)
                    a = i * 12 + (PART2 + 6 * (k0 + e) + j)
                    dve.wait_ge(ada_landed[j % 2], i * 96 + 16 * (3 * (k0 + e) + j // 2 + 1))
                    if first and piece_k_first:
                        if j == 0:
                            dve.wait_ge(acc_bias[1], 16)
                        if j == 2:
                            dve.wait_ge(acc_bias[3], 16)
                    else:
                        dve.wait_ge(ada_summed, a - 5)
                    add_ada(a, ada_ring[:, j % 2, :], k,
                            ga1[:, j * ADA_W:(j + 1) * ADA_W] if j < 2 else acc[:, j - 2, :])
                return each
            stream(g_in_a, drain_proj(g_in_a, proj, 0), each=ada2(0, True), nxt=g_in_b)
            dve.wait_ge(gates_mm, 1)
            V.tensor_copy(gsb[:, :, :], tp[:, 0, 0:ST * 4 * HA].rearrange("p (t n) -> p t n", t=ST)
                          ).then_inc(gates_out, 1)
            each_b = ada2(g_in_a.chunks, False)
            stream(g_in_b, drain_proj(g_in_b, proj, QB0), each=each_b, nxt=g_out)
            for k in range(g_in_a.chunks + g_in_b.chunks, DT):
                for j in range(6):
                    each_b((k - g_in_a.chunks) // 2, k % 2, j, False)
            dve.wait_ge(mod_sum, 2)
            mod_columns(1, "g2")
            for b in range(2):
                V.tensor_copy(ga1[:, b * 2 * CW:(b + 1) * 2 * CW],
                              gp[b][:, :, :].rearrange("p t n -> p (t n)")).then_inc(mod_ready, 1)
            dve.wait_ge(gt_mm, 1)
            for y in range(4):
                link(V.tensor_scalar(GTR[:, y, :], tp[0:HA, 1 + y // 2, (y % 2) * S:(y % 2 + 1) * S],
                                     bg[:, y:y + 1], None, ALU.add))
            V.memset(stat[:, 9:10], 0.0).then_inc(gt_ready, 1)
            dve.wait_ge(gl_ln, 1)
            fg, ig = GTR[:, 1:4:2, :], GTR[:, 0:4:2, :]
            link(V.scalar_tensor_tensor(fg, fg, 0.0, ga_t[:, 0:2, :], ALU.min, ALU.subtract))
            bf, bb = ga_t[:, 0, :], ga_t[:, 1, :]
            link(V.tensor_tensor_scan(bf, GTR[:, 1, :], GTR[:, 1, :], 0.0, ALU.add, ALU.bypass))
            link(V.tensor_tensor_scan(bb[:, ::-1], GTR[:, 3, ::-1], GTR[:, 3, ::-1], 0.0, ALU.add, ALU.bypass))
            link(V.tensor_tensor(ig, ig, ga_t[:, 0:2, :], ALU.subtract))
            mf, mb = ga_t[:, 2, :], ga_t[:, 3, :]
            link(V.tensor_tensor_scan(mf, GTR[:, 0, :], GTR[:, 0, :], -3e38, ALU.max, ALU.bypass))
            link(V.tensor_tensor_scan(mb[:, ::-1], GTR[:, 2, ::-1], GTR[:, 2, ::-1], -3e38, ALU.max, ALU.bypass))
            V.tensor_tensor(fg, ga_t[:, 0:2, :], ga_t[:, 2:4, :], ALU.add).then_inc(gm_ready, 1)
            dve.wait_ge(gc_mm, 1)
            V.tensor_copy(gcol[:, :, :, :].rearrange("p t y h -> p (t y h)"), tp[:, 0, 0:ST * 4 * HA]
                          ).then_inc(gc_ready, 1)
            for h in range(HA):
                dve.wait_ge(ml_s, h + 1)
                if h:
                    dve.wait_ge(ml_num, h)
                for a, n, q, t0, m in ((0, S, 0, 0, mask_f[:, :]), (S, P, 0, P, mask_f[:, 0:P]),
                                       (S + P, P, 1, 0, mask_b[:, P:S]), (2 * S, S, 1, 0, mask_b[:, :])):
                    last = V.tensor_tensor(ml_e[:, a:a + n], m, tp[:, 2, q * S + t0:q * S + t0 + n],
                                           ALU.subtract)
                last.then_inc(ml_arg, 1)
                for k, (a, n, t, t0) in enumerate(((0, S, 0, 0), (S, P, 1, P), (S + P, P, 0, 0), (2 * S, S, 1, 0))):
                    dve.wait_ge(ml_exp, 4 * h + k + 1)
                    V.tensor_tensor(ml_e[:, a:a + n], ml_e[:, a:a + n], tp[:, 3, t * S + t0:t * S + t0 + n],
                                    ALU.mult).then_inc(ml_p, 1)
                dve.wait_ge(ml_den, h + 1)
                r = hcol[:, 0, 0:4].rearrange("p (t q) -> p t q", t=ST)
                link(V.tensor_tensor(r, r, gcol[:, :, 1:4:2, h], ALU.max))
                link(V.reciprocal(r, r))
                for t in range(ST):
                    ht = proj[:, t, h * DA:(h + 1) * DA]
                    link(V.tensor_scalar(ht, gp[0][:, t, 0:DA], hcol[:, 0, 2 * t:2 * t + 1], None, ALU.mult))
                    last = V.scalar_tensor_tensor(ht, gp[0][:, t, DA:2 * DA], hcol[:, 0, 2 * t + 1:2 * t + 2], ht,
                                                  ALU.mult, ALU.add)
                last.then_inc(ml_h, 1)
            dve.wait_ge(ml_sq, 2 * HA)
            V.tensor_scalar(hcol[:, 1, :], hcol[:, 1, :], 1.0 / DA, EPS, ALU.mult, ALU.add).then_inc(ml_ms, 1)
            dve.wait_ge(ml_rms, 1)
            link(V.reciprocal(hcol[:, 2, :], hcol[:, 2, :]))
            for t in range(ST):
                dve.wait_ge(ml_rms, 2 + t)
                for h in range(HA):
                    ht = proj[:, t, h * DA:(h + 1) * DA]
                    last = V.scalar_tensor_tensor(ht, ht, hcol[:, 2, 2 * h + t:2 * h + t + 1],
                                                  proj[:, t, 3 * WA + h * DA:3 * WA + (h + 1) * DA],
                                                  ALU.mult, ALU.mult)
            last.then_inc(ml_out, 1)
            low_direct(HB_ML, range(4), h_hi, h_lo, vcol[:, 0, VC["ghead"]:VC["ghead"] + 8])
            for step in range(HB + 3):
                n = step - 1
                if 0 <= n < HB:
                    dve.wait_ge(na_s, n + 1)
                    V.tensor_reduce(nst[:, n % 2, 0, :], tp[:, 2 + n % 2, :].rearrange("p (t s) -> p t s", t=ST),
                                    AX_X, ALU.max, negate=True).then_inc(na_max, 1)
                    dve.wait_ge(na_exp, 2 * (n + 1))
                    link(V.reciprocal(nst[:, n % 2, 2, :], nst[:, n % 2, 1, :]))
                    for t in range(ST):
                        last = V.tensor_scalar(na_sc[:, n % 2, t], na_sc[:, n % 2, t],
                                               nst[:, n % 2, 2, t:t + 1], None, ALU.mult)
                    last.then_inc(na_p, 1)
                n = step - 3
                if n >= 0:
                    dve.wait_ge(na_hi, n + 1)
                    V.tensor_tensor(h_lo[:, HB + n, :], gp[1][:, n % 2, 0:S], h_hi[:, HB + n, :].bitcast(F32),
                                    ALU.subtract).then_inc(na_lo, 1)

            def drain_gated(g, gate, buf, done0):
                def drain(i, e):
                    chunk_done(g, i, e)
                    c_ = 2 * i + e
                    if c_ >= 2:
                        dve.wait_ge(x_final, done0 + 2 * (c_ - 1))
                    for t in range(ST):
                        V.tensor_tensor(buf[:, e, t, :], gp[g.bank(e)][:, t, :], gate[:, bass.ds(g.col(i, e), CW)],
                                        ALU.mult).then_inc(drained[t], 1)
                return drain

            def ada3(i, e, j, first):
                a = i * 16 + (PART3 + 8 * e + j)
                dve.wait_ge(ada_landed[j % 2], i * 128 + 16 * (3 * DT + 4 * e + j // 2 + 1))
                if first and j < 2:
                    dve.wait_ge(acc_bias[2], 16)
                else:
                    dve.wait_ge(ada_summed, a - 1)
                add_ada(a, ada_ring[:, j % 2, :], i * 8 + (4 * e + j // 2),
                        gate2[:, (j % 2) * ADA_W:(j % 2 + 1) * ADA_W])
            stream(g_out, drain_gated(g_out, ga1, xt1, 0), each=ada3, nxt=g_up)
            dve.wait_ge(mod_sum, 3)
            for b in range(2):
                V.tensor_copy(gate2[:, b * 2 * CW:(b + 1) * 2 * CW],
                              gp[b][:, :, :].rearrange("p t n -> p (t n)")).then_inc(mod_ready, 1)
            norm_stats(1)
            make_diag(1)
            handover(NP8, HB_NORM1, hf_ff, mod[:, 3, :], mod[:, 2, :])

            def drain_g(i, e):
                if e == 1:
                    chunk_done(g_up, i, e)
                    for t in range(ST):
                        dve.wait_ge(drained[t], g_up.chunk(i, e))
                        V.tensor_copy(ff[:, 1, t, :], gp[g_up.bank(e)][:, t, :]).then_inc(drained[t], 1)

            def glu_side(i):
                gt = tp[:, 2:4, :].rearrange("p b (a s) -> p (b a) s", a=2)
                ut = tp[:, 0:2, :].rearrange("p b (a s) -> p (b a) s", a=2)

                def col(tile, r, f):
                    return vcol[:, tile, bass.ds(i * 4 + (r + f), 1)]
                dve.wait_ge(ff_t, i + 1)
                for f in range(4):
                    V.tensor_scalar(g4[:, f, :], gt[:, f, :], col(1, FT, f), col(2, FT, f), ALU.mult, ALU.add
                                    ).then_inc(ff_conv, 1)
                for f in range(4):
                    dve.wait_ge(ff_conv, i * 12 + (f + 1))
                    V.scalar_tensor_tensor(g4[:, f, 1:S], gt[:, f, 0:S - 1], col(1, 0, f), g4[:, f, 1:S],
                                           ALU.mult, ALU.add).then_inc(ff_conv, 1)
                for f in range(4):
                    dve.wait_ge(ff_conv, i * 12 + (f + 5))
                    V.scalar_tensor_tensor(g4[:, f, 0:S - 1], gt[:, f, 1:S], col(2, 0, f), g4[:, f, 0:S - 1],
                                           ALU.mult, ALU.add).then_inc(ff_conv, 1)
                dve.wait_ge(ff_act, i + 1)
                V.tensor_tensor(g4, g4, ut, ALU.mult).then_inc(ff_mul, 1)
                dve.wait_ge(ff_hi, i + 1)
                V.tensor_tensor(a_lo[:, bass.ds(i * 4, 4), :], g4, a_hi[:, bass.ds(i * 4, 4), :].bitcast(F32),
                                ALU.subtract).then_inc(ff_lo, 1)
                dve.wait_ge(ff_lo, i + 1)
            stream(g_up, drain_g, side=glu_side, nxt=g_down)
            gain2 = vcol[:, 0, VC["gfin"]:VC["gfin"] + DT]
            gain3 = vcol[:, 0, VC["ffng"]:VC["ffng"] + DT]

            def early(base, scale):
                def each(i, e, j, first):
                    c_ = 2 * i + e - 1
                    if j == 7 and not first:
                        low_direct(base, (2 * c_, 2 * c_ + 1), h_hi, h_lo, scale)
                return each
            stream(g_down, drain_gated(g_down, gate2, ff, ST * g_out.chunks), each=early(HB_NORM2, gain2),
                   nxt=g_in2a)
            low_direct(HB_NORM2, (6, 7), h_hi, h_lo, gain2)

            def between(i, e, j, first):
                if first:
                    if j == 4:
                        norm_stats(2)
                        dve.wait_ge(gain_landed, 16)
                    if j in (4, 5):
                        t = j - 4
                        V.scalar_tensor_tensor(xres[:, t, :], xres[:, t, :], rstd[:, 2, t:t + 1], gate2[:, :],
                                               ALU.mult, ALU.mult).then_inc(gain_used, 1)
                    if j == 7:
                        norm_stats(3)
                        V.tensor_tensor(rows2[:, :], rstd[:, 2, :], rstd[:, 3, :], ALU.mult
                                        ).then_inc(rows_ready, 1)

            def scaled_drain(g, dst, rows):
                def drain(i, e):
                    chunk_done(g, i, e)
                    if g is g_in2a:
                        dve.wait_ge(rows_ready, 1)
                    V.tensor_scalar(dst[:, 1, bass.ds(i * 2 * CW + e * CW, CW)], gp[g.bank(e)][:, 1, :],
                                    rows[:, 1:2], None, ALU.mult).then_inc(drained[1], 1)
                return drain
            stream(g_in2a, scaled_drain(g_in2a, proj2, rows2), each=between, nxt=g_in2b)
            ka = proj2[:, :, KA2:KA2 + HK * DH].rearrange("p t (g d) -> p t g d", g=HK)
            dve.wait_ge(drained[0], g_in2b.chunk0)
            dve.wait_ge(drained[1], g_in2b.chunk0)
            for u in range(2):
                for t in range(ST):
                    last = V.tensor_copy(kdup[:, t, :, u, :], ka[:, t])
            last.then_inc(kdup_ready, 1)

            def mixers_before(k):
                if SW0 <= k < SK0:
                    h = k - SW0
                    if h < HS:
                        sw = SW[:, h % 2]
                        dve.wait_ge(sw_s, h + 1)
                        dve.wait_ge(sw_bias, h + 1)
                        if h >= 2:
                            dve.wait_ge(sw_ptm, h - 1)
                        link(V.scalar_tensor_tensor(SC[:, h % 2], tp[:, h % 2, 0:SW_N], DH ** -0.5,
                                                    TB[:, h % 2], ALU.mult, ALU.add))
                        V.tensor_reduce(sw[:, 0, 0:1], SC[:, h % 2, 0:P], AX_X, ALU.max)
                        link(V.tensor_reduce(sw[:, 0, 1:2], SC[:, h % 2, P:SW_N], AX_X, ALU.max))
                        V.tensor_scalar(sw[:, 1, 0:2], sw[:, 0, 0:2], sink[:, h:h + 1], -1.0, ALU.max, ALU.mult
                                        ).then_inc(sw_max, 1)
                if SK1 <= k < SK_END:
                    h = k - SK1 - 2
                    if 0 <= h < HS:
                        dve.wait_ge(sk_suf, h + 1)
                        V.tensor_tensor(LB[:, h % 2], LB[:, h % 2], tp[:, 2, 0:SW_N], ALU.subtract
                                        ).then_inc(sk_arg, 1)

            def mixers_after(k):
                if SW0 <= k < SK0:
                    h = k - SW0
                    if h < HS:
                        sw = SW[:, h % 2]
                        dve.wait_ge(sw_exp, h + 1)
                        link(V.tensor_tensor(sw[:, 2, 0:2], sw[:, 2, 0:2], sw[:, 3, 0:2], ALU.add))
                        link(V.reciprocal(sw[:, 2, 0:2], sw[:, 2, 0:2]))
                        for t, (a, n) in enumerate(((0, P), (P, S))):
                            last = V.tensor_scalar(SC[:, h % 2, a:a + n], SC[:, h % 2, a:a + n],
                                                   sw[:, 2, t:t + 1], None, ALU.mult)
                        last.then_inc(sw_p, 1)
                if SK1 <= k < SK_END:
                    h = k - SK1
                    if h < HS:
                        z = tp[:, h % 2, 0:SW_N]
                        spv = SP_[:, h % 2].rearrange("p (a b) -> p a b", a=3)[:, 0:3:2, :]
                        if h == 0:
                            dve.wait_ge(sk_mask, 1)
                        dve.wait_ge(sk_l, h + 1)
                        if h >= 2:
                            dve.wait_ge(sk_suf, h - 1)
                        link(V.scalar_tensor_tensor(SP_[:, h % 2], z, 0.0, LL[:, h % 2], ALU.max, ALU.add))
                        V.tensor_tensor(spv, spv, M2, ALU.mult).then_inc(sk_sp, 1)
                        if h >= 2:
                            dve.wait_ge(sk_exp, h - 1)
                        V.scalar_tensor_tensor(LB[:, h % 2], z, 0.0, LL[:, h % 2], ALU.min, ALU.subtract
                                               ).then_inc(sk_lb, 1)

            def at(part):
                def hook(i, e, j, first):
                    k = (2 * i + e) * g_in2b.nb + j - LAG
                    if k >= 0:
                        part(k)
                return hook
            stream(g_in2b, scaled_drain(g_in2b, gates2, rows2), each=at(mixers_after),
                   before=at(mixers_before), nxt=g_bra, unrolled=True)
            for kp in range(NP8):
                dve.wait_ge(o2_hi, kp + 1)
                sl = slice(2 * kp, 2 * kp + 2)
                V.tensor_tensor(h_lo[:, sl, :], mixer_out(kp), h_hi[:, sl, :].bitcast(F32), ALU.subtract
                                ).then_inc(o2_lo, 1)

            def drain_branch(g, col0):
                def drain(i, e):
                    chunk_done(g, i, e)
                    for t in range(ST):
                        dve.wait_ge(sig_ready, i * 2 * ST + (ST * (g.chunk0 - g_bra.chunk0 + e) + t + 1))
                        gate = gates2[:, t, bass.ds(col0 + g.col(i, e), CW)]
                        V.tensor_tensor(gate, gp[g.bank(e)][:, t, :], gate, ALU.mult).then_inc(drained[t], 1)
                return drain
            stream(g_bra, drain_branch(g_bra, 0), nxt=g_brb)
            stream(g_brb, drain_branch(g_brb, D), nxt=g_out2)
            low_direct(HB_MERGE, range(NP8), m_hi, m_lo)

            def drain_add(g):
                def drain(i, e):
                    chunk_done(g, i, e)
                    for t in range(ST):
                        xs = xres[:, t, bass.ds(g.col(i, e), CW)]
                        V.tensor_tensor(xs, gp[g.bank(e)][:, t, :], xs, ALU.add).then_inc(drained[t], 1)
                return drain
            stream(g_out2, drain_add(g_out2), each=early(HB_NORM3, gain3), nxt=g_up2)
            low_direct(HB_NORM3, (6, 7), h_hi, h_lo, gain3)

            def rows3(i, e, j, first):
                if first and j == 4:
                    norm_stats(4)
                    V.memset(stat[:, 10:11], 0.0).then_inc(rows_ready, 1)

            def drain_up(i, e):
                if e == 1:
                    chunk_done(g_up2, i, e)
                    for t in range(ST):
                        dve.wait_ge(drained[t], g_up2.chunk(i, 0) + 1)
                        V.scalar_tensor_tensor(ff[:, 1, t, :], gp[g_up2.bank(e)][:, t, :], rstd[:, 4, t:t + 1],
                                               ff[:, 0, t, :], ALU.mult, ALU.mult).then_inc(drained[t], 1)

            def swiglu_side(i):
                dve.wait_ge(ff_hi, i + (g_up.chunks // 2 + 1))
                sl = bass.ds(i * 4, 4)
                V.tensor_tensor(a_lo[:, sl, :], tp[:, 0:2, :].rearrange("p b (a s) -> p (b a) s", a=2),
                                a_hi[:, sl, :].bitcast(F32), ALU.subtract).then_inc(ff_lo, 1)
            stream(g_up2, drain_up, side=swiglu_side, each=rows3, nxt=g_down2)
            stream(g_down2, drain_add(g_down2))
            norm_stats(5)
            dve.wait_ge(gain_landed, 32)
            for t in range(ST):
                for q in range(2):
                    xs = xres[:, t, q * (D // 2):(q + 1) * (D // 2)]
                    V.scalar_tensor_tensor(xs, xs, rstd[:, 5, t:t + 1], gate2[:, q * (D // 2):(q + 1) * (D // 2)],
                                           ALU.mult, ALU.mult).then_inc(out_ready, 1)


_INS = ["x", "c", "w_ada", "b_ada", "g_norm1", "w_in", "b_gates", "g_head_a", "rpb", "w_out", "g_norm2",
        "w_up", "conv_w", "conv_b", "w_down", "g_final", "norm_mix_g_2", "w_in_2", "sink_logits_2",
        "w_branch_a_2", "w_branch_b_2", "w_out_2", "norm_ffn_g_2", "w_ffn_in_2", "w_ffn_down_2",
        "norm_final_g_2"]


def kernel(**inputs):
    import numpy as _np
    import concourse.bacc as _bacc
    from concourse import mybir as _mybir
    from concourse.bass_utils import run_bass_kernel_spmd as _run

    nc = _bacc.Bacc("TRN2", target_bir_lowering=False, num_devices=1)
    arrays, args = {}, []
    for name in _INS:
        a = _np.ascontiguousarray(inputs[name])
        arrays[f"in_{name}_dram"] = a
        args.append(nc.dram_tensor(f"in_{name}_dram", a.shape, _mybir.dt.from_np(a.dtype),
                                   kind="ExternalInput").ap())
    shape = inputs["x"].shape
    args.append(nc.dram_tensor("out_0_dram", shape, _mybir.dt.float32, kind="ExternalOutput").ap())
    two_blocks(nc, *args)
    r = _run(nc, [arrays], core_ids=[0])
    return r.results[0]["out_0_dram"]
```

```python
from contextlib import ExitStack

import concourse.bass as bass
from concourse import mybir

F32 = mybir.dt.float32
F32R = mybir.dt.float32r
I32 = mybir.dt.int32
ALU = mybir.AluOpType
ACT = mybir.ActivationFunctionType
AX_X = mybir.AxisListType.X

P = 128
S = 256
ST = S // P
CW = 512
KB = 2
RING = 4
NEG = -1e30
EPS = 1e-6
ADA_W = 1024


class Gemm:

    def __init__(self, w, chunks, block0, chunk0, col0, col_e, col_i, rot):
        self.w = w.rearrange("(t p) n -> p t n", p=P)
        self.kts = w.shape[0] // P
        self.nb = self.kts // KB
        self.chunks, self.block0, self.chunk0 = chunks, block0, chunk0
        self.col0, self.col_e, self.col_i, self.rot = col0, col_e, col_i, rot
        assert (2 * self.nb) % RING == 0 and block0 % RING == 0

    def block(self, i, e, j):
        return self.block0 + e * self.nb + j + i * (2 * self.nb)

    def kt(self, j):
        return (j + self.rot) % self.nb * KB

    def slot(self, e, j):
        return (e * self.nb + j) % RING

    def turn(self, i, e, j):
        return self.block0 // RING + (e * self.nb + j) // RING + i * (2 * self.nb // RING)

    def done(self, i, e):
        return self.block0 + (e + 1) * self.nb + i * (2 * self.nb)

    def chunk(self, i, e):
        return self.chunk0 + e + i * 2

    def bank(self, e):
        return (self.chunk0 + e) % 2

    def col(self, i, e):
        return self.col0 + e * self.col_e + i * self.col_i


def walk(eng, chunks, step, cut=0):
    step(0, 0, True)
    pairs = (chunks - 1) // 2
    if pairs == 1:
        step(0, 1, False)
        step(1, 0, False)
    else:
        if cut:
            with eng.Fori(0, cut) as i:
                step(i, 1, False, True)
                step(i + 1, 0, False, True)
        with eng.Fori(cut, pairs) as i:
            step(i, 1, False)
            step(i + 1, 0, False)
    if chunks % 2 == 0:
        step((chunks - 1) // 2, 1, False)


def walk_unrolled(eng, chunks, step):
    for c in range(chunks):
        step(c // 2, c % 2, c == 0)


def two_blocks(nc, x, c, w_ada, b_ada, g_norm1, w_in, b_gates, g_head_a, rpb, w_out, g_norm2, w_up,
               conv_w, conv_b, w_down, g_final, norm_mix_g_2, w_in_2, sink_logits_2, w_branch_a_2,
               w_branch_b_2, w_out_2, norm_ffn_g_2, w_ffn_in_2, w_ffn_down_2, norm_final_g_2, out):
    D = x.shape[2]
    DT = D // P
    F = w_down.shape[1]
    FT = F // P
    HA = b_gates.shape[1] // 4
    DA = g_head_a.shape[1] // HA
    WA = HA * DA
    HB = rpb.shape[1]
    RR, RC = rpb.shape[2], rpb.shape[3]
    GW = 64
    GR = S // GW
    WC = 16
    DB = WA // HB
    HS, HK, DH = 16, 4, 64
    NJ = GR + 2
    w_ada, w_in, w_out, w_up, w_down = w_ada[0], w_in[0], w_out[0], w_up[0], w_down[0]
    w_in_2, w_out_2, w_ffn_in_2, w_ffn_down_2 = w_in_2[0], w_out_2[0], w_ffn_in_2[0], w_ffn_down_2[0]
    w_branch_a_2, w_branch_b_2 = w_branch_a_2[0], w_branch_b_2[0]
    GATES0 = 4 * WA
    QB0 = GATES0

    gemms = []

    def gemm(w, chunks, col0=0, col_e=CW, col_i=2 * CW, rot=0):
        last = gemms[-1] if gemms else None
        g = Gemm(w, chunks, last.block0 + last.chunks * last.nb if last else 0,
                 last.chunk0 + last.chunks if last else 0, col0, col_e, col_i, rot)
        gemms.append(g)
        return g

    g_in_a = gemm(w_in, 3 * WA // CW)
    g_in_b = gemm(w_in, 3 * WA // CW, col0=GATES0 + 4 * HA)
    g_in_o = gemm(w_in, WA // CW, col0=3 * WA)
    g_out = gemm(w_out, D // CW, rot=WA // P // KB)
    g_up = gemm(w_up, 2 * F // CW, col_e=F, col_i=CW)
    g_down = gemm(w_down, D // CW)
    N_QKV2 = HS * DH + 2 * HK * DH + 3 * HS * DH
    g_in2a = gemm(w_in_2, N_QKV2 // CW)
    g_in2b = gemm(w_in_2, 2 * D // CW, col0=N_QKV2)
    g_bra = gemm(w_branch_a_2, D // CW)
    g_brb = gemm(w_branch_b_2, D // CW)
    g_out2 = gemm(w_out_2, D // CW)
    g_up2 = gemm(w_ffn_in_2, 2 * F // CW, col_e=F, col_i=CW)
    g_down2 = gemm(w_ffn_down_2, D // CW)

    ctx = ExitStack()

    def sb(name, shape, dt=F32, scope=ctx):
        return scope.enter_context(nc.sbuf_tensor(name, shape, dt))

    def sem(name):
        return ctx.enter_context(nc.semaphore(name))

    with ctx:
        raw = sb("raw", [P, RING, KB, CW])
        w_hi = sb("w_hi", [P, RING, KB, CW], F32R)
        w_lo = sb("w_lo", [P, RING, KB, CW], F32R)
        xres = sb("xres", [P, ST, D])
        h_hi = sb("h_hi", [P, DT, S], F32R)
        h_lo = sb("h_lo", [P, DT, S], F32R)
        gate2 = sb("gate2", [P, D])
        ident = sb("ident", [P, P])
        ones = sb("ones", [P, P])
        diag = sb("diag", [P, ST, P])
        vcol = sb("vcol", [P, 3, 104])
        stat = sb("stat", [P, 16])
        rstd = sb("rstd", [P, 6, ST])
        rows2 = sb("rows2", [P, ST])
        ssq = sb("ssq", [P, ST, 4])
        junk = sb("junk", [P, CW])
        mod = sb("mod", [P, 4, DT])
        c_act = sb("c_act", [P, DT])
        VC = {"c": 0, "g1": 16, "g2": 32, "mixg": 48, "ffng": 64, "ghead": 80, "gfin": 88}

        s0 = ExitStack()
        sb("before_wg", [P, 2 * 7 * WA - 2 * DT * P], scope=s0)
        wg_hi = sb("wg_hi", [P, DT, P], F32R, scope=s0)
        wg_lo = sb("wg_lo", [P, DT, P], F32R, scope=s0)
        s0.close()

        s1 = ExitStack()
        proj = sb("proj", [P, ST, 7 * WA], scope=s1)
        ada_sum = sb("ada_sum", [P, 6, ADA_W], scope=s1)
        ga1 = ada_sum[:, 0:2, :].rearrange("p a b -> p (a b)")
        acc = ada_sum[:, 2:6, :]
        ada_ring = sb("ada_ring", [P, 2, ADA_W], scope=s1)
        sel = sb("sel", [HA, HA, P], scope=s1)
        pick = sb("pick", [P, 4 * DT - 1], scope=s1)
        srow = sb("srow", [2 * DT, P], scope=s1)
        flip = sb("flip", [P, P], scope=s1)
        mask_f = sb("mask_f", [P, S], scope=s1)
        mask_b = sb("mask_b", [P, S], scope=s1)
        gcol = sb("gcol", [P, ST, 4, HA], scope=s1)
        bg = sb("bg", [HA, 4], scope=s1)
        hcol = sb("hcol", [P, 3, 8], scope=s1)
        nst = sb("nst", [P, 2, 3, 2], scope=s1)
        ada_first = proj[:, :, :].rearrange("p a b -> p (a b)")[:, 0:8 * ADA_W].rearrange(
            "p (s n) -> p s n", s=8)
        vrows = proj[0:104, 1, 1536:1536 + 3 * P].rearrange("p (a b) -> p a b", a=3)
        wg = proj[:, 1, 2048:2048 + DT * 4 * HA].rearrange("p (t n) -> p t n", t=DT)

        def gate_columns(w):
            return w[:, :, :].rearrange("p t (y h) -> p t y h", y=4)[:, :, :, 0:HA]
        accf = acc.rearrange("p a b -> p (a b)")
        hf = proj[:, 0, 0:WA].rearrange("p (b a s) -> p b a s", b=2, a=2)
        ml_qk = proj[:, 0, 3 * WA:4 * WA].rearrange("p (q d s) -> p q d s", q=2, d=2)
        ml_e = proj[:, 1, 3 * WA:3 * WA + 768]
        GTR = gate2[0:HA, 0:1024].rearrange("p (y s) -> p y s", y=4)
        ga_t = gate2[0:HA, 1024:2048].rearrange("p (y s) -> p y s", y=4)
        na_qk = proj[:, 0, WA:2 * WA].rearrange("p (b q s) -> p b q s", b=2, q=2)
        na_sc = proj[:, 0, 2 * WA:3 * WA].rearrange("p (b t s) -> p b t s", b=2, t=2)
        na_pt = proj[:, 1, WA:2 * WA].rearrange("p (b t s) -> p b t s", b=2, t=2)
        na_bias = gate2[:, 0:4 * NJ * GW].rearrange(
            "p (b j c) -> p b j c", b=4, j=NJ)
        xt1 = proj[:, :, QB0 + WA:QB0 + 2 * WA].rearrange("p t (b n) -> p b t n", b=2)

        def na_out(kp):
            return proj[:, :, QB0 + 2 * kp * DB:QB0 + 2 * (kp + 1) * DB].rearrange("p t (a s) -> p a t s", a=2)
        s1.close()

        s2 = ExitStack()
        a_hi = sb("a_hi", [P, FT, S], F32R, scope=s2)
        a_lo = sb("a_lo", [P, FT, S], F32R, scope=s2)
        ff = sb("ff", [P, 2, ST, CW], scope=s2)
        hf_ff = ff[:, 0].rearrange("p b (a s) -> p b a s", a=2)
        g4 = ff[:, 1].rearrange("p t (a s) -> p (t a) s", a=2)
        s2.close()

        s3 = ExitStack()
        proj2 = sb("proj2", [P, ST, N_QKV2], scope=s3)
        gates2 = sb("gates2", [P, ST, 2 * D], scope=s3)
        tmp = sb("tmp", [P, 7680], scope=s3)
        sink = sb("sink", [P, HS], scope=s3)
        s3.close()
        s4 = ExitStack()
        m_hi = sb("m_hi", [P, DT, S], F32R, scope=s4)
        m_lo = sb("m_lo", [P, DT, S], F32R, scope=s4)
        s4.close()

        gp = [ctx.enter_context(nc.psum_tensor(f"gp{i}", [P, ST, CW], F32)) for i in range(2)]
        tp = ctx.enter_context(nc.psum_tensor("tp", [P, 4, CW], F32))

        raw_landed = [sem(f"raw_landed{i}") for i in range(RING)]
        hi_ready = sem("hi_ready")
        lo_ready = sem("lo_ready")
        block_used = sem("block_used")
        drained = [sem(f"drained{i}") for i in range(ST)]
        ada1_landed = [sem(f"ada1_landed{i}") for i in range(8)]
        ada_landed = [sem(f"ada_landed{i}") for i in range(2)]
        ada_summed = sem("ada_summed")
        acc_bias = [sem(f"acc_bias{i}") for i in range(4)]
        mod_sum = sem("mod_sum")
        mod_rows = sem("mod_rows")
        mod_ready = sem("mod_ready")
        x_landed = [sem(f"x_landed{i}") for i in range(ST)]
        vec_landed = sem("vec_landed")
        wg_landed = sem("wg_landed")
        const_ready = sem("const_ready")
        ident_ready = sem("ident_ready")
        c_landed = sem("c_landed")
        c_t = sem("c_t")
        vec_t = sem("vec_t")
        vec_ready = sem("vec_ready")
        silu_ready = sem("silu_ready")
        wg_clear = sem("wg_clear")
        wg_split = sem("wg_split")
        wg_high = sem("wg_high")
        gates_mm = sem("gates_mm")
        x_final = sem("x_final")
        sq_ready = sem("sq_ready")
        ms_ready = sem("ms_ready")
        rms_ready = sem("rms_ready")
        rows_ready = sem("rows_ready")
        diag_ready = sem("diag_ready")
        xt_ready = sem("xt_ready")
        h_full = sem("h_full")
        h_high = sem("h_high")
        h_ready = sem("h_ready")
        act_chain = sem("act_chain")
        dve_chain = sem("dve_chain")
        pool_chain = sem("pool_chain")
        gt_ready = sem("gt_ready")
        gl_ln = sem("gl_ln")
        gm_ready = sem("gm_ready")
        em_ready = sem("em_ready")
        gc_mm = sem("gc_mm")
        gc_ready = sem("gc_ready")
        ml_t = sem("ml_t")
        ml_tq = sem("ml_tq")
        ml_s = sem("ml_s")
        ml_arg = sem("ml_arg")
        ml_exp = sem("ml_exp")
        ml_p = sem("ml_p")
        ml_num = sem("ml_num")
        ml_den = sem("ml_den")
        ml_h = sem("ml_h")
        ml_sq = sem("ml_sq")
        ml_ms = sem("ml_ms")
        ml_rms = sem("ml_rms")
        ml_out = sem("ml_out")
        na_bias_landed = [sem(f"na_bias_landed{i}") for i in range(4)]
        na_bias_ready = sem("na_bias_ready")
        na_t = sem("na_t")
        na_tq = sem("na_tq")
        na_s = sem("na_s")
        na_max = sem("na_max")
        na_exp = sem("na_exp")
        na_p = sem("na_p")
        na_ptm = sem("na_ptm")
        na_ptc = sem("na_ptc")
        na_o = sem("na_o")
        na_stored = sem("na_stored")
        na_hi = sem("na_hi")
        na_lo = sem("na_lo")
        ff_conv = sem("ff_conv")
        ff_t = sem("ff_t")
        ff_act = sem("ff_act")
        ff_mul = sem("ff_mul")
        ff_hi = sem("ff_hi")
        ff_lo = sem("ff_lo")
        gain_landed = sem("gain_landed")
        gain_used = sem("gain_used")
        sink_landed = sem("sink_landed")
        q2_t = sem("q2_t")
        q2_c = sem("q2_c")
        kdup_ready = sem("kdup_ready")
        sw_s = sem("sw_s")
        sw_bias = sem("sw_bias")
        sw_max = sem("sw_max")
        sw_exp = sem("sw_exp")
        sw_p = sem("sw_p")
        sw_ptm = sem("sw_ptm")
        sw_ptc = sem("sw_ptc")
        o2_mm = sem("o2_mm")
        o2_out = sem("o2_out")
        o2_hi = sem("o2_hi")
        o2_lo = sem("o2_lo")
        sk_z = sem("sk_z")
        sk_l = sem("sk_l")
        sk_sp = sem("sk_sp")
        sk_lb = sem("sk_lb")
        sk_suf = sem("sk_suf")
        sk_arg = sem("sk_arg")
        sk_exp = sem("sk_exp")
        sk_a = sem("sk_a")
        sk_mask = sem("sk_mask")
        sig_ready = sem("sig_ready")
        merged = sem("merged")
        gained = sem("gained")
        final_rstd = sem("final_rstd")
        half_out = [sem(f"half_out{i}") for i in range(2 * ST)]
        out_landed = sem("out_landed")

        PART2 = 4 * DT
        PART2B = PART2 + 6 * 12
        PART2C = PART2B + 2 * 4
        K1 = DT - 4
        CUT = DT // 2 - 1
        PART3 = PART2 + 6 * DT
        ADA_N = PART3 + 2 * DT
        NP8 = DT // 2
        HB_NORM0, HB_ML, HB_NORM1, HB_NORM2 = 0, NP8, NP8 + 4, 2 * NP8 + 4
        HB_MERGE, HB_NORM3 = 3 * NP8 + 4, 4 * NP8 + 4
        LAG = RING - 1
        SW0 = 7
        SK0 = SW0 + HS + 5
        SK1 = SK0 + 9
        SK_END = SK1 + HS + 5
        assert SK_END + LAG <= g_in2b.chunks * g_in2b.nb

        ML0, ML_H = 6, 8
        assert ML0 + HA * ML_H + LAG <= g_in_b.chunks * g_in_b.nb
        assert HB + 3 + LAG <= g_in_o.chunks * g_in_o.nb

        def carve(a, n):
            return tmp[:, a:a + n]
        Q2 = carve(0, 2048).rearrange("p (t s) -> p t s", t=8)
        K2 = carve(2048, 2048).rearrange("p (t s) -> p t s", t=8)
        kdup = carve(4096, 1024).rearrange("p (t g u d) -> p t g u d", t=ST, g=HK, u=2)
        ND = carve(4096 + 1024, 384)
        NDI = carve(4096 + 1024 + 384, 384)
        TB = carve(2048 + 1024, 768).rearrange("p (b n) -> p b n", b=2)
        SC = carve(5888, 768).rearrange("p (b n) -> p b n", b=2)
        PT = carve(5888 + 768, 768).rearrange("p (b n) -> p b n", b=2)
        SW = carve(7424, 64).rearrange("p (b a n) -> p b a n", b=2, a=4)
        LL = carve(4096, 768).rearrange("p (b n) -> p b n", b=2)
        SP_ = carve(4864, 768).rearrange("p (b n) -> p b n", b=2)
        LB = carve(5888, 768).rearrange("p (b n) -> p b n", b=2)
        AA = carve(5888 + 768, 768).rearrange("p (b n) -> p b n", b=2)
        M2 = gate2[:, 0:256].rearrange("p (a b) -> p a b", a=2)
        TRI = gate2[:, 256:384]
        QA2, KA2 = 0, HS * DH
        VA2 = KA2 + HK * DH
        QS2 = VA2 + HK * DH
        KS2, VS2 = QS2 + HS * DH, QS2 + 2 * HS * DH
        OA = proj2[:, :, QA2:QA2 + HS * DH].rearrange("p a (b s) -> p a b s", b=4)
        OS = proj2[:, :, QS2:QS2 + HS * DH].rearrange("p a (b s) -> p a b s", b=4)

        def mixer_out(kp):
            return (OA, OS)[kp // 4][:, (kp % 4) // 2, 2 * (kp % 2):2 * (kp % 2) + 2, :]
        SW_N = S + P

        def chain(sem_, eng):
            count = [0]

            def link(ins):
                count[0] += 1
                ins.then_inc(sem_, 1)
                eng.wait_ge(sem_, count[0])
            return link

        block = ctx.enter_context(nc.Block())

        @block.sync
        def _(sp):
            def load(g, i, e, j):
                b = g.block(i, e, j)
                if not isinstance(b, int) or b >= RING:
                    sp.wait_ge(lo_ready, b - (RING - 1))
                s = g.slot(e, j)
                sp.dma_start(raw[:, s], g.w[:, g.kt(j):g.kt(j) + KB, bass.ds(g.col(i, e), CW)]
                             ).then_inc(raw_landed[s], 16)

            def ada(a, slot, k, col):
                if not isinstance(a, int) or a >= PART2 + 2:
                    sp.wait_ge(ada_summed, a - 1)
                sp.dma_start(ada_ring[:, slot, :], w_ada[bass.ds(k * P, P), bass.ds(col, ADA_W)]
                             ).then_inc(ada_landed[slot], 16)

            def prime(g):
                for j in range(RING):
                    load(g, 0, 0, j)

            sp.dma_start(xres[:, 0, :], x[0, 0:P, :]).then_inc(x_landed[0], 16)
            sp.dma_start(xres[:, 1, :], x[0, P:S, :]).then_inc(x_landed[1], 16)
            for k in range(2):
                for p in range(4):
                    sp.dma_start(ada_first[:, 4 * k + p, :],
                                 w_ada[k * P:(k + 1) * P, p * ADA_W:(p + 1) * ADA_W]
                                 ).then_inc(ada1_landed[4 * k + p], 16)
            prime(g_in_a)
            with sp.Fori(1, DT // 2) as i:
                for k in range(2):
                    for p in range(4):
                        sp.wait_ge(ada_summed, i * 8 + (4 * k + p - 7))
                        sp.dma_start(ada_first[:, 4 * k + p, :],
                                     w_ada[bass.ds(i * 2 * P + k * P, P), p * ADA_W:(p + 1) * ADA_W]
                                     ).then_inc(ada1_landed[4 * k + p], 16)

            def stream(g, side=None, nxt=None, early=None, unrolled=False):
                def step(i, e, first, extra=False):
                    for j in range(g.nb):
                        if not (first and j < RING):
                            load(g, i, e, j)
                        if side:
                            side(i, e, j)
                        if early and (first or extra):
                            early(i, e, j)
                if unrolled:
                    walk_unrolled(sp, g.chunks, step)
                else:
                    walk(sp, g.chunks, step, CUT if early else 0)
                if nxt:
                    prime(nxt)

            def ada_in(k0):
                def side(i, e, j):
                    if k0 == 0 and isinstance(i, int) and i + e == 0:
                        for m in (j,) if j < 2 else (2, 3, 4, 5) if j == 7 else ():
                            ada(PART2 + m, m % 2, 0, 2 * D + m * ADA_W)
                    elif j < 6:
                        ada(i * 12 + (PART2 + 6 * (k0 + e) + j), j % 2, i * 2 + (k0 + e), 2 * D + j * ADA_W)
                return side

            def ada_out(i, e, j):
                c_ = 2 * i + e
                for m in ((j,) if j < 4 else ()) if c_ else {6: (0, 1), 7: (2, 3)}.get(j, ()):
                    ada(PART2C + 4 * c_ + m, m % 2, K1 + c_, 2 * D + (m + 2) * ADA_W)

            def ada_up(i, e, j):
                if isinstance(i, int) and i + e == 0:
                    for m in (j,) if j < 2 else (2, 3) if j == 7 else ():
                        ada(PART3 + m, m % 2, m // 2, 5 * D + (m % 2) * ADA_W)
                elif j < 2:
                    ada(i * 4 + (PART3 + 2 + 2 * e + j), j, i * 2 + (e + 1), 5 * D + j * ADA_W)

            def bias(n):
                if n < 4:
                    sp.wait_ge(ml_s, HA)
                else:
                    sp.wait_ge(na_s, n - 3)
                for a in range(2):
                    src = bass.AP(tensor=rpb.tensor, offset=rpb.offset + n * RR * RC
                                  + (RR // 2 - 2 - a) * RC + RC // 2 - (GW - 1),
                                  ap=[[1, GW], [RC, NJ], [1, GW]])
                    sp.dma_start(na_bias[a * GW:(a + 1) * GW, n % 4], src
                                 ).then_inc(na_bias_landed[n % 4], 16)

            def biases(i, e, j):
                k = (2 * i + e) * g_in_o.nb + j
                if j < 4:
                    n = 4 * e + j
                    ada(PART2B + n, n % 2, K1 + n // 2, 2 * D + (n % 2) * ADA_W)
                if k == 0:
                    for n in range(4):
                        bias(n)
                if 6 <= k < 6 + HB - 4:
                    bias(k - 2)
            assert g_in_a.chunks == g_in_b.chunks == 6
            stream(g_in_a, ada_in(0), g_in_b)
            stream(g_in_b, ada_in(g_in_a.chunks), g_in_o)
            stream(g_in_o, biases, g_out, unrolled=True)
            stream(g_out, ada_out, g_up)
            stream(g_up, None, g_down, early=ada_up)
            stream(g_down, None, g_in2a)
            sp.wait_ge(drained[1], g_down.chunk0 + g_down.chunks)
            sp.dma_start(gate2[:, :], bass.AP(tensor=g_final.tensor, offset=g_final.offset,
                                              ap=[[0, P], [1, D]])).then_inc(gain_landed, 16)
            sp.wait_ge(x_final, 2 * (g_out.chunks + g_down.chunks))
            sp.dma_start(sink[:, :], bass.AP(tensor=sink_logits_2.tensor, offset=sink_logits_2.offset,
                                             ap=[[0, P], [1, HS]])).then_inc(sink_landed, 16)
            stream(g_in2a, None, g_in2b)
            stream(g_in2b, None, g_bra)
            stream(g_bra, None, g_brb)
            stream(g_brb, None, g_out2)
            sp.wait_ge(sk_a, HS)
            sp.wait_ge(sk_suf, HS)
            sp.dma_start(gate2[:, :], bass.AP(tensor=norm_final_g_2.tensor, offset=norm_final_g_2.offset,
                                              ap=[[0, P], [1, D]])).then_inc(gain_landed, 16)
            stream(g_out2, None, g_up2)
            stream(g_up2, None, g_down2)
            stream(g_down2)
            for t, q in ((0, 0), (1, 0), (0, 1), (1, 1)):
                sp.wait_ge(half_out[2 * t + q], 1)
                sp.dma_start(out[0, t * P:(t + 1) * P, q * (D // 2):(q + 1) * (D // 2)],
                             xres[:, t, q * (D // 2):(q + 1) * (D // 2)]).then_inc(out_landed, 16)
            sp.wait_ge(out_landed, 16 * 2 * ST)

        @block.gpsimd
        def _(pool):
            link = chain(pool_chain, pool)

            def pred(ap, cmp, fill, base, pattern, mul):
                link(nc.gpsimd.affine_select(out=ap, in_=ap, compare_op=cmp, fill=fill, base=base,
                                             pattern=pattern, channel_multiplier=mul))
            link(nc.gpsimd.memset(ident[:, :], 0.0))
            nc.gpsimd.affine_select(out=ident[:, :], in_=ident[:, :], compare_op=ALU.not_equal, fill=1.0, base=0,
                                    pattern=[[-1, P]], channel_multiplier=1).then_inc(ident_ready, 1)
            link(nc.gpsimd.memset(acc, 0.0))
            pool.dma_start(accf[0:1, :], b_ada[0:1, 0:2 * D]).then_inc(acc_bias[0], 16)
            link(nc.gpsimd.memset(pick[:, :], 0.0))
            link(nc.gpsimd.memset(pick[:, 2 * DT - 1:2 * DT], 1.0))
            nc.gpsimd.memset(ones[:, :], 1.0).then_inc(const_ready, 1)
            with nc.allow_non_contiguous_dma(reason="gate columns"):
                pool.dma_start(wg, w_in.rearrange("(t p) n -> p t n", p=P)[:, :, GATES0:GATES0 + 4 * HA]
                               ).then_inc(wg_landed, 16)
                pool.dma_start(bg[:, :], b_gates[0].rearrange("(y h) -> h y", h=HA)).then_inc(wg_landed, 16)
            nc.gpsimd.memset(wg_hi[:, :, :].bitcast(F32), 0.0).then_inc(wg_clear, 1)
            nc.gpsimd.memset(wg_lo[:, :, :].bitcast(F32), 0.0).then_inc(wg_clear, 1)
            link(nc.gpsimd.memset(sel[:, :, :], 0.0))
            pred(sel[:, :, :], ALU.not_equal, 1.0, 0, [[-1, HA], [0, P]], 1)
            link(nc.gpsimd.memset(flip[:, :], 0.0))
            pred(flip[:, :], ALU.not_equal, 1.0, -(GW - 1), [[1, P]], 1)
            pred(flip[:, :], ALU.not_equal, 1.0, -(3 * GW - 1), [[1, P]], 1)
            link(nc.gpsimd.memset(mask_f[:, :], 0.0))
            pred(mask_f[:, 0:P], ALU.is_ge, NEG, 0, [[1, P]], -1)
            link(nc.gpsimd.memset(mask_b[:, :], 0.0))
            nc.gpsimd.affine_select(out=mask_b[:, P:S], in_=mask_b[:, P:S], compare_op=ALU.is_ge, fill=NEG,
                                    base=0, pattern=[[-1, P]], channel_multiplier=1
                                    ).then_inc(const_ready, 1)
            link(nc.gpsimd.memset(ga1, 0.0))
            pool.dma_start(ga1[0:1, :], b_ada[0:1, 2 * D:3 * D]).then_inc(acc_bias[1], 16)
            pool.wait_ge(mod_ready, 1)
            link(nc.gpsimd.memset(acc, 0.0))
            pool.dma_start(accf[0:1, :], b_ada[0:1, 3 * D:5 * D]).then_inc(acc_bias[3], 16)
            for n in range(HB):
                pool.wait_ge(na_bias_landed[n % 4], 32 * (n // 4 + 1))
                for a in range(2):
                    v = na_bias[a * GW:(a + 1) * GW, n % 4]
                    pred(v[:, :, 0:GW - WC], ALU.is_ge, NEG, WC // 2 - (GW - 1), [[0, NJ], [1, GW - WC]], 1)
                    right = v[:, :, WC:GW]
                    nc.gpsimd.affine_select(out=right, in_=right, compare_op=ALU.is_ge, fill=NEG,
                                            base=GW - 1 + WC // 2 - 1 - WC, pattern=[[0, NJ], [-1, GW - WC]],
                                            channel_multiplier=-1).then_inc(na_bias_ready, 1)

            pool.wait_ge(na_s, HB)
            link(nc.gpsimd.memset(gate2[:, :], 0.0))
            pool.dma_start(gate2[0:1, :], b_ada[0:1, 5 * D:6 * D]).then_inc(acc_bias[2], 16)

            def add_x(g, buf):
                def step(i, e, first):
                    for t in range(ST):
                        pool.wait_ge(drained[t], g.chunk(i, e) + 1)
                        xs = xres[:, t, bass.ds(g.col(i, e), CW)]
                        nc.gpsimd.tensor_tensor(xs, xs, buf[:, e, t, :], ALU.add).then_inc(x_final, 1)
                walk(pool, g.chunks, step)
            add_x(g_out, xt1)
            add_x(g_down, ff)
            pool.wait_ge(gain_used, ST)
            for a, base in ((0, 0), (P, -P)):
                n = P if a == 0 else S
                nd = ND[:, a:a + n]
                link(nc.gpsimd.iota(NDI[:, a:a + n].bitcast(I32), [[1, n]], base=base, channel_multiplier=-1))
                link(nc.gpsimd.tensor_copy(nd, NDI[:, a:a + n].bitcast(I32)))
                pred(nd, ALU.is_ge, NEG, -base, [[-1, n]], 1)
                if a:
                    pred(nd, ALU.is_ge, NEG, P - 1 + base, [[1, n]], -1)
            link(nc.gpsimd.memset(M2, 1.0))
            pred(M2, ALU.is_gt, 0.0, 0, [[0, 2], [1, P]], -1)
            link(nc.gpsimd.memset(TRI, 1.0))
            nc.gpsimd.affine_select(out=TRI, in_=TRI, compare_op=ALU.is_gt, fill=0.0, base=0,
                                    pattern=[[-1, P]], channel_multiplier=1).then_inc(sk_mask, 1)
            for h in range(HS):
                if h >= 2:
                    pool.wait_ge(sw_max, h - 1)
                slope = 2.0 ** (-8.0 * (h + 1) / HS)
                nc.gpsimd.tensor_scalar(TB[:, h % 2], ND, slope, None, ALU.mult).then_inc(sw_bias, 1)
            for h in range(HS):
                pool.wait_ge(sk_exp, h + 1)
                av = AA[:, h % 2].rearrange("p (a b) -> p a b", a=3)[:, 0:3:2, :]
                nc.gpsimd.tensor_tensor(av, av, M2, ALU.mult).then_inc(sk_a, 1)

            def step_b(i, e, first):
                for t in range(ST):
                    pool.wait_ge(drained[t], g_brb.chunk(i, e) + 1)
                    m = gates2[:, t, bass.ds(g_brb.col(i, e), CW)]
                    nc.gpsimd.tensor_tensor(m, m, gates2[:, t, bass.ds(D + g_brb.col(i, e), CW)],
                                            ALU.add).then_inc(merged, 1)
            walk(pool, g_brb.chunks, step_b)

        @block.scalar
        def _(act):
            link = chain(act_chain, act)

            def split(g, i, e, j):
                b, s = g.block(i, e, j), g.slot(e, j)
                act.wait_ge(raw_landed[s], 16 * (g.turn(i, e, j) + 1))
                if not isinstance(b, int) or b >= RING:
                    act.wait_ge(block_used, b - (RING - 1))
                nc.scalar.copy(w_hi[:, s], raw[:, s]).then_inc(hi_ready, 1)

            def prime(g, js=range(RING)):
                for j in js:
                    split(g, 0, 0, j)

            def stream(g, drain, side=None, each=None, nxt=None, tail=None, unrolled=False):
                def step(i, e, first):
                    for j in range(g.nb):
                        if not (first and j < RING):
                            split(g, i, e, j)
                        if j == RING - 1 and not first:
                            drain(i if e else i - 1, 1 - e)
                        if each:
                            each(i, e, j, first)
                    if side and not first and e == 0:
                        side(i - 1)
                (walk_unrolled if unrolled else walk)(act, g.chunks, step)
                if nxt:
                    prime(nxt, range(RING - 1 if tail else RING))
                if tail:
                    chunk_done(g, (g.chunks - 1) // 2, (g.chunks - 1) % 2)
                    tail()
                    prime(nxt, (RING - 1,))
                drain((g.chunks - 1) // 2, (g.chunks - 1) % 2)

            def chunk_done(g, i, e):
                act.wait_ge(block_used, g.done(i, e))

            def drain_proj(g, dst, col0):
                def drain(i, e):
                    chunk_done(g, i, e)
                    nc.scalar.copy(dst[:, 0, bass.ds(col0 + i * 2 * CW + e * CW, CW)], gp[g.bank(e)][:, 0, :]
                                   ).then_inc(drained[0], 1)
                return drain

            def square(n, c, x_ready):
                for t in range(ST):
                    x_ready(t)
                    if c == 0 and n and t == 0:
                        act.wait_ge(ms_ready, n)
                    k = 4 * ST * n + c * ST + t
                    if k:
                        act.wait_ge(sq_ready, k)
                    nc.scalar.activation(junk[:, :], xres[:, t, c * CW:(c + 1) * CW], ACT.Square,
                                         accum_out=ssq[:, t, c:c + 1]).then_inc(sq_ready, 1)

            def root(n):
                act.wait_ge(ms_ready, n + 1)
                nc.scalar.activation(stat[:, 4:6], stat[:, 2:4], ACT.Sqrt).then_inc(rms_ready, 1)

            def added(g, c, done0):
                return lambda t: act.wait_ge(x_final, done0 + ST * c + t + 1)

            def drained_to(g, c):
                return lambda t: act.wait_ge(drained[t], g.chunk0 + c + 1)

            def high(full0, base, src):
                for kp in range(NP8):
                    act.wait_ge(h_full, full0 + kp + 1)
                    nc.scalar.copy(h_hi[:, 2 * kp:2 * kp + 2, :], src[:, kp % 2]).then_inc(h_high, 1)

            def high_direct(base, kps, dst, scale=None):
                for kp in kps:
                    act.wait_ge(xt_ready, base + kp + 1)
                    src = tp[:, kp % 4, :].rearrange("p (a s) -> p a s", a=2)
                    if scale is None:
                        last = nc.scalar.copy(dst[:, 2 * kp:2 * kp + 2, :], src)
                    else:
                        for a in range(2):
                            kt = 2 * kp + a
                            last = nc.scalar.activation(dst[:, kt, :], src[:, a], ACT.Identity,
                                                        scale=scale[:, kt:kt + 1])
                    last.then_inc(h_high, 1)

            def rows(tile, r, vec, landed=vec_landed):
                n = vec.shape[0] // P
                act.dma_start(vrows[r:r + n, tile, :], vec.rearrange("(t p) -> t p", p=P)
                               ).then_inc(landed, 16)
            rows(0, VC["c"], c[0], c_landed)
            rows(0, VC["g1"], g_norm1[0])
            rows(0, VC["g2"], g_norm2[0])
            rows(0, VC["mixg"], norm_mix_g_2[0])
            rows(0, VC["ffng"], norm_ffn_g_2[0])
            rows(0, VC["ghead"], g_head_a[0])
            rows(0, VC["gfin"], g_final)
            rows(1, 0, conv_w[0, 0])
            rows(1, FT, conv_w[0, 1])
            rows(2, 0, conv_w[0, 2])
            rows(2, FT, conv_b[0])
            act.wait_ge(c_t, 1)
            nc.scalar.activation(c_act[:, :], tp[:, 3, 0:DT], ACT.Silu).then_inc(silu_ready, 1)
            act.wait_ge(vec_t, 1)
            nc.scalar.copy(vcol[:, 0, :], tp[:, 0, 0:104]).then_inc(vec_ready, 1)
            nc.scalar.copy(vcol[:, 1:3, 0:2 * FT], tp[:, 1:3, 0:2 * FT]).then_inc(vec_ready, 1)
            act.wait_ge(wg_landed, 32)
            act.wait_ge(wg_clear, 1)
            nc.scalar.copy(gate_columns(wg_hi), wg.rearrange("p t (y h) -> p t y h", y=4)).then_inc(wg_high, 1)
            for c_ in range(4):
                square(0, c_, lambda t: act.wait_ge(x_landed[t], 16))
            root(0)
            prime(g_in_a)
            high(0, HB_NORM0, hf)
            stream(g_in_a, drain_proj(g_in_a, proj, 0), nxt=g_in_b)
            act.preload_act_table_set("natural_log_exp_and_others")

            def at(g, part):
                def hook(i, e, j, first):
                    k = (2 * i + e) * g.nb + j - LAG
                    if k >= 0:
                        part(k)
                return hook

            fg = GTR[:, 1:4:2, :]

            def mlstm(k):
                if k == 0:
                    act.wait_ge(gt_ready, 1)
                    link(nc.scalar.activation(ga_t[:, 0:2, :], fg, ACT.Abs))
                    link(nc.scalar.activation(ga_t[:, 0:2, :], ga_t[:, 0:2, :], ACT.Exp, scale=-1.0))
                    nc.scalar.activation(ga_t[:, 0:2, :], ga_t[:, 0:2, :], ACT.Ln, bias=1.0).then_inc(gl_ln, 1)
                if k == 2:
                    act.wait_ge(gm_ready, 1)
                    nc.scalar.activation(fg, fg, ACT.Exp, scale=-1.0).then_inc(em_ready, 1)
                h, part = (k - ML0) // ML_H, (k - ML0) % ML_H
                if k < ML0 or h >= HA:
                    return
                if part == 0:
                    act.wait_ge(ml_t, h + 1)
                    nc.scalar.copy(ml_qk[:, 0], tp[:, 0, :].rearrange("p (d s) -> p d s", d=2)).then_inc(ml_tq, 1)
                    nc.scalar.mul(ml_qk[:, 1], tp[:, 1, :].rearrange("p (d s) -> p d s", d=2), DA ** -0.5
                                  ).then_inc(ml_tq, 1)
                if part == 2:
                    act.wait_ge(ml_arg, h + 1)
                    act.wait_ge(gc_ready, 1)
                    for a, n, t, q in ((0, 256, 0, 0), (256, 128, 1, 0), (384, 128, 0, 2), (512, 256, 1, 2)):
                        nc.scalar.activation(ml_e[:, a:a + n], ml_e[:, a:a + n], ACT.Exp,
                                             bias=gcol[:, t, q, h:h + 1]).then_inc(ml_exp, 1)
                if part == 5:
                    act.wait_ge(ml_num, h + 1)
                    nc.scalar.activation(hcol[:, 0, 0:4], tp[:, 2, 0:4], ACT.Abs).then_inc(ml_den, 1)
                if part == 6:
                    act.wait_ge(ml_h, h + 1)
                    for t in range(ST):
                        if 2 * h + t:
                            act.wait_ge(ml_sq, 2 * h + t)
                        else:
                            act.wait_ge(sq_ready, 4 * ST)
                        nc.scalar.activation(junk[:, 0:DA], proj[:, t, h * DA:(h + 1) * DA], ACT.Square,
                                             accum_out=hcol[:, 1, 2 * h + t:2 * h + t + 1]).then_inc(ml_sq, 1)
            stream(g_in_b, drain_proj(g_in_b, proj, QB0), each=at(g_in_b, mlstm), nxt=g_in_o, unrolled=True)

            def neighbours(k):
                n = k
                if 0 <= n < HB:
                    act.wait_ge(na_t, n + 1)
                    nc.scalar.mul(na_qk[:, n % 2, 0], tp[:, 0, 0:S], DB ** -0.5).then_inc(na_tq, 1)
                    nc.scalar.copy(na_qk[:, n % 2, 1], tp[:, 0, S:2 * S]).then_inc(na_tq, 1)
                n = k - 1
                if 0 <= n < HB:
                    act.wait_ge(na_max, n + 1)
                    if n >= 2:
                        act.wait_ge(na_ptm, n - 1)
                    for t in range(ST):
                        nc.scalar.activation(na_sc[:, n % 2, t], tp[:, 1, t * S:(t + 1) * S], ACT.Exp,
                                             bias=nst[:, n % 2, 0, t:t + 1],
                                             accum_out=nst[:, n % 2, 1, t:t + 1]).then_inc(na_exp, 1)
                n = k - 2
                if 0 <= n < HB:
                    act.wait_ge(na_ptm, n + 1)
                    if n >= 2:
                        act.wait_ge(na_o, n - 1)
                    nc.scalar.copy(na_pt[:, n % 2], tp[:, 2, :].rearrange("p (t s) -> p t s", t=2)
                                   ).then_inc(na_ptc, 1)
                n = k - 3
                if 0 <= n < HB:
                    act.wait_ge(na_o, n + 1)
                    nc.scalar.copy(proj[:, :, QB0 + n * DB:QB0 + (n + 1) * DB],
                                   tp[:, 3, 0:S].rearrange("p (t s) -> p t s", t=2)).then_inc(na_stored, 1)

            def na_high():
                act.wait_ge(na_stored, HB)
                for kp in range(4):
                    sl = slice(HB + 2 * kp, HB + 2 * kp + 2)
                    nc.scalar.copy(h_hi[:, sl, :].rearrange("p a (t s) -> p a t s", t=2), na_out(kp)
                                   ).then_inc(na_hi, 1)
            stream(g_in_o, drain_proj(g_in_o, proj, 3 * WA), each=at(g_in_o, neighbours), nxt=g_out,
                   tail=na_high, unrolled=True)
            act.wait_ge(ml_ms, 1)
            nc.scalar.activation(hcol[:, 2, :], hcol[:, 1, :], ACT.Sqrt).then_inc(ml_rms, 1)
            for t in range(ST):
                act.wait_ge(drained[t], g_out.chunk0)
                og = proj[:, t, 3 * WA:4 * WA]
                nc.scalar.activation(og, og, ACT.Sigmoid).then_inc(ml_rms, 1)

            def nothing(i, e):
                pass

            def quarter(n, g, x_ready):
                def each(i, e, j, first):
                    if j == 7 and not first:
                        square(n, 2 * i + e - 1, x_ready(2 * i + e - 1))
                return each

            def x_out(c_):
                return added(g_out, c_, 0)

            def x_down(c_):
                return added(g_down, c_, ST * g_out.chunks)

            quarter1 = quarter(1, g_out, x_out)

            def out_each(i, e, j, first):
                if first and j == 4:
                    high_direct(HB_ML, range(4), h_hi, vcol[:, 0, VC["ghead"]:VC["ghead"] + 8])
                    act.wait_ge(ml_sq, 2 * HA)
                quarter1(i, e, j, first)
            stream(g_out, nothing, each=out_each, nxt=g_up)
            square(1, 3, x_out(3))
            root(1)
            high(NP8, HB_NORM1, hf_ff)

            def drain_u(i, e):
                if e == 0:
                    chunk_done(g_up, i, e)
                    for t in range(ST):
                        act.wait_ge(drained[t], g_up.chunk(i, e))
                        nc.scalar.copy(ff[:, 0, t, :], gp[g_up.bank(e)][:, t, :]).then_inc(drained[t], 1)

            def gelu(i):
                act.wait_ge(ff_conv, i * 12 + 12)
                nc.scalar.activation(g4, g4, ACT.Gelu).then_inc(ff_act, 1)

            def glu_each(i, e, j, first):
                if e == 0 and not first and j == 5:
                    gelu(i - 1)
                if e == 0 and not first and j == 7:
                    glu_parts(i - 1)

            def glu_parts(i):
                act.wait_ge(ff_mul, i + 1)
                nc.scalar.copy(a_hi[:, bass.ds(i * 4, 4), :], g4).then_inc(ff_hi, 1)
            act.preload_act_table(ACT.Gelu)
            stream(g_up, drain_u, each=glu_each, nxt=g_down)
            def early(n, base, x_ready, scale):
                def each(i, e, j, first):
                    c_ = 2 * i + e - 1
                    if j == 7 and not first:
                        square(n, c_, x_ready(c_))
                        high_direct(base, (2 * c_, 2 * c_ + 1), h_hi, scale)
                return each
            gain2 = vcol[:, 0, VC["gfin"]:VC["gfin"] + DT]
            gain3 = vcol[:, 0, VC["ffng"]:VC["ffng"] + DT]
            early2 = early(2, HB_NORM2, x_down, gain2)

            def down_each(i, e, j, first):
                if first and j == 5:
                    gelu(g_up.chunks // 2 - 1)
                if first and j == 7:
                    glu_parts(g_up.chunks // 2 - 1)
                early2(i, e, j, first)
            stream(g_down, nothing, each=down_each, nxt=g_in2a)
            high_direct(HB_NORM2, (6, 7), h_hi, gain2)
            square(2, 3, x_down(3))

            def scaled_drain(g, dst, rows):
                def drain(i, e):
                    chunk_done(g, i, e)
                    if g is g_in2a:
                        act.wait_ge(rows_ready, 1)
                    nc.scalar.activation(dst[:, 0, bass.ds(i * 2 * CW + e * CW, CW)], gp[g.bank(e)][:, 0, :],
                                         ACT.Identity, scale=rows[:, 0:1]).then_inc(drained[0], 1)
                return drain

            def between(i, e, j, first):
                if first:
                    if j == 4:
                        root(2)
                    if j in (5, 6):
                        for c_ in (0, 1) if j == 5 else (2, 3):
                            square(3, c_, lambda t: act.wait_ge(gain_used, ST))
                    if j == 7:
                        root(3)
            stream(g_in2a, scaled_drain(g_in2a, proj2, rows2), each=between, nxt=g_in2b)
            act.preload_act_table_set("natural_log_exp_and_others")

            def mixers(k):
                if k < 6:
                    n = k
                    act.wait_ge(q2_t, n + 1)
                    dst = Q2[:, 2 * n:2 * n + 2] if n < 4 else K2[:, 2 * (n - 4):2 * (n - 4) + 2]
                    nc.scalar.copy(dst, tp[:, n % 4, :].rearrange("p (a s) -> p a s", a=2)).then_inc(q2_c, 1)
                if SW0 <= k < SK0:
                    h = k - SW0
                    if h < HS:
                        if h == 0:
                            act.wait_ge(sink_landed, 16)
                        act.wait_ge(sw_max, h + 1)
                        for t, (a, n) in enumerate(((0, P), (P, S))):
                            nc.scalar.activation(SC[:, h % 2, a:a + n], SC[:, h % 2, a:a + n], ACT.Exp,
                                                 bias=SW[:, h % 2, 1, t:t + 1],
                                                 accum_out=SW[:, h % 2, 2, t:t + 1])
                        nc.scalar.activation(SW[:, h % 2, 3, 0:2], SW[:, h % 2, 1, 0:2], ACT.Exp,
                                             bias=sink[:, h:h + 1]).then_inc(sw_exp, 1)
                    h = k - SW0 - 2
                    if 0 <= h < HS:
                        act.wait_ge(sw_ptm, h + 1)
                        if h >= 2:
                            act.wait_ge(o2_mm, h - 1)
                        nc.scalar.copy(PT[:, h % 2], tp[:, 2, 0:SW_N]).then_inc(sw_ptc, 1)
                    h = k - SW0 - 4
                    if 0 <= h < HS and h % 2:
                        act.wait_ge(o2_mm, h + 1)
                        nc.scalar.copy(OA[:, h // 8, (h // 2) % 4], tp[:, 3, 0:S]).then_inc(o2_out, 1)
                if SK0 <= k < SK0 + 8:
                    n = k - SK0
                    act.wait_ge(q2_t, 6 + n + 1)
                    src = tp[:, n % 4, :].rearrange("p (a s) -> p a s", a=2)
                    if n < 4:
                        nc.scalar.copy(Q2[:, 2 * n:2 * n + 2], src).then_inc(q2_c, 1)
                    else:
                        nc.scalar.mul(K2[:, 2 * (n - 4):2 * (n - 4) + 2], src, DH ** -0.5).then_inc(q2_c, 1)
                if SK1 <= k < SK_END:
                    h = k - SK1
                    if h < HS:
                        act.wait_ge(sk_z, h + 1)
                        if h >= 2:
                            act.wait_ge(sk_lb, h - 1)
                        link(nc.scalar.activation(LL[:, h % 2], tp[:, h % 2, 0:SW_N], ACT.Abs))
                        link(nc.scalar.activation(LL[:, h % 2], LL[:, h % 2], ACT.Exp, scale=-1.0))
                        nc.scalar.activation(LL[:, h % 2], LL[:, h % 2], ACT.Ln, bias=1.0).then_inc(sk_l, 1)
                    h = k - SK1 - 2
                    if 0 <= h < HS:
                        act.wait_ge(sk_arg, h + 1)
                        if h >= 2:
                            act.wait_ge(o2_mm, HS + h - 1)
                        nc.scalar.activation(AA[:, h % 2], LB[:, h % 2], ACT.Exp).then_inc(sk_exp, 1)
                    h = k - SK1 - 4
                    if 0 <= h < HS and h % 2:
                        act.wait_ge(o2_mm, HS + h + 1)
                        nc.scalar.copy(OS[:, h // 8, (h // 2) % 4], tp[:, 3, 0:S]).then_inc(o2_out, 1)

            def mixed_high():
                act.wait_ge(o2_out, HS)
                for kp in range(NP8):
                    nc.scalar.copy(h_hi[:, 2 * kp:2 * kp + 2, :], mixer_out(kp)).then_inc(o2_hi, 1)
            stream(g_in2b, scaled_drain(g_in2b, gates2, rows2), each=at(g_in2b, mixers), nxt=g_bra,
                   tail=mixed_high, unrolled=True)
            for t in range(ST):
                act.wait_ge(drained[t], g_bra.chunk0)

            def gate_sigmoid(g, col0):
                def each(i, e, j, first):
                    if j == 0:
                        for t in range(ST):
                            gg = gates2[:, t, bass.ds(col0 + g.col(i, e), CW)]
                            nc.scalar.activation(gg, gg, ACT.Sigmoid).then_inc(sig_ready, 1)
                return each
            stream(g_bra, nothing, each=gate_sigmoid(g_bra, 0), nxt=g_brb)
            stream(g_brb, nothing, each=gate_sigmoid(g_brb, D), nxt=g_out2)
            high_direct(HB_MERGE, range(NP8), m_hi)
            def x_out2(c_):
                return drained_to(g_out2, c_)
            stream(g_out2, nothing, each=early(4, HB_NORM3, x_out2, gain3), nxt=g_up2)
            high_direct(HB_NORM3, (6, 7), h_hi, gain3)
            square(4, 3, x_out2(3))

            def root4(i, e, j, first):
                if first and j == 4:
                    root(4)

            def drain_gate(i, e):
                if e == 0:
                    chunk_done(g_up2, i, e)
                    for t in range(ST):
                        act.wait_ge(drained[t], g_up2.chunk(i, e))
                        act.wait_ge(rows_ready, 2)
                        nc.scalar.activation(ff[:, 0, t, :], gp[g_up2.bank(e)][:, t, :], ACT.Silu,
                                             scale=rstd[:, 4, t:t + 1]).then_inc(drained[t], 1)

            def swiglu_side(i):
                act.wait_ge(ff_t, i + (g_up.chunks // 2 + 1))
                nc.scalar.copy(a_hi[:, bass.ds(i * 4, 4), :], tp[:, 0:2, :].rearrange(
                    "p a (b s) -> p (a b) s", b=2)).then_inc(ff_hi, 1)
            stream(g_up2, drain_gate, side=swiglu_side, each=root4, nxt=g_down2)

            def x_down2(c_):
                return drained_to(g_down2, c_)
            act.preload_act_table(ACT.Sqrt)
            quarter5 = quarter(5, g_down2, x_down2)

            def down2_each(i, e, j, first):
                if first and j == 4:
                    swiglu_side(g_up2.chunks // 2 - 1)
                quarter5(i, e, j, first)
            stream(g_down2, nothing, each=down2_each)
            square(5, 3, x_down2(3))
            root(5)
            act.wait_ge(final_rstd, 1)
            act.wait_ge(gained, ST * 4)
            xs = xres[:, 1, 0:D // 2]
            nc.scalar.activation(xs, xs, ACT.Identity, scale=rstd[:, 5, 1:2]).then_inc(half_out[2], 1)

        @block.tensor
        def _(pe):
            mm = nc.tensor.matmul

            def stream(g, hi, lo, kt0, ready, side=None, each=None, unrolled=False):
                def step(i, e, first):
                    if not (first and g.chunk0 < 2):
                        for t in range(ST):
                            pe.wait_ge(drained[t], g.chunk(i, e) - 1)
                    for j in range(g.nb):
                        pe.wait_ge(lo_ready, g.block(i, e, j) + 1)
                        if first:
                            ready(j)
                        s = g.slot(e, j)
                        for k in range(KB):
                            kt, n = g.kt(j) + k, j * KB + k
                            for t in range(ST):
                                ps = slice(t * P, (t + 1) * P)
                                o = gp[g.bank(e)][:, t, :]
                                mm(o, hi[:, kt0 + kt, ps], w_hi[:, s, k, :], start=n == 0, stop=False)
                                mm(o, hi[:, kt0 + kt, ps], w_lo[:, s, k, :], start=False, stop=False)
                                last = mm(o, lo[:, kt0 + kt, ps], w_hi[:, s, k, :], start=False,
                                          stop=n == g.kts - 1)
                        last.then_inc(block_used, 1)
                        if side and e == 0 and not first and j == 2:
                            side(i - 1)
                        if each:
                            each(i, e, j, first)
                (walk_unrolled if unrolled else walk)(pe, g.chunks, step)

            def h_pairs(base):
                return lambda j: pe.wait_ge(h_ready, base + j + 1)

            def transpose_x(n, base, full0):
                pe.wait_ge(diag_ready, ST * (n + 1))
                for kp in range(NP8):
                    if kp >= 4:
                        pe.wait_ge(h_full, full0 + kp - 3)
                    for a in range(2):
                        kt = 2 * kp + a
                        for t in range(ST):
                            last = mm(tp[:, kp % 4, a * S + t * P:a * S + (t + 1) * P],
                                      xres[:, t, kt * P:(kt + 1) * P], diag[:, t, :], start=True, stop=True)
                    last.then_inc(xt_ready, 1)

            def transpose_in(base, kps, src, col0, ready=None):
                for kp in kps:
                    if kp >= 4:
                        pe.wait_ge(h_ready, base + kp - 3)
                    for a in range(2):
                        kt = 2 * kp + a
                        for t in range(ST):
                            if ready:
                                ready(t)
                            last = nc.tensor.transpose(tp[:, kp % 4, a * S + t * P:a * S + (t + 1) * P],
                                                       src[:, t, col0 + kt * P:col0 + (kt + 1) * P], ident[:, :])
                    last.then_inc(xt_ready, 1)

            def sum_rows(ready=None):
                for q in range(2 * DT):
                    if ready and q % 8 == 0:
                        ready(q // 8)
                    last = mm(tp[0:2 * DT, 3, 0:P], pick[:, 2 * DT - 1 - q:4 * DT - 1 - q],
                              acc[:, q // 8, (q % 8) * P:(q % 8 + 1) * P], start=q == 0, stop=q == 2 * DT - 1)
                last.then_inc(mod_sum, 1)

            def rows_to_columns(n):
                pe.wait_ge(mod_rows, n)
                nc.tensor.transpose(tp[:, 2, 0:2 * DT], srow[:, :], ident[0:2 * DT, 0:2 * DT]).then_inc(mod_sum, 1)

            def sum_broadcast(src, bank):
                for q in range(4):
                    last = mm(bank(q), ones[:, :], src[:, q * CW:(q + 1) * CW],
                              start=True, stop=True)
                return last

            pe.wait_ge(ident_ready, 1)
            pe.wait_ge(c_landed, 16)
            nc.tensor.transpose(tp[:, 3, 0:DT], vrows[0:DT, 0, :], ident[0:DT, 0:DT]).then_inc(c_t, 1)
            pe.wait_ge(vec_landed, 10 * 16)
            for n, r in enumerate((104, 2 * FT, 2 * FT)):
                last = nc.tensor.transpose(tp[:, n, 0:r], vrows[0:r, n, :], ident[0:r, 0:r])
            last.then_inc(vec_t, 1)
            pe.wait_ge(const_ready, 1)
            sum_rows(lambda p: pe.wait_ge(ada_summed, PART2 - 3 + p))
            pe.wait_ge(vec_ready, 2)
            rows_to_columns(1)
            pe.wait_ge(mod_ready, 1)
            transpose_x(0, HB_NORM0, 0)
            stream(g_in_a, h_hi, h_lo, 0, h_pairs(HB_NORM0))

            def mlstm(k):
                if k == 0:
                    pe.wait_ge(wg_split, 1)
                    for kt in range(DT):
                        o = tp[:, 0, 0:S]
                        mm(o, wg_hi[:, kt, :], h_hi[:, kt, :], start=kt == 0, stop=False)
                        mm(o, wg_hi[:, kt, :], h_lo[:, kt, :], start=False, stop=False)
                        last = mm(o, wg_lo[:, kt, :], h_hi[:, kt, :], start=False, stop=kt == DT - 1)
                    last.then_inc(gates_mm, 1)
                if k == 4:
                    pe.wait_ge(em_ready, 1)
                    for t in range(ST):
                        for y in range(4):
                            q = (t * 4 + y) * HA
                            last = nc.tensor.transpose(tp[:, 0, q:q + HA], GTR[:, y, t * P:(t + 1) * P],
                                                       ident[0:HA, 0:HA])
                    last.then_inc(gc_mm, 1)
                h, part = (k - ML0) // ML_H, (k - ML0) % ML_H
                if k < ML0 or h >= HA:
                    return
                if part == 0:
                    if h:
                        pe.wait_ge(ml_h, h)
                    else:
                        pe.wait_ge(gc_ready, 1)
                        for t in range(ST):
                            pe.wait_ge(drained[t], g_in_b.chunk0)
                    for q in range(2):
                        for d in range(2):
                            for t in range(ST):
                                col = q * WA + h * DA + d * P
                                last = nc.tensor.transpose(tp[:, q, d * S + t * P:d * S + (t + 1) * P],
                                                           proj[:, t, col:col + P], ident[:, :])
                    last.then_inc(ml_t, 1)
                if part == 2:
                    if h:
                        pe.wait_ge(ml_den, h)
                        pe.wait_ge(ml_p, 4 * h)
                    for q in range(2):
                        mm(tp[:, 2, q * S:(q + 1) * S], sel[:, h, :], ga_t[:, 2 + q, :], start=True, stop=True)
                    pe.wait_ge(ml_tq, 2 * h + 2)
                    for t in range(ST):
                        for d in range(2):
                            last = mm(tp[:, 3, t * S:(t + 1) * S], ml_qk[:, 1, d, t * P:(t + 1) * P],
                                      ml_qk[:, 0, d, :], start=d == 0, stop=d == 1)
                    last.then_inc(ml_s, 1)
                if part == 5:
                    pe.wait_ge(ml_p, 4 * h + 4)
                    terms = {(0, 0): ((0, 0),), (1, 0): ((P, 0), (S, 1)),
                             (0, 1): ((S + P, 0), (2 * S, 1)), (1, 1): ((2 * S + P, 1),)}
                    for (t, q), parts in terms.items():
                        for rhs_n in range(2):
                            for m, (a, ks) in enumerate(parts):
                                lhs = ml_e[:, a:a + P]
                                se = dict(start=m == 0, stop=m == len(parts) - 1)
                                if rhs_n == 0:
                                    mm(tp[:, t, q * DA:(q + 1) * DA], lhs,
                                       proj[:, ks, 2 * WA + h * DA:2 * WA + (h + 1) * DA], **se)
                                else:
                                    last = mm(tp[:, 2, 2 * t + q:2 * t + q + 1], lhs, ones[:, 0:1], **se)
                    last.then_inc(ml_num, 1)

            def at(g, part):
                return lambda i, e, j, first: part((2 * i + e) * g.nb + j)
            stream(g_in_b, h_hi, h_lo, 0, lambda j: None, each=at(g_in_b, mlstm), unrolled=True)

            def neighbours(k):
                n = k
                if 0 <= n < HB:
                    if n == 0:
                        pe.wait_ge(ml_h, HA)
                        pe.wait_ge(ml_den, HA)
                        for t in range(ST):
                            pe.wait_ge(drained[t], g_in_o.chunk0)
                    else:
                        pe.wait_ge(na_tq, 2 * n)
                    for q in range(2):
                        for t in range(ST):
                            col = QB0 + q * WA + n * DB
                            last = nc.tensor.transpose(tp[:, 0, q * S + t * P:q * S + (t + 1) * P],
                                                       proj[:, t, col:col + DB], ident[:, :])
                    last.then_inc(na_t, 1)
                n = k - 1
                if 0 <= n < HB:
                    pe.wait_ge(na_tq, 2 * (n + 1))
                    pe.wait_ge(na_bias_ready, 2 * (n + 1))
                    if n:
                        pe.wait_ge(na_exp, 2 * n)
                    for t in range(ST):
                        o = tp[:, 1, t * S:(t + 1) * S]
                        mm(o, flip[:, :], na_bias[:, n % 4, 2 - 2 * t:2 - 2 * t + GR, :], start=True, stop=False)
                        last = mm(o, na_qk[:, n % 2, 0, t * P:(t + 1) * P], na_qk[:, n % 2, 1, :],
                                  start=False, stop=True)
                    last.then_inc(na_s, 1)
                n = k - 2
                if 0 <= n < HB:
                    pe.wait_ge(na_p, n + 1)
                    if n:
                        pe.wait_ge(na_ptc, n)
                    for kk in range(ST):
                        for t in range(ST):
                            last = nc.tensor.transpose(tp[:, 2, kk * S + t * P:kk * S + (t + 1) * P],
                                                       na_sc[:, n % 2, t, kk * P:(kk + 1) * P], ident[:, :])
                    last.then_inc(na_ptm, 1)
                n = k - 3
                if 0 <= n < HB:
                    pe.wait_ge(na_ptc, n + 1)
                    if n:
                        pe.wait_ge(na_stored, n)
                    for kk in range(ST):
                        col = QB0 + 2 * WA + n * DB
                        last = mm(tp[:, 3, 0:S], proj[:, kk, col:col + DB], na_pt[:, n % 2, kk, :],
                                  start=kk == 0, stop=kk == 1)
                    last.then_inc(na_o, 1)
            stream(g_in_o, h_hi, h_lo, 0, lambda j: None, each=at(g_in_o, neighbours), unrolled=True)

            def mixed_ready(j):
                if j < 4:
                    pe.wait_ge(na_lo, j + 1)
                else:
                    pe.wait_ge(h_ready, HB_ML + j - 3)

            def out_each(i, e, j, first):
                if first and j == 3:
                    pe.wait_ge(ml_out, 1)
                    transpose_in(HB_ML, range(4), proj, 0)
                if first and j == 6:
                    pe.wait_ge(ada_summed, PART2C)
                    pe.wait_ge(h_ready, HB_ML + 4)
                    sum_broadcast(ga1, lambda q: tp[:, q, :]).then_inc(mod_sum, 1)
                if i == 1 and e == 1 and j == 4:
                    pe.wait_ge(mod_ready, 3)
                    sum_rows(lambda p: pe.wait_ge(ada_summed, PART3))
            stream(g_out, h_hi, h_lo, 0, mixed_ready, each=out_each)
            rows_to_columns(2)
            pe.wait_ge(mod_ready, 4)
            transpose_x(1, HB_NORM1, NP8)

            def pair_up(i):
                for t in range(ST):
                    pe.wait_ge(drained[t], g_up.chunk(i, 1) + 1)
                for b in range(2):
                    for f in range(4):
                        for t in range(ST):
                            o = (f % 2) * S + t * P
                            last = nc.tensor.transpose(tp[:, 2 * b + f // 2, o:o + P],
                                                       ff[:, b, t, f * P:(f + 1) * P], ident[:, :])
                last.then_inc(ff_t, 1)
            stream(g_up, h_hi, h_lo, 0, h_pairs(HB_NORM1), pair_up)

            def early(base, x_ready):
                def each(i, e, j, first):
                    c_ = 2 * i + e - 1
                    if j == 3 and not first:
                        transpose_in(base, (2 * c_, 2 * c_ + 1), xres, 0, x_ready(c_))
                return each

            def late(base, x_ready):
                def each(i, e, j, first):
                    if first and j == 1:
                        transpose_in(base, (6, 7), xres, 0, x_ready(3))
                return each

            def x_down(c_):
                return lambda t: pe.wait_ge(x_final, ST * (g_out.chunks + c_) + t + 1)
            early2 = early(HB_NORM2, x_down)

            def down_each(i, e, j, first):
                if first and j == 1:
                    pair_up(g_up.chunks // 2 - 1)
                if first and j == 5:
                    pe.wait_ge(ada_summed, ADA_N)
                    pe.wait_ge(ff_mul, g_up.chunks // 2)
                    sum_broadcast(gate2, lambda q: tp[:, q, :]).then_inc(mod_sum, 1)
                if first and j == 14:
                    pe.wait_ge(mod_ready, 6)
                early2(i, e, j, first)
            stream(g_down, a_hi, a_lo, 0, lambda j: pe.wait_ge(ff_lo, j // 2 + 1), each=down_each)
            stream(g_in2a, h_hi, h_lo, 0, h_pairs(HB_NORM2), each=late(HB_NORM2, x_down))

            def outputs(n0, h, v, w):
                half = slice((h % 2) * DH, (h % 2 + 1) * DH)
                if h % 2 == 0 and n0 + h:
                    pe.wait_ge(o2_out, (n0 + h) // 2)
                mm(tp[half, 3, 0:S], proj2[:, 0, v:v + DH], w[:, 0:S], start=True, stop=False)
                mm(tp[half, 3, P:S], proj2[:, 1, v:v + DH], w[:, S:SW_N], start=False, stop=True
                   ).then_inc(o2_mm, 1)

            def mixers(k):
                if k < 6:
                    n = k
                    if n == 0:
                        for t in range(ST):
                            pe.wait_ge(drained[t], g_in2b.chunk0)
                    if n == 4:
                        pe.wait_ge(kdup_ready, 1)
                    if n >= 4:
                        pe.wait_ge(q2_c, n - 3)
                    for a in range(2):
                        for t in range(ST):
                            src = (proj2[:, t, QA2 + (2 * n + a) * P:QA2 + (2 * n + a + 1) * P] if n < 4 else
                                   kdup[:, t, 2 * (n - 4) + a].rearrange("p u d -> p (u d)"))
                            last = nc.tensor.transpose(tp[:, n % 4, a * S + t * P:a * S + (t + 1) * P], src,
                                                       ident[:, :])
                    last.then_inc(q2_t, 1)
                if SW0 <= k < SK0:
                    h = k - SW0
                    if h < HS:
                        if h == 0:
                            pe.wait_ge(q2_c, 6)
                        if h >= 2:
                            pe.wait_ge(sw_max, h - 1)
                        half = slice((h % 2) * DH, (h % 2 + 1) * DH)
                        g = h // (HS // HK)
                        mm(tp[:, h % 2, 0:P], Q2[half, h // 2, 0:P], K2[half, g, 0:P], start=True, stop=True)
                        mm(tp[:, h % 2, P:SW_N], Q2[half, h // 2, P:S], K2[half, g, :], start=True, stop=True
                           ).then_inc(sw_s, 1)
                    h = k - SW0 - 2
                    if 0 <= h < HS:
                        pe.wait_ge(sw_p, h + 1)
                        if h >= 1:
                            pe.wait_ge(sw_ptc, h)
                        for m in range(3):
                            last = nc.tensor.transpose(tp[:, 2, m * P:(m + 1) * P],
                                                       SC[:, h % 2, m * P:(m + 1) * P], ident[:, :])
                        last.then_inc(sw_ptm, 1)
                    h = k - SW0 - 4
                    if 0 <= h < HS:
                        pe.wait_ge(sw_ptc, h + 1)
                        outputs(0, h, VA2 + (h // (HS // HK)) * DH, PT[:, h % 2])
                if SK0 <= k < SK0 + 8:
                    n = k - SK0
                    if n == 0:
                        pe.wait_ge(o2_out, HS // 2)
                    if n >= 4:
                        pe.wait_ge(q2_c, 6 + n - 3)
                    col = (QS2 if n < 4 else KS2) + 2 * (n % 4) * P
                    for a in range(2):
                        for t in range(ST):
                            last = nc.tensor.transpose(tp[:, n % 4, a * S + t * P:a * S + (t + 1) * P],
                                                       proj2[:, t, col + a * P:col + (a + 1) * P], ident[:, :])
                    last.then_inc(q2_t, 1)
                if SK1 <= k < SK_END:
                    h = k - SK1
                    if h < HS:
                        if h == 0:
                            pe.wait_ge(q2_c, 14)
                        if h >= 2:
                            pe.wait_ge(sk_lb, h - 1)
                        half = slice((h % 2) * DH, (h % 2 + 1) * DH)
                        mm(tp[:, h % 2, 0:S], K2[half, h // 2, 0:P], Q2[half, h // 2, :], start=True, stop=True)
                        mm(tp[:, h % 2, S:SW_N], K2[half, h // 2, P:S], Q2[half, h // 2, P:S], start=True,
                           stop=True).then_inc(sk_z, 1)
                    h = k - SK1 - 2
                    if 0 <= h < HS:
                        pe.wait_ge(sk_sp, h + 1)
                        pe.wait_ge(sk_mask, 1)
                        if h >= 1:
                            pe.wait_ge(sk_arg, h)
                        o = tp[:, 2]
                        mm(o[:, 0:S], TRI, SP_[:, h % 2, 0:S], start=True, stop=False)
                        mm(o[:, P:S], ones[:, :], SP_[:, h % 2, S:SW_N], start=False, stop=True)
                        mm(o[:, S:SW_N], TRI, SP_[:, h % 2, S:SW_N], start=True, stop=True).then_inc(sk_suf, 1)
                    h = k - SK1 - 4
                    if 0 <= h < HS:
                        pe.wait_ge(sk_a, h + 1)
                        outputs(HS, h, VS2 + h * DH, AA[:, h % 2])

            stream(g_in2b, h_hi, h_lo, 0, lambda j: None, each=at(g_in2b, mixers), unrolled=True)
            stream(g_bra, h_hi, h_lo, 0, lambda j: pe.wait_ge(o2_lo, j + 1))
            stream(g_brb, h_hi, h_lo, WA // P, lambda j: pe.wait_ge(o2_lo, g_bra.nb + j + 1))
            pe.wait_ge(merged, ST * g_brb.chunks)
            transpose_in(HB_MERGE, range(NP8), gates2, 0)

            def x_out2(c_):
                return lambda t: pe.wait_ge(drained[t], g_out2.chunk0 + c_ + 1)
            stream(g_out2, m_hi, m_lo, 0, h_pairs(HB_MERGE), each=early(HB_NORM3, x_out2))

            def pair_up2(i):
                for t in range(ST):
                    pe.wait_ge(drained[t], g_up2.chunk(i, 1) + 1)
                for f in range(4):
                    for t in range(ST):
                        o = (f % 2) * S + t * P
                        last = nc.tensor.transpose(tp[:, f // 2, o:o + P], ff[:, 1, t, f * P:(f + 1) * P],
                                                   ident[:, :])
                last.then_inc(ff_t, 1)
            stream(g_up2, h_hi, h_lo, 0, h_pairs(HB_NORM3), pair_up2, each=late(HB_NORM3, x_out2))

            def last_pair2(i, e, j, first):
                if first and j == 1:
                    pair_up2(g_up2.chunks // 2 - 1)
            stream(g_down2, a_hi, a_lo, 0, lambda j: pe.wait_ge(ff_lo, g_up.chunks // 2 + j // 2 + 1),
                   each=last_pair2)

        @block.vector
        def _(dve):
            link = chain(dve_chain, dve)
            V = nc.vector

            def split(g, i, e, j):
                s = g.slot(e, j)
                dve.wait_ge(hi_ready, g.block(i, e, j) + 1)
                V.tensor_tensor(w_lo[:, s], raw[:, s], w_hi[:, s].bitcast(F32), ALU.subtract
                                ).then_inc(lo_ready, 1)

            def prime(g, js=range(RING)):
                for j in js:
                    split(g, 0, 0, j)

            def stream(g, drain, side=None, each=None, before=None, nxt=None, tail=None, early=None,
                       unrolled=False):
                def step(i, e, first, extra=False):
                    for j in range(g.nb):
                        if before:
                            before(i, e, j, first)
                        if not (first and j < RING):
                            split(g, i, e, j)
                        if j == RING - 1 and not first:
                            drain(i if e else i - 1, 1 - e)
                        if each:
                            each(i, e, j, first)
                        if early and (first or extra):
                            early(i, e, j, first)
                    if side and not first and e == 0:
                        side(i - 1)
                if unrolled:
                    walk_unrolled(dve, g.chunks, step)
                else:
                    walk(dve, g.chunks, step, CUT if early else 0)
                if nxt:
                    prime(nxt, range(RING - 1 if tail else RING))
                if tail:
                    tail()
                    prime(nxt, (RING - 1,))
                drain((g.chunks - 1) // 2, (g.chunks - 1) % 2)

            def chunk_done(g, i, e):
                dve.wait_ge(block_used, g.done(i, e))

            def nothing(i, e):
                pass

            def drain_proj(g, dst, col0):
                def drain(i, e):
                    chunk_done(g, i, e)
                    V.tensor_copy(dst[:, 1, bass.ds(col0 + i * 2 * CW + e * CW, CW)], gp[g.bank(e)][:, 1, :]
                                  ).then_inc(drained[1], 1)
                return drain

            def norm_stats(n):
                dve.wait_ge(sq_ready, 4 * ST * (n + 1))
                link(V.tensor_reduce(stat[:, 0:2], ssq[:, :, :], AX_X, ALU.add))
                V.tensor_scalar(stat[:, 2:4], stat[:, 0:2], 1.0 / D, EPS, ALU.mult, ALU.add
                                ).then_inc(ms_ready, 1)
                dve.wait_ge(rms_ready, n + 1)
                link(V.reciprocal(rstd[:, n, :], stat[:, 4:6]))

            def make_diag(n):
                for t in range(ST):
                    V.tensor_scalar(diag[:, t, :], ident[:, :], rstd[:, n, t:t + 1], None, ALU.mult
                                    ).then_inc(diag_ready, 1)

            def handover(full0, base, buf, scale, shift):
                def low(kp):
                    dve.wait_ge(h_high, base + kp + 1)
                    sl = slice(2 * kp, 2 * kp + 2)
                    V.tensor_tensor(h_lo[:, sl, :], buf[:, kp % 2], h_hi[:, sl, :].bitcast(F32), ALU.subtract
                                    ).then_inc(h_ready, 1)
                for kp in range(NP8):
                    dve.wait_ge(xt_ready, base + kp + 1)
                    if kp >= 2:
                        dve.wait_ge(h_ready, base + kp - 1)
                    for a in range(2):
                        kt = 2 * kp + a
                        last = V.tensor_scalar(buf[:, kp % 2, a], tp[:, kp % 4, a * S:(a + 1) * S],
                                               scale[:, kt:kt + 1], shift[:, kt:kt + 1], ALU.mult, ALU.add)
                    last.then_inc(h_full, 1)
                    if kp:
                        low(kp - 1)
                low(NP8 - 1)

            def low_direct(base, kps, hi, lo, scale=None):
                for kp in kps:
                    dve.wait_ge(h_high, base + kp + 1)
                    src = tp[:, kp % 4, :].rearrange("p (a s) -> p a s", a=2)
                    sl = slice(2 * kp, 2 * kp + 2)
                    if scale is None:
                        last = V.tensor_tensor(lo[:, sl, :], src, hi[:, sl, :].bitcast(F32), ALU.subtract)
                    else:
                        for a in range(2):
                            kt = 2 * kp + a
                            last = V.scalar_tensor_tensor(lo[:, kt, :], src[:, a], scale[:, kt:kt + 1],
                                                          hi[:, kt, :].bitcast(F32), ALU.mult, ALU.subtract)
                    last.then_inc(h_ready, 1)

            def mod_columns(which, g):
                V.tensor_copy(mod[:, 2 * which, :], tp[:, 2, 0:DT])
                link(V.scalar_tensor_tensor(mod[:, 2 * which + 1, :], tp[:, 2, DT:2 * DT], 1.0,
                                            vcol[:, 0, VC[g]:VC[g] + DT], ALU.add, ALU.mult))

            def add_ada(a, ring, k, dst):
                V.scalar_tensor_tensor(dst, ring, c_act[:, bass.ds(k, 1)], dst, ALU.mult, ALU.add
                                       ).then_inc(ada_summed, 1)

            dve.wait_ge(silu_ready, 1)
            dve.wait_ge(acc_bias[0], 16)

            def ada_part1(i, k2, peeled):
                for p in range(4):
                    dve.wait_ge(ada1_landed[4 * k2 + p], i * 16 + 16)
                    if not (peeled and k2 == 0):
                        dve.wait_ge(ada_summed, i * 8 + (4 * k2 + p - 3))
                    add_ada(None, ada_first[:, 4 * k2 + p, :], i * 2 + k2, acc[:, p, :])
            for k2 in range(2):
                ada_part1(0, k2, True)
            dve.wait_ge(vec_ready, 1)
            link(V.tensor_tensor(vcol[:, 0, VC["gfin"]:VC["gfin"] + DT], vcol[:, 0, VC["gfin"]:VC["gfin"] + DT],
                                 vcol[:, 0, VC["mixg"]:VC["mixg"] + DT], ALU.mult))
            dve.wait_ge(ident_ready, 1)
            norm_stats(0)
            make_diag(0)
            prime(g_in_a)
            with dve.Fori(1, DT // 2) as i:
                for k2 in range(2):
                    ada_part1(i, k2, False)
            dve.wait_ge(wg_high, 1)
            dve.wait_ge(wg_clear, 2)
            V.tensor_tensor(gate_columns(wg_lo), wg.rearrange("p t (y h) -> p t y h", y=4),
                            gate_columns(wg_hi).bitcast(F32), ALU.subtract).then_inc(wg_split, 1)
            dve.wait_ge(mod_sum, 1)
            V.tensor_copy(srow[:, :], tp[0:2 * DT, 3, 0:P]).then_inc(mod_rows, 1)
            dve.wait_ge(mod_sum, 2)
            mod_columns(0, "g1")
            V.memset(stat[:, 8:9], 0.0).then_inc(mod_ready, 1)
            handover(0, HB_NORM0, hf, mod[:, 1, :], mod[:, 0, :])

            def ada2(k0):
                def each(i, e, j, first):
                    if first and k0 == 0:
                        if j in (2, 3):
                            return
                        j -= 2 if j > 3 else 0
                    if j >= 6:
                        return
                    a = i * 12 + (PART2 + 6 * (k0 + e) + j)
                    dve.wait_ge(ada_landed[j % 2], i * 96 + 16 * (3 * (k0 + e) + j // 2 + 1))
                    if first and k0 == 0:
                        if j == 0:
                            dve.wait_ge(acc_bias[1], 16)
                        if j == 2:
                            dve.wait_ge(acc_bias[3], 16)
                    else:
                        dve.wait_ge(ada_summed, a - 5)
                    add_ada(a, ada_ring[:, j % 2, :], i * 2 + (k0 + e), ada_sum[:, j, :])
                return each
            stream(g_in_a, drain_proj(g_in_a, proj, 0), each=ada2(0), nxt=g_in_b)

            def at(g, part):
                def hook(i, e, j, first):
                    k = (2 * i + e) * g.nb + j - LAG
                    if k >= 0:
                        part(k)
                return hook

            fg, ig = GTR[:, 1:4:2, :], GTR[:, 0:4:2, :]
            bf, bb, mf, mb = (ga_t[:, y, :] for y in range(4))

            def mlstm_before(k):
                if k == 0:
                    dve.wait_ge(gates_mm, 1)
                    for y in range(4):
                        last = V.tensor_copy(GTR[:, y, :], tp[32 * y:32 * y + HA, 0, 0:S])
                    link(last)
                    for y in range(4):
                        last = V.tensor_scalar(GTR[:, y, :], GTR[:, y, :], bg[:, y:y + 1], None, ALU.add)
                    last.then_inc(gt_ready, 1)
                h, part = (k - ML0) // ML_H, (k - ML0) % ML_H
                if k >= ML0 and h < HA and part == 2:
                    dve.wait_ge(ml_s, h + 1)
                    if h:
                        dve.wait_ge(ml_num, h)
                    for a, n, q, t0, m in ((0, S, 0, 0, mask_f[:, :]), (S, P, 0, P, mask_f[:, 0:P]),
                                           (S + P, P, 1, 0, mask_b[:, P:S]), (2 * S, S, 1, 0, mask_b[:, :])):
                        last = V.tensor_tensor(ml_e[:, a:a + n], m, tp[:, 2, q * S + t0:q * S + t0 + n],
                                               ALU.subtract)
                    last.then_inc(ml_arg, 1)

            def mlstm_after(k):
                if k == 1:
                    dve.wait_ge(gl_ln, 1)
                    link(V.scalar_tensor_tensor(fg, fg, 0.0, ga_t[:, 0:2, :], ALU.min, ALU.subtract))
                    V.tensor_tensor_scan(bf, GTR[:, 1, :], GTR[:, 1, :], 0.0, ALU.add, ALU.bypass)
                    link(V.tensor_tensor_scan(bb[:, ::-1], GTR[:, 3, ::-1], GTR[:, 3, ::-1], 0.0, ALU.add,
                                              ALU.bypass))
                    link(V.tensor_tensor(ig, ig, ga_t[:, 0:2, :], ALU.subtract))
                if k == 2:
                    V.tensor_tensor_scan(mf, GTR[:, 0, :], GTR[:, 0, :], -3e38, ALU.max, ALU.bypass)
                    link(V.tensor_tensor_scan(mb[:, ::-1], GTR[:, 2, ::-1], GTR[:, 2, ::-1], -3e38, ALU.max,
                                              ALU.bypass))
                    V.tensor_tensor(fg, ga_t[:, 0:2, :], ga_t[:, 2:4, :], ALU.add).then_inc(gm_ready, 1)
                if k == 4:
                    dve.wait_ge(gc_mm, 1)
                    V.tensor_copy(gcol[:, :, :, :].rearrange("p t y h -> p (t y h)"), tp[:, 0, 0:ST * 4 * HA]
                                  ).then_inc(gc_ready, 1)
                h, part = (k - ML0) // ML_H, (k - ML0) % ML_H
                if k >= ML0 and h < HA and part == 2:
                    for m, (a, n, t, t0) in enumerate(((0, S, 0, 0), (S, P, 1, P), (S + P, P, 0, 0),
                                                       (2 * S, S, 1, 0))):
                        dve.wait_ge(ml_exp, 4 * h + m + 1)
                        V.tensor_tensor(ml_e[:, a:a + n], ml_e[:, a:a + n], tp[:, 3, t * S + t0:t * S + t0 + n],
                                        ALU.mult).then_inc(ml_p, 1)
                if k >= ML0 and h < HA and part == 5:
                    dve.wait_ge(ml_den, h + 1)
                    r = hcol[:, 0, 0:4].rearrange("p (t q) -> p t q", t=ST)
                    link(V.tensor_tensor(r, r, gcol[:, :, 1:4:2, h], ALU.max))
                    link(V.reciprocal(r, r))
                    for t in range(ST):
                        last = V.tensor_scalar(proj[:, t, h * DA:(h + 1) * DA], tp[:, t, 0:DA],
                                               hcol[:, 0, 2 * t:2 * t + 1], None, ALU.mult)
                    link(last)
                    for t in range(ST):
                        ht = proj[:, t, h * DA:(h + 1) * DA]
                        last = V.scalar_tensor_tensor(ht, tp[:, t, DA:2 * DA], hcol[:, 0, 2 * t + 1:2 * t + 2],
                                                      ht, ALU.mult, ALU.add)
                    last.then_inc(ml_h, 1)
                if k == ML0 + HA * ML_H:
                    dve.wait_ge(ml_sq, 2 * HA)
                    V.tensor_scalar(hcol[:, 1, :], hcol[:, 1, :], 1.0 / DA, EPS, ALU.mult, ALU.add
                                    ).then_inc(ml_ms, 1)
            ada2b, ml_after = ada2(g_in_a.chunks), at(g_in_b, mlstm_after)

            def in_b_each(i, e, j, first):
                ada2b(i, e, j, first)
                ml_after(i, e, j, first)
            stream(g_in_b, drain_proj(g_in_b, proj, QB0), each=in_b_each, before=at(g_in_b, mlstm_before),
                   nxt=g_in_o, unrolled=True)

            def neighbours_before(k):
                n = k - 1
                if 0 <= n < HB:
                    dve.wait_ge(na_s, n + 1)
                    V.tensor_reduce(nst[:, n % 2, 0, :], tp[:, 1, :].rearrange("p (t s) -> p t s", t=ST),
                                    AX_X, ALU.max, negate=True).then_inc(na_max, 1)

            def neighbours_after(k):
                n = k - 1
                if 0 <= n < HB:
                    dve.wait_ge(na_exp, 2 * (n + 1))
                    link(V.reciprocal(nst[:, n % 2, 2, :], nst[:, n % 2, 1, :]))
                    for t in range(ST):
                        last = V.tensor_scalar(na_sc[:, n % 2, t], na_sc[:, n % 2, t],
                                               nst[:, n % 2, 2, t:t + 1], None, ALU.mult)
                    last.then_inc(na_p, 1)

            def na_low():
                for kp in range(4):
                    sl = slice(HB + 2 * kp, HB + 2 * kp + 2)
                    dve.wait_ge(na_hi, kp + 1)
                    V.tensor_tensor(h_lo[:, sl, :].rearrange("p a (t s) -> p a t s", t=2), na_out(kp),
                                    h_hi[:, sl, :].bitcast(F32).rearrange("p a (t s) -> p a t s", t=2),
                                    ALU.subtract).then_inc(na_lo, 1)
            na_after = at(g_in_o, neighbours_after)

            def in_o_each(i, e, j, first):
                if j < 4:
                    n = 4 * e + j
                    dve.wait_ge(ada_landed[n % 2], 16 * (3 * K1 + n // 2 + 1))
                    dve.wait_ge(ada_summed, PART2B + n - (1 if n >= 2 else 5))
                    add_ada(None, ada_ring[:, n % 2, :], K1 + n // 2, ada_sum[:, n % 2, :])
                na_after(i, e, j, first)
            stream(g_in_o, drain_proj(g_in_o, proj, 3 * WA), each=in_o_each,
                   before=at(g_in_o, neighbours_before), nxt=g_out, tail=na_low, unrolled=True)
            dve.wait_ge(ml_rms, 1)
            link(V.reciprocal(hcol[:, 2, :], hcol[:, 2, :]))
            for t in range(ST):
                dve.wait_ge(ml_rms, 2 + t)
                for h in range(HA):
                    ht = proj[:, t, h * DA:(h + 1) * DA]
                    last = V.scalar_tensor_tensor(ht, ht, hcol[:, 2, 2 * h + t:2 * h + t + 1],
                                                  proj[:, t, 3 * WA + h * DA:3 * WA + (h + 1) * DA],
                                                  ALU.mult, ALU.mult)
            last.then_inc(ml_out, 1)

            def drain_gated(g, gate, buf, done0):
                def drain(i, e):
                    chunk_done(g, i, e)
                    c_ = 2 * i + e
                    if c_ >= 2:
                        dve.wait_ge(x_final, done0 + 2 * (c_ - 1))
                    for t in range(ST):
                        V.tensor_tensor(buf[:, e, t, :], gp[g.bank(e)][:, t, :], gate[:, bass.ds(g.col(i, e), CW)],
                                        ALU.mult).then_inc(drained[t], 1)
                return drain

            def spread(dst, b0):
                for b in range(2):
                    V.tensor_copy(dst[:, b * 2 * CW:(b + 1) * 2 * CW],
                                  tp[:, 2 * b:2 * b + 2, :].rearrange("p t n -> p (t n)")).then_inc(mod_ready, 1)
                dve.wait_ge(mod_ready, b0 + 2)

            def out_each(i, e, j, first):
                c_ = 2 * i + e
                if first and j == 4:
                    low_direct(HB_ML, range(4), h_hi, h_lo, vcol[:, 0, VC["ghead"]:VC["ghead"] + 8])
                m = j if c_ else j - 4
                if 0 <= m < 4:
                    dve.wait_ge(ada_landed[m % 2], 16 * (3 * K1 + 4 + 2 * c_ + m // 2 + 1))
                    dve.wait_ge(ada_summed, PART2C + 4 * c_ + m - (3 if c_ else 11))
                    add_ada(None, ada_ring[:, m % 2, :], K1 + c_, acc[:, m, :])
                if c_ == 1 and j == 1:
                    dve.wait_ge(mod_sum, 3)
                    spread(ga1, 1)
                if c_ == 3 and j == 7:
                    dve.wait_ge(mod_sum, 4)
                    V.tensor_copy(srow[:, :], tp[0:2 * DT, 3, 0:P]).then_inc(mod_rows, 1)
            stream(g_out, drain_gated(g_out, ga1, xt1, 0), each=out_each, nxt=g_up)
            dve.wait_ge(mod_sum, 5)
            mod_columns(1, "g2")
            V.memset(stat[:, 9:10], 0.0).then_inc(mod_ready, 1)
            norm_stats(1)
            make_diag(1)
            handover(NP8, HB_NORM1, hf_ff, mod[:, 3, :], mod[:, 2, :])

            def drain_g(i, e):
                if e == 1:
                    chunk_done(g_up, i, e)
                    for t in range(ST):
                        dve.wait_ge(drained[t], g_up.chunk(i, e))
                        V.tensor_copy(ff[:, 1, t, :], gp[g_up.bank(e)][:, t, :]).then_inc(drained[t], 1)

            gt = tp[:, 2:4, :].rearrange("p b (a s) -> p (b a) s", a=2)
            ut = tp[:, 0:2, :].rearrange("p b (a s) -> p (b a) s", a=2)

            def conv(i, half):
                def col(tile, r, f):
                    return vcol[:, tile, bass.ds(i * 4 + (r + f), 1)]
                fs, n0 = (2 * half, 2 * half + 1), 6 * half
                dve.wait_ge(ff_t, i + 1)
                for f in fs:
                    V.tensor_scalar(g4[:, f, :], gt[:, f, :], col(1, FT, f), col(2, FT, f), ALU.mult, ALU.add
                                    ).then_inc(ff_conv, 1)
                for f in fs:
                    dve.wait_ge(ff_conv, i * 12 + (n0 + f % 2 + 1))
                    V.scalar_tensor_tensor(g4[:, f, 1:S], gt[:, f, 0:S - 1], col(1, 0, f), g4[:, f, 1:S],
                                           ALU.mult, ALU.add).then_inc(ff_conv, 1)
                for f in fs:
                    dve.wait_ge(ff_conv, i * 12 + (n0 + f % 2 + 3))
                    V.scalar_tensor_tensor(g4[:, f, 0:S - 1], gt[:, f, 1:S], col(2, 0, f), g4[:, f, 0:S - 1],
                                           ALU.mult, ALU.add).then_inc(ff_conv, 1)

            def conv_each(i, e, j, first):
                if e == 0 and not first and j in (4, 5):
                    conv(i - 1, j - 4)
                if e == 0 and not first and j == 6:
                    times_u(i - 1)
                if e == 0 and not first and j == 7:
                    glu_parts(i - 1)

            def times_u(i):
                dve.wait_ge(ff_act, i + 1)
                V.tensor_tensor(g4, g4, ut, ALU.mult).then_inc(ff_mul, 1)

            def glu_parts(i):
                dve.wait_ge(ff_hi, i + 1)
                V.tensor_tensor(a_lo[:, bass.ds(i * 4, 4), :], g4, a_hi[:, bass.ds(i * 4, 4), :].bitcast(F32),
                                ALU.subtract).then_inc(ff_lo, 1)
                dve.wait_ge(ff_lo, i + 1)
            def ada3(i, e, j, first):
                if first:
                    n = 4
                    if j in (2, 3):
                        return
                    j -= 2 if j > 3 else 0
                    a, k, landed = PART3 + j, j // 2, 16 * (3 * DT + j // 2 + 1)
                else:
                    n = 2
                    a, k, landed = i * 4 + (PART3 + 2 + 2 * e + j), i * 2 + (e + 1), i * 32 + 16 * (3 * DT + e + 2)
                if j < n:
                    dve.wait_ge(ada_landed[j % 2], landed)
                    if first and j < 2:
                        dve.wait_ge(acc_bias[2], 16)
                    else:
                        dve.wait_ge(ada_summed, a - 1)
                    add_ada(a, ada_ring[:, j % 2, :], k, gate2[:, (j % 2) * ADA_W:(j % 2 + 1) * ADA_W])
            stream(g_up, drain_g, each=conv_each, early=ada3, nxt=g_down)
            gain2 = vcol[:, 0, VC["gfin"]:VC["gfin"] + DT]
            gain3 = vcol[:, 0, VC["ffng"]:VC["ffng"] + DT]

            def early(base, scale):
                def each(i, e, j, first):
                    c_ = 2 * i + e - 1
                    if j == 7 and not first:
                        low_direct(base, (2 * c_, 2 * c_ + 1), h_hi, h_lo, scale)
                return each
            early2 = early(HB_NORM2, gain2)

            def down_each(i, e, j, first):
                last_pair = g_up.chunks // 2 - 1
                if first and j in (4, 5):
                    conv(last_pair, j - 4)
                if first and j == 6:
                    times_u(last_pair)
                if first and j == 7:
                    glu_parts(last_pair)
                if first and j == 9:
                    dve.wait_ge(mod_sum, 6)
                    spread(gate2, 4)
                early2(i, e, j, first)
            stream(g_down, drain_gated(g_down, gate2, ff, ST * g_out.chunks), each=down_each, nxt=g_in2a)
            low_direct(HB_NORM2, (6, 7), h_hi, h_lo, gain2)

            def between(i, e, j, first):
                if first:
                    if j == 4:
                        norm_stats(2)
                        dve.wait_ge(gain_landed, 16)
                    if j in (4, 5):
                        t = j - 4
                        V.scalar_tensor_tensor(xres[:, t, :], xres[:, t, :], rstd[:, 2, t:t + 1], gate2[:, :],
                                               ALU.mult, ALU.mult).then_inc(gain_used, 1)
                    if j == 7:
                        norm_stats(3)
                        V.tensor_tensor(rows2[:, :], rstd[:, 2, :], rstd[:, 3, :], ALU.mult
                                        ).then_inc(rows_ready, 1)

            def scaled_drain(g, dst, rows):
                def drain(i, e):
                    chunk_done(g, i, e)
                    if g is g_in2a:
                        dve.wait_ge(rows_ready, 1)
                    V.tensor_scalar(dst[:, 1, bass.ds(i * 2 * CW + e * CW, CW)], gp[g.bank(e)][:, 1, :],
                                    rows[:, 1:2], None, ALU.mult).then_inc(drained[1], 1)
                return drain
            stream(g_in2a, scaled_drain(g_in2a, proj2, rows2), each=between, nxt=g_in2b)
            ka = proj2[:, :, KA2:KA2 + HK * DH].rearrange("p t (g d) -> p t g d", g=HK)
            dve.wait_ge(drained[0], g_in2b.chunk0)
            dve.wait_ge(drained[1], g_in2b.chunk0)
            for u in range(2):
                for t in range(ST):
                    last = V.tensor_copy(kdup[:, t, :, u, :], ka[:, t])
            last.then_inc(kdup_ready, 1)

            def mixers_before(k):
                if SW0 <= k < SK0:
                    h = k - SW0
                    if h < HS:
                        sw = SW[:, h % 2]
                        dve.wait_ge(sw_s, h + 1)
                        dve.wait_ge(sw_bias, h + 1)
                        if h >= 2:
                            dve.wait_ge(sw_ptm, h - 1)
                        link(V.scalar_tensor_tensor(SC[:, h % 2], tp[:, h % 2, 0:SW_N], DH ** -0.5,
                                                    TB[:, h % 2], ALU.mult, ALU.add))
                        V.tensor_reduce(sw[:, 0, 0:1], SC[:, h % 2, 0:P], AX_X, ALU.max)
                        link(V.tensor_reduce(sw[:, 0, 1:2], SC[:, h % 2, P:SW_N], AX_X, ALU.max))
                        V.tensor_scalar(sw[:, 1, 0:2], sw[:, 0, 0:2], sink[:, h:h + 1], -1.0, ALU.max, ALU.mult
                                        ).then_inc(sw_max, 1)
                if SK1 <= k < SK_END:
                    h = k - SK1 - 2
                    if 0 <= h < HS:
                        dve.wait_ge(sk_suf, h + 1)
                        V.tensor_tensor(LB[:, h % 2], LB[:, h % 2], tp[:, 2, 0:SW_N], ALU.subtract
                                        ).then_inc(sk_arg, 1)

            def mixers_after(k):
                if SW0 <= k < SK0:
                    h = k - SW0
                    if h < HS:
                        sw = SW[:, h % 2]
                        dve.wait_ge(sw_exp, h + 1)
                        link(V.tensor_tensor(sw[:, 2, 0:2], sw[:, 2, 0:2], sw[:, 3, 0:2], ALU.add))
                        link(V.reciprocal(sw[:, 2, 0:2], sw[:, 2, 0:2]))
                        for t, (a, n) in enumerate(((0, P), (P, S))):
                            last = V.tensor_scalar(SC[:, h % 2, a:a + n], SC[:, h % 2, a:a + n],
                                                   sw[:, 2, t:t + 1], None, ALU.mult)
                        last.then_inc(sw_p, 1)
                if SK1 <= k < SK_END:
                    h = k - SK1
                    if h < HS:
                        z = tp[:, h % 2, 0:SW_N]
                        spv = SP_[:, h % 2].rearrange("p (a b) -> p a b", a=3)[:, 0:3:2, :]
                        if h == 0:
                            dve.wait_ge(sk_mask, 1)
                        dve.wait_ge(sk_l, h + 1)
                        if h >= 2:
                            dve.wait_ge(sk_suf, h - 1)
                        link(V.scalar_tensor_tensor(SP_[:, h % 2], z, 0.0, LL[:, h % 2], ALU.max, ALU.add))
                        V.tensor_tensor(spv, spv, M2, ALU.mult).then_inc(sk_sp, 1)
                        if h >= 2:
                            dve.wait_ge(sk_exp, h - 1)
                        V.scalar_tensor_tensor(LB[:, h % 2], z, 0.0, LL[:, h % 2], ALU.min, ALU.subtract
                                               ).then_inc(sk_lb, 1)

            def mixed_low():
                for kp in range(NP8):
                    dve.wait_ge(o2_hi, kp + 1)
                    sl = slice(2 * kp, 2 * kp + 2)
                    V.tensor_tensor(h_lo[:, sl, :], mixer_out(kp), h_hi[:, sl, :].bitcast(F32), ALU.subtract
                                    ).then_inc(o2_lo, 1)
            stream(g_in2b, scaled_drain(g_in2b, gates2, rows2), each=at(g_in2b, mixers_after),
                   before=at(g_in2b, mixers_before), nxt=g_bra, tail=mixed_low, unrolled=True)

            def drain_branch(g, col0):
                def drain(i, e):
                    chunk_done(g, i, e)
                    for t in range(ST):
                        dve.wait_ge(sig_ready, i * 2 * ST + (ST * (g.chunk0 - g_bra.chunk0 + e) + t + 1))
                        gate = gates2[:, t, bass.ds(col0 + g.col(i, e), CW)]
                        V.tensor_tensor(gate, gp[g.bank(e)][:, t, :], gate, ALU.mult).then_inc(drained[t], 1)
                return drain
            stream(g_bra, drain_branch(g_bra, 0), nxt=g_brb)
            stream(g_brb, drain_branch(g_brb, D), nxt=g_out2)
            low_direct(HB_MERGE, range(NP8), m_hi, m_lo)

            def drain_add(g):
                def drain(i, e):
                    chunk_done(g, i, e)
                    for t in range(ST):
                        xs = xres[:, t, bass.ds(g.col(i, e), CW)]
                        V.tensor_tensor(xs, gp[g.bank(e)][:, t, :], xs, ALU.add).then_inc(drained[t], 1)
                return drain
            stream(g_out2, drain_add(g_out2), each=early(HB_NORM3, gain3), nxt=g_up2)
            low_direct(HB_NORM3, (6, 7), h_hi, h_lo, gain3)

            def rows3(i, e, j, first):
                if first and j == 4:
                    norm_stats(4)
                    V.memset(stat[:, 10:11], 0.0).then_inc(rows_ready, 1)

            def drain_up(i, e):
                if e == 1:
                    chunk_done(g_up2, i, e)
                    for t in range(ST):
                        dve.wait_ge(drained[t], g_up2.chunk(i, 0) + 1)
                        V.scalar_tensor_tensor(ff[:, 1, t, :], gp[g_up2.bank(e)][:, t, :], rstd[:, 4, t:t + 1],
                                               ff[:, 0, t, :], ALU.mult, ALU.mult).then_inc(drained[t], 1)

            def swiglu_side(i):
                dve.wait_ge(ff_hi, i + (g_up.chunks // 2 + 1))
                sl = bass.ds(i * 4, 4)
                V.tensor_tensor(a_lo[:, sl, :], tp[:, 0:2, :].rearrange("p b (a s) -> p (b a) s", a=2),
                                a_hi[:, sl, :].bitcast(F32), ALU.subtract).then_inc(ff_lo, 1)
            stream(g_up2, drain_up, side=swiglu_side, each=rows3, nxt=g_down2)
            def gain(c_):
                for t in range(ST):
                    dve.wait_ge(sq_ready, 4 * ST * 5 + ST * c_ + t + 1)
                    xs = xres[:, t, c_ * CW:(c_ + 1) * CW]
                    V.tensor_tensor(xs, xs, gate2[:, c_ * CW:(c_ + 1) * CW], ALU.mult).then_inc(gained, 1)

            def gain_each(i, e, j, first):
                if first and j == 4:
                    swiglu_side(g_up2.chunks // 2 - 1)
                if j == 9 and not first:
                    if 2 * i + e == 1:
                        dve.wait_ge(gain_landed, 32)
                    gain(2 * i + e - 1)
            stream(g_down2, drain_add(g_down2), each=gain_each, unrolled=True)
            norm_stats(5)
            V.memset(stat[:, 11:12], 0.0).then_inc(final_rstd, 1)
            gain(3)
            dve.wait_ge(gained, ST * 4)
            for n in (0, 1, 3):
                xs = xres[:, n // 2, (n % 2) * (D // 2):(n % 2 + 1) * (D // 2)]
                V.tensor_scalar(xs, xs, rstd[:, 5, n // 2:n // 2 + 1], None, ALU.mult).then_inc(half_out[n], 1)


_INS = ["x", "c", "w_ada", "b_ada", "g_norm1", "w_in", "b_gates", "g_head_a", "rpb", "w_out", "g_norm2",
        "w_up", "conv_w", "conv_b", "w_down", "g_final", "norm_mix_g_2", "w_in_2", "sink_logits_2",
        "w_branch_a_2", "w_branch_b_2", "w_out_2", "norm_ffn_g_2", "w_ffn_in_2", "w_ffn_down_2",
        "norm_final_g_2"]


def kernel(**inputs):
    import numpy as _np
    import concourse.bacc as _bacc
    from concourse import mybir as _mybir
    from concourse.bass_utils import run_bass_kernel_spmd as _run

    nc = _bacc.Bacc("TRN2", target_bir_lowering=False, num_devices=1)
    arrays, args = {}, []
    for name in _INS:
        a = _np.ascontiguousarray(inputs[name])
        arrays[f"in_{name}_dram"] = a
        args.append(nc.dram_tensor(f"in_{name}_dram", a.shape, _mybir.dt.from_np(a.dtype),
                                   kind="ExternalInput").ap())
    shape = inputs["x"].shape
    args.append(nc.dram_tensor("out_0_dram", shape, _mybir.dt.float32, kind="ExternalOutput").ap())
    two_blocks(nc, *args)
    r = _run(nc, [arrays], core_ids=[0])
    return r.results[0]["out_0_dram"]
```
